# Optimizing a Trainium2 kernel written in Bass

```python
import math
import jax
import jax.numpy as jnp
from jax import lax
import numpy as np

D_MODEL = 1024
BATCH = 1
SEQ = 128
DEPTH = 2
DEC_BATCH = 1
DEC_SEQ = 1024
PAST_LEN = 128

GRID_W = 64
N_EVEN = (DEPTH + 1) // 2
N_ODD = DEPTH // 2
H_A = 4
DV_A = D_MODEL // 8
DQK_A = DV_A // 2
W_A = H_A * DV_A
H_B = 4
DH_B = D_MODEL // 8
W_B = H_B * DH_B
KCONV = 3
MLSTM_CHUNK = 128
H_C = 8
DH_C = D_MODEL // H_C
W_C = H_C * DH_C
HGRN_CHUNK = 32
N_EXPERTS = 16
EXPERT_FF = D_MODEL
CAPACITY_FACTOR = 2
ROPE_BASE = 10000.0
RMS_EPS = 1e-6
Q_BLOCK = 128
NEG_BIG = -1e30
AB_SIZES = (W_A, W_A, W_A, W_B, W_B, W_B, W_B, 2 * H_B, 2 * H_B)
AB_SPLITS = tuple(sum(AB_SIZES[:i + 1]) for i in range(len(AB_SIZES) - 1))
P_AB = sum(AB_SIZES)
P_C = 5 * W_C

kernel_name = 'hybrid_diffattn_mlstm_hgrn2_ecmoe_step'

def rms_norm(x, g):
    xf = x.astype(jnp.float32)
    y = xf * lax.rsqrt(jnp.mean(xf * xf, axis=-1, keepdims=True) + RMS_EPS)
    return (y * g.astype(jnp.float32)).astype(x.dtype)

def adaln(cond, w, b):
    return jnp.split(jax.nn.silu(cond) @ w + b, 6, axis=-1)

def modulate(h, shift, scale):
    return h * (1.0 + scale[:, None, :]) + shift[:, None, :]

def axial_rope(T):
    rows = T // GRID_W
    row = jnp.repeat(jnp.arange(rows, dtype=jnp.float32), GRID_W)
    col = jnp.tile(jnp.arange(GRID_W, dtype=jnp.float32), rows)
    n_freq = DQK_A // 4
    inv_freq = jnp.power(ROPE_BASE, -jnp.arange(n_freq, dtype=jnp.float32) / n_freq)
    ang = jnp.concatenate([row[:, None] * inv_freq, col[:, None] * inv_freq], axis=-1)
    return jnp.cos(ang), jnp.sin(ang)

def apply_rope(x, cos, sin):
    half = DQK_A // 2
    xf = x.astype(jnp.float32)
    x1, x2 = xf[..., :half], xf[..., half:]
    c = cos[:, None, None, :]
    s = sin[:, None, None, :]
    return jnp.concatenate([x1 * c - x2 * s, x2 * c + x1 * s], axis=-1).astype(x.dtype)

def centred_depthwise_conv(x, w):
    K = w.shape[0]
    pad = K // 2
    T = x.shape[1]
    xp = jnp.pad(x, ((0, 0), (pad, pad), (0, 0)))
    return sum(xp[:, j:j + T] * w[j] for j in range(K))

def _bidir(a_fwd, a_bwd):
    return jnp.concatenate([a_fwd, a_bwd[:, ::-1]], axis=0)

def _merge_dirs(h, B):
    return h[:B] + h[B:, ::-1]

def _dir_major(s):
    s = jnp.swapaxes(s, 0, 1)
    return s.reshape(s.shape[0] * s.shape[1], *s.shape[2:]).astype(jnp.float32)

def _batch_major(s, B):
    return jnp.swapaxes(s.reshape(2, B, *s.shape[1:]), 0, 1)

def _to_chunks(a, L):
    N, T, H = a.shape[:3]
    a = a.reshape(N, T // L, L, H, *a.shape[3:])
    return jnp.moveaxis(a, (1, 3), (0, 2))

def _from_chunks(a):
    a = jnp.moveaxis(a, (0, 2), (1, 3))
    N, nc, L, H = a.shape[:4]
    return a.reshape(N, nc * L, H, *a.shape[4:])

def diff_attention(q, k, v, lam):
    B, Tq = q.shape[:2]
    nb = Tq // Q_BLOCK
    qb = jnp.swapaxes(q.reshape(B, nb, Q_BLOCK, *q.shape[2:]), 0, 1)
    scale = DQK_A ** -0.5

    def one_block(qblk):
        s = jnp.einsum('bqhjd,bkhjd->bhjqk', qblk, k).astype(jnp.float32) * scale
        p = jax.nn.softmax(s, axis=-1)
        a = p[:, :, 0] - lam * p[:, :, 1]
        return jnp.einsum('bhqk,bkhe->bqhe', a.astype(v.dtype), v)

    o = lax.map(one_block, qb)
    return jnp.swapaxes(o, 0, 1).reshape(B, Tq, *o.shape[3:])

def mlstm_scan(q, k, v, log_i, log_f, C0, n0, m0):
    L = MLSTM_CHUNK
    causal = jnp.tril(jnp.ones((L, L), dtype=bool))

    def step(carry, inp):
        C, n, m = carry
        qc, kc, vc, ic, fc = inp
        b = jnp.cumsum(fc, axis=-1)
        a = b + m[..., None]
        dmat = jnp.where(causal, b[..., :, None] - b[..., None, :] + ic[..., None, :], NEG_BIG)
        m_t = jnp.maximum(a, jnp.max(dmat, axis=-1))
        w_inter = jnp.exp(a - m_t)
        s = jnp.einsum('nhtd,nhsd->nhts', qc, kc) * jnp.exp(dmat - m_t[..., None])
        num = w_inter[..., None] * jnp.einsum('nhtd,nhde->nhte', qc, C) + jnp.einsum('nhts,nhse->nhte', s, vc)
        den = w_inter * jnp.einsum('nhtd,nhd->nht', qc, n) + jnp.sum(s, axis=-1)
        h = num / jnp.maximum(jnp.abs(den), jnp.exp(-m_t))[..., None]
        b_end = b[..., -1]
        g = b_end[..., None] - b + ic
        m_new = jnp.maximum(b_end + m, jnp.max(g, axis=-1))
        w_old = jnp.exp(b_end + m - m_new)
        w_s = jnp.exp(g - m_new[..., None])
        C_new = w_old[..., None, None] * C + jnp.einsum('nhs,nhsd,nhse->nhde', w_s, kc, vc)
        n_new = w_old[..., None] * n + jnp.einsum('nhs,nhsd->nhd', w_s, kc)
        return (C_new, n_new, m_new), h

    xs = tuple(_to_chunks(a.astype(jnp.float32), L) for a in (q, k, v, log_i, log_f))
    (C, n, m), h = lax.scan(step, (C0, n0, m0), xs)
    return _from_chunks(h), C, n, m

def hgrn2_scan(q, k, v, log_f, S0):
    L = HGRN_CHUNK
    causal = jnp.tril(jnp.ones((L, L), dtype=bool))[:, :, None]

    def step(S, inp):
        qc, kc, vc, fc = inp
        b = jnp.cumsum(fc, axis=2)
        inter = jnp.einsum('nhtk,nhkv->nhtv', qc * jnp.exp(b), S)
        decay = jnp.exp(jnp.where(causal, b[:, :, :, None, :] - b[:, :, None, :, :], NEG_BIG))
        att = jnp.einsum('nhtk,nhsk,nhtsk->nhts', qc, kc, decay)
        b_end = b[:, :, -1:, :]
        S_new = jnp.exp(b_end[:, :, 0])[..., None] * S + jnp.einsum('nhsk,nhsv->nhkv', kc * jnp.exp(b_end - b), vc)
        return S_new, inter + jnp.einsum('nhts,nhsv->nhtv', att, vc)

    xs = tuple(_to_chunks(a.astype(jnp.float32), L) for a in (q, k, v, log_f))
    S, o = lax.scan(step, S0.astype(jnp.float32), xs)
    return _from_chunks(o), S

def dattn_mlstm_mixer(h, w_in, b_ig, b_fg, lam_p, conv_w, g_attn, g_mlstm, w_out, layer, rope, ctx):
    B, T, _ = h.shape
    aq, ak, av, bq, bk, bv, bo, bi, bf = jnp.split(h @ w_in, AB_SPLITS, axis=-1)
    aq = aq.reshape(B, T, H_A, 2, DQK_A)
    ak = ak.reshape(B, T, H_A, 2, DQK_A)
    av = av.reshape(B, T, H_A, DV_A)
    if rope is not None:
        aq = apply_rope(aq, *rope)
        ak = apply_rope(ak, *rope)
    keys, vals = ak, av
    if ctx is not None:
        keys = jnp.concatenate([ctx[0].reshape(B, -1, H_A, 2, DQK_A).astype(ak.dtype), ak], axis=1)
        vals = jnp.concatenate([ctx[1].astype(av.dtype), av], axis=1)
    lam_init = 0.8 - 0.6 * math.exp(-0.3 * layer)
    lp = lam_p.astype(jnp.float32)
    lam = jnp.exp(jnp.sum(lp[0] * lp[1])) - jnp.exp(jnp.sum(lp[2] * lp[3])) + lam_init
    o_a = rms_norm(diff_attention(aq, keys, vals, lam), g_attn) * (1.0 - lam_init)
    qk = jax.nn.silu(centred_depthwise_conv(jnp.concatenate([bq, bk], axis=-1), conv_w))
    bq, bk = jnp.split(qk, 2, axis=-1)
    bq = bq.reshape(B, T, H_B, DH_B)
    bk = bk.reshape(B, T, H_B, DH_B) * (DH_B ** -0.5)
    bv = bv.reshape(B, T, H_B, DH_B)
    log_i = bi.reshape(B, T, 2, H_B).astype(jnp.float32) + b_ig
    log_f = jax.nn.log_sigmoid(bf.reshape(B, T, 2, H_B).astype(jnp.float32) + b_fg)
    if ctx is None:
        C0 = jnp.zeros((2 * B, H_B, DH_B, DH_B), jnp.float32)
        n0 = jnp.zeros((2 * B, H_B, DH_B), jnp.float32)
        m0 = jnp.zeros((2 * B, H_B), jnp.float32)
    else:
        C0, n0, m0 = _dir_major(ctx[2]), _dir_major(ctx[3]), _dir_major(ctx[4])
    hs, C, n, m = mlstm_scan(_bidir(bq, bq), _bidir(bk, bk), _bidir(bv, bv),
                             _bidir(log_i[:, :, 0], log_i[:, :, 1]), _bidir(log_f[:, :, 0], log_f[:, :, 1]),
                             C0, n0, m0)
    h_b = _merge_dirs(hs, B).astype(h.dtype)
    o_b = jax.nn.sigmoid(bo.reshape(B, T, H_B, DH_B)) * rms_norm(h_b, g_mlstm)
    out = jnp.concatenate([o_a.reshape(B, T, W_A), o_b.reshape(B, T, W_B)], axis=-1) @ w_out
    ctx_new = (ak.reshape(B, T, H_A, 2 * DQK_A), av, _batch_major(C, B), _batch_major(n, B), _batch_major(m, B))
    return out, ctx_new

def hgrn2_mixer(h, w_in, b_f, gamma_lb, g_hgrn, w_out, layer, S0):
    B, T, _ = h.shape
    q, i, g, f_pre = jnp.split(h @ w_in, (W_C, 2 * W_C, 3 * W_C), axis=-1)
    f_pre = f_pre.reshape(B, T, 2, W_C).astype(jnp.float32) + b_f
    lbs = jnp.cumsum(jax.nn.softmax(gamma_lb.astype(jnp.float32), axis=0), axis=0)
    lb = jnp.maximum(lbs[layer] - lbs[0], 0.0)
    log_f = jnp.logaddexp(jnp.log(lb), jnp.log1p(-lb) + jax.nn.log_sigmoid(f_pre))
    k = (1.0 - lb) * jax.nn.sigmoid(-f_pre)
    shp = (B, T, 2, H_C, DH_C)
    log_f = log_f.reshape(shp)
    k = k.reshape(shp)
    q = q.reshape(B, T, H_C, DH_C)
    v = i.reshape(B, T, H_C, DH_C)
    S_init = jnp.zeros((2 * B, H_C, DH_C, DH_C), jnp.float32) if S0 is None else _dir_major(S0)
    o, S = hgrn2_scan(_bidir(q, q), _bidir(k[:, :, 0], k[:, :, 1]), _bidir(v, v),
                      _bidir(log_f[:, :, 0], log_f[:, :, 1]), S_init)
    o = rms_norm(_merge_dirs(o, B).astype(h.dtype), g_hgrn) * jax.nn.silu(g.reshape(B, T, H_C, DH_C))
    return o.reshape(B, T, W_C) @ w_out, _batch_major(S, B)

def expert_choice_moe(h, w_router, w_gate, w_up, w_down):
    B, T, D = h.shape
    cap = CAPACITY_FACTOR * T // N_EXPERTS
    aff = jax.nn.softmax((h @ w_router).astype(jnp.float32), axis=-1)
    gate, idx = lax.top_k(jnp.swapaxes(aff, 1, 2), cap)
    bidx = jnp.arange(B)[:, None, None]
    xin = h[bidx, idx]
    a = jnp.einsum('becd,edf->becf', xin, w_gate)
    u = jnp.einsum('becd,edf->becf', xin, w_up)
    y = jnp.einsum('becf,efd->becd', jax.nn.silu(a) * u, w_down) * gate[..., None].astype(h.dtype)
    return jnp.zeros_like(h).at[bidx, idx].add(y)

def _stream(x, cond, rope, cache, w_ada, b_ada, g_norm, g_final, w_in_ab, b_ig_ab, b_fg_ab, lam_ab, conv_ab,
            g_attn_ab, g_mlstm_ab, w_out_ab, w_in_c, b_f_c, gamma_lb, g_hgrn_c, w_out_c,
            w_router, w_gate_e, w_up_e, w_down_e):
    even_out, odd_out = [], []
    for l in range(DEPTH):
        j = l // 2
        sh1, sc1, gt1, sh2, sc2, gt2 = adaln(cond, w_ada[l], b_ada[l])
        h = modulate(rms_norm(x, g_norm[l, 0]), sh1, sc1)
        if l % 2 == 0:
            ctx = None if cache is None else tuple(a[:, j] for a in cache[:5])
            mix, ctx_new = dattn_mlstm_mixer(h, w_in_ab[j], b_ig_ab[j], b_fg_ab[j], lam_ab[j], conv_ab[j],
                                             g_attn_ab[j], g_mlstm_ab[j], w_out_ab[j], l, rope, ctx)
            even_out.append(ctx_new)
        else:
            S0 = None if cache is None else cache[5][:, j]
            mix, S_new = hgrn2_mixer(h, w_in_c[j], b_f_c[j], gamma_lb, g_hgrn_c[j], w_out_c[j], l, S0)
            odd_out.append(S_new)
        x = x + gt1[:, None, :] * mix
        h = modulate(rms_norm(x, g_norm[l, 1]), sh2, sc2)
        x = x + gt2[:, None, :] * expert_choice_moe(h, w_router[l], w_gate_e[l], w_up_e[l], w_down_e[l])
    return rms_norm(x, g_final), even_out, odd_out

def setup_inputs(seed: int = 0) -> dict:
    key = jax.random.key(seed)
    keys = iter(jax.random.split(key, 32))

    def nrm(shape, scale=1.0):
        return scale * jax.random.normal(next(keys), shape, dtype=jnp.float32)

    D = D_MODEL
    f_bias = jnp.linspace(3.0, 6.0, H_B, dtype=jnp.float32)
    return {
        'x_prompt': nrm((BATCH, SEQ, D)),
        'x_sample': nrm((DEC_BATCH, DEC_SEQ, D)),
        'cache_dattn_k': nrm((DEC_BATCH, N_EVEN, PAST_LEN, H_A, 2 * DQK_A)),
        'cache_dattn_v': nrm((DEC_BATCH, N_EVEN, PAST_LEN, H_A, DV_A)),
        'state_mlstm_C': nrm((DEC_BATCH, N_EVEN, 2, H_B, DH_B, DH_B), 0.1),
        'state_mlstm_n': nrm((DEC_BATCH, N_EVEN, 2, H_B, DH_B), 0.5),
        'state_mlstm_m': nrm((DEC_BATCH, N_EVEN, 2, H_B)),
        'state_hgrn_S': nrm((DEC_BATCH, N_ODD, 2, H_C, DH_C, DH_C), 0.5),
        'c': nrm((DEC_BATCH, D)),
        'c_ctx': nrm((D,)),
        'w_ada': nrm((DEPTH, D, 6 * D), 0.5 * D ** -0.5),
        'b_ada': nrm((DEPTH, 6 * D), 0.02),
        'g_norm': 1.0 + nrm((DEPTH, 2, D), 0.02),
        'g_final': 1.0 + nrm((D,), 0.02),
        'w_in_ab': nrm((N_EVEN, D, P_AB), D ** -0.5),
        'b_ig_ab': nrm((N_EVEN, 2, H_B), 0.1),
        'b_fg_ab': f_bias + nrm((N_EVEN, 2, H_B), 0.1),
        'lam_ab': nrm((N_EVEN, 4, DQK_A), 0.1),
        'conv_ab': nrm((N_EVEN, KCONV, 2 * W_B), KCONV ** -0.5),
        'g_attn_ab': 1.0 + nrm((N_EVEN, H_A, DV_A), 0.02),
        'g_mlstm_ab': 1.0 + nrm((N_EVEN, H_B, DH_B), 0.02),
        'w_out_ab': nrm((N_EVEN, W_A + W_B, D), (W_A + W_B) ** -0.5),
        'w_in_c': nrm((N_ODD, D, P_C), D ** -0.5),
        'b_f_c': nrm((N_ODD, 2, W_C), 0.1),
        'gamma_lb': nrm((DEPTH, W_C)),
        'g_hgrn_c': 1.0 + nrm((N_ODD, H_C, DH_C), 0.02),
        'w_out_c': nrm((N_ODD, W_C, D), W_C ** -0.5),
        'w_router': nrm((DEPTH, D, N_EXPERTS), D ** -0.5),
        'w_gate_e': nrm((DEPTH, N_EXPERTS, D, EXPERT_FF), D ** -0.5),
        'w_up_e': nrm((DEPTH, N_EXPERTS, D, EXPERT_FF), D ** -0.5),
        'w_down_e': nrm((DEPTH, N_EXPERTS, EXPERT_FF, D), EXPERT_FF ** -0.5),
    }

def reference(x_prompt, x_sample, cache_dattn_k, cache_dattn_v, state_mlstm_C, state_mlstm_n, state_mlstm_m,
              state_hgrn_S, c, c_ctx, w_ada, b_ada, g_norm, g_final, w_in_ab, b_ig_ab, b_fg_ab, lam_ab, conv_ab,
              g_attn_ab, g_mlstm_ab, w_out_ab, w_in_c, b_f_c, gamma_lb, g_hgrn_c, w_out_c,
              w_router, w_gate_e, w_up_e, w_down_e):
    cond_ctx = jnp.broadcast_to(c_ctx, (x_prompt.shape[0], D_MODEL))
    y_prompt, ev, od = _stream(x_prompt, cond_ctx, None, None, w_ada, b_ada, g_norm, g_final, w_in_ab, b_ig_ab,
                               b_fg_ab, lam_ab, conv_ab, g_attn_ab, g_mlstm_ab, w_out_ab, w_in_c, b_f_c, gamma_lb,
                               g_hgrn_c, w_out_c, w_router, w_gate_e, w_up_e, w_down_e)
    new_dattn_k = jnp.stack([e[0] for e in ev], axis=1)
    new_dattn_v = jnp.stack([e[1] for e in ev], axis=1)
    new_mlstm_C = jnp.stack([e[2] for e in ev], axis=1)
    new_mlstm_n = jnp.stack([e[3] for e in ev], axis=1)
    new_mlstm_m = jnp.stack([e[4] for e in ev], axis=1)
    new_hgrn_S = jnp.stack(od, axis=1)
    cache = (cache_dattn_k, cache_dattn_v, state_mlstm_C, state_mlstm_n, state_mlstm_m, state_hgrn_S)
    y_sample, _, _ = _stream(x_sample, c, axial_rope(x_sample.shape[1]), cache, w_ada, b_ada, g_norm, g_final,
                             w_in_ab, b_ig_ab, b_fg_ab, lam_ab, conv_ab, g_attn_ab, g_mlstm_ab, w_out_ab, w_in_c,
                             b_f_c, gamma_lb, g_hgrn_c, w_out_c, w_router, w_gate_e, w_up_e, w_down_e)
    return (y_prompt, y_sample, new_dattn_k, new_dattn_v, new_mlstm_C, new_mlstm_n, new_mlstm_m, new_hgrn_S)


_drawn_inputs = setup_inputs


def setup_inputs(seed=0):
    import zlib

    import numpy as np

    out = dict(_drawn_inputs(seed))
    spreads = {}
    factors = {'cache_dattn_k': 4.22,
     'cache_dattn_v': 3.678,
     'state_mlstm_C': 7.732,
     'state_mlstm_n': 8.0,
     'state_mlstm_m': 8.0,
     'state_hgrn_S': 4.199,
     'g_final': 7.465,
     'lam_ab': 8.0,
     'g_attn_ab': 8.0,
     'g_mlstm_ab': 28.977,
     'g_hgrn_c': 33.577}
    for name, (base, spread) in spreads.items():
        noise = np.random.default_rng([zlib.crc32(name.encode()), seed]).standard_normal(out[name].shape)
        drawn = base * np.exp(spread * noise) if base else spread * noise
        out[name] = jnp.asarray(drawn.astype(out[name].dtype))
    for name, factor in factors.items():
        out[name] = (out[name] * factor).astype(out[name].dtype)
    return out
```

```python
from contextlib import ExitStack

import numpy as np
import concourse.bass as bass
from concourse import mybir

P = 128
D = 1024
KT = D // P
T_S, T_P = 1024, 128
T = T_S + T_P
NT = T // P
NS = T_S // P
STREAMS = 2
DEPTH = 2
HEADS_A = HEADS_B = 4
HEADS_C = 8
DQK = 64
GRID_W = 64
EXPERTS = 16
CAP_S, CAP_P = 2 * T_S // EXPERTS, 2 * T_P // EXPERTS
CAP = CAP_S + CAP_P
PIECE = 512
SLOTS = 6
EPS = 1e-6
LAM_INIT = float(0.8 - 0.6 * np.exp(-0.3 * 0))
NEG = -1e30
LEVELS = 7

F32 = mybir.dt.float32
U32 = mybir.dt.uint32
I32 = mybir.dt.int32
ALU = mybir.AluOpType
ACT = mybir.ActivationFunctionType
AX_X = mybir.AxisListType.X


def fields(sizes):
    out, at = {}, 0
    for name, n in sizes:
        out[name] = (at, n)
        at += n
    return out, at


PARAMS, N_PARAMS = fields([
    ("c", KT), ("c_ctx", KT), ("b_ada", DEPTH * 6 * KT), ("g_norm", DEPTH * 2 * KT),
    ("g_attn", 4), ("g_mlstm", 4), ("conv", 3 * 8), ("b_f", 16), ("gamma", 16), ("g_hgrn", 8)])
CONSTS, N_CONSTS = fields([
    ("ident", P), ("ones", P), ("neg_fwd", P), ("neg_bwd", P)])


def weight_pieces(d):
    def cols(w, c):
        return w.rearrange("(k p) f -> p k f", p=P)[:, :, c * PIECE:(c + 1) * PIECE]

    out = [cols(d["w_ada"][l], c) for l in range(DEPTH) for c in range(12)]
    out += [cols(d["w_in_ab"][0], c) for c in AB_FEATURE + AB_TOKEN]
    for l in range(DEPTH):
        if l == 1:
            out += [cols(d["w_in_c"][0], c) for c in C_FEATURE + C_TOKEN]
        w_out = d["w_out_ab"][0] if l == 0 else d["w_out_c"][0]
        out += [cols(w_out, c) for c in range(2)]
        for e in range(EXPERTS):
            out += [cols(w, c) for c in range(2) for w in (d["w_gate_e"][l, e], d["w_up_e"][l, e])]
            out += [cols(d["w_down_e"][l, e], c) for c in range(2)]
    return out


AB_FEATURE, AB_TOKEN = [3, 4, 6], [0, 1, 2, 5]
C_FEATURE, C_TOKEN = [0, 1, 4, 5, 6, 7, 8, 9], [2, 3]
N_ADA = 24
AT_IN_AB = N_ADA
AT_OUT = [AT_IN_AB + 7, AT_IN_AB + 7 + 2 + 6 * EXPERTS + 10]
AT_EXPERTS = [a + 2 for a in AT_OUT]
AT_IN_C = AT_EXPERTS[0] + 6 * EXPERTS


class Shared:

    def __init__(self, nc, d, ctx, sb, dram, sems):
        self.nc, self.d, self.sems = nc, d, sems
        self.W = sb("weights", [P, SLOTS, KT, PIECE])
        self.pieces = weight_pieces(d)
        self.w_used = ctx.enter_context(nc.semaphore("w_used"))
        self.w_loaded = [ctx.enter_context(nc.semaphore(f"w_loaded{i}")) for i in range(SLOTS)]
        self.loaded_after = [0, 30, 30, 37, 37, 37, 37, 39, 39, 135, 135, 145, 145, 147, 147, 237, 237]
        self.ps = ctx.enter_context(nc.psum_tensor("ps", [P, 8 * PIECE], F32))
        self.par, self.cst = sb("params_sb", [P, N_PARAMS]), sb("consts_sb", [P, N_CONSTS])
        self.eps = sb("eps", [P, 1])
        self.level_masks = sb("level_masks_sb", [P, LEVELS, P], U32)
        self.w_router = sb("w_router_sb", [P, DEPTH, KT, EXPERTS])
        self.lam_row = sb("lam_row", [1, 4 * DQK])
        self.hT = sb("hT", [P, KT, T])
        self.ada, self.scale = sb("ada", [P, STREAMS, DEPTH * 6 * KT]), sb("scale", [P, DEPTH, 2, STREAMS, KT])
        self.idx_s, self.gate_s = sb("idx_s", [P, EXPERTS], I32), sb("gate_s", [P, EXPERTS])
        self.idx_p, self.gate_p = sb("idx_p", [CAP_P, EXPERTS], I32), sb("gate_p", [CAP_P, EXPERTS])
        self.w_arg, self.w_state = sb("w_arg", [P, 2, NT, HEADS_B]), sb("w_state", [P, 2, NT, HEADS_B])
        self.xres, self.xnorm = dram("x_residual", [T, D]), dram("x_norm", [T, D])
        self.gate1_rows = dram("gate1_rows", [DEPTH, STREAMS, D])
        self.featT, self.tok = dram("feature_rows", [32, P, T]), dram("token_rows", [4, NT, P, PIECE])
        self.gate_rows, self.mrows = dram("mlstm_gate_rows", [4, 4, T]), dram("mlstm_rows", [2, 2, 4, T])
        self.msmall = dram("mlstm_chunks", [2, 2, 4, NT])

    def p(self, name):
        at, n = PARAMS[name]
        return self.par[:, at:at + n]

    def c(self, name):
        at, n = CONSTS[name]
        return self.cst[:, at:at + n]


class Steps:

    def __init__(self, eng, sem, turn=0, per=0):
        self.eng, self.sem, self.base, self.k, self.per = eng, sem, turn * per, 0, per

    def did(self, ins):
        ins.then_inc(self.sem, 1)
        self.k += 1

    def wait(self):
        self.eng.wait_ge(self.sem, self.base + self.k)

    def close(self):
        assert self.k == self.per, self.k


def load_piece(K, sp, n, src=None):
    if n >= SLOTS:
        sp.wait_ge(K.w_used, n - SLOTS + 1)
    sp.dma_start(K.W[:, n % SLOTS], K.pieces[n] if src is None else src).then_inc(K.w_loaded[n % SLOTS], 16)


def wait_piece(K, pe, n):
    pe.wait_ge(K.w_loaded[n % SLOTS], 16 * (n // SLOTS + 1))


def stage_adaln(K):
    nc, d = K.nc, K.d
    with ExitStack() as ctx:
        s = K.sems("ada", "par", "silu", "added", "mod", "turned", "rows", "rows_out", "x_copied", "consts", "pack", "copied", "columns", "turning")
        condT = ctx.enter_context(nc.sbuf_tensor("condT", [P, KT, STREAMS], F32))
        cpack = ctx.enter_context(nc.sbuf_tensor("cpack", [P, KT, STREAMS], F32))
        row2 = ctx.enter_context(nc.sbuf_tensor("ada_rows", [STREAMS, 2, PIECE], F32))
        rows = ctx.enter_context(nc.sbuf_tensor("gate_rows", [KT, DEPTH * STREAMS * P], F32))
        with nc.Block() as block:
            @block.sync
            def _(sp):
                for n in range(SLOTS):
                    load_piece(K, sp, n)
                for n in range(SLOTS, N_ADA + SLOTS):
                    load_piece(K, sp, n)

            @block.gpsimd
            def _(pool):
                pool.dma_start(K.xres[0:T_S, :], d["x_sample"][0]).then_inc(s["x_copied"], 16)
                pool.dma_start(K.xres[T_S:T, :], d["x_prompt"][0]).then_inc(s["x_copied"], 16)
                pool.wait_ge(s["rows"], 1)
                for l in range(DEPTH):
                    for r in range(STREAMS):
                        j = (l * STREAMS + r) * P
                        pool.dma_start(K.gate1_rows[l, r].rearrange("(k p) -> k p", p=P),
                                       rows[:, j:j + P]).then_inc(s["rows_out"], 16)
                pool.wait_ge(s["rows_out"], 16 * DEPTH * STREAMS)
                pool.wait_ge(s["x_copied"], 32)

            @block.scalar
            def _(act):
                act.dma_start(K.par[:], d["params"]).then_inc(s["par"], 16)
                act.dma_start(K.cst[:], d["consts"]).then_inc(s["consts"], 16)
                act.dma_start(K.level_masks[:], d["level_masks"]).then_inc(s["consts"], 16)
                act.dma_start(K.w_router[:], d["w_router"].rearrange("l (k p) e -> p l k e", p=P)).then_inc(s["consts"], 16)
                act.dma_start(K.lam_row[:], d["lam_ab"]).then_inc(s["consts"], 16)
                act.wait_ge(s["pack"], 3)
                act.activation(condT[:], cpack[:], ACT.Silu).then_inc(s["silu"], 1)
                act.sem_inc(s["copied"], 2)
                with act.Fori(0, N_ADA // 2) as i:
                    for par in range(2):
                        q = i * 2 + par
                        act.wait_ge(K.w_used, q + 1)
                        act.wait_ge(s["added"], q + 1)
                        act.copy(row2[:, par], K.ps[0:STREAMS, par * PIECE:(par + 1) * PIECE]).then_inc(s["copied"], 1)
                act.wait_ge(s["consts"], 64)

            @block.tensor
            def _(pe):
                def product(q, bank, turn):
                    pe.wait_ge(s["copied"], q + 1)
                    pe.wait_ge(K.w_loaded[bank], turn * 16 + 16)
                    for k in range(KT):
                        mm = pe.matmul(K.ps[0:STREAMS, bank % 2 * PIECE:(bank % 2 + 1) * PIECE], condT[:, k, :], K.W[:, bank, k],
                                       start=(k == 0), stop=(k == KT - 1))
                    mm.then_inc(K.w_used, 1)

                def turn_rows(q, bank):
                    pe.wait_ge(s["copied"], q + 3)
                    pe.wait_ge(s["added"], q + 1)
                    pe.sem_inc(s["turning"], 1)
                    for ft in range(4):
                        a = (2 + bank % 2) * PIECE + ft * STREAMS
                        mm = pe.transpose(K.ps[:, a:a + STREAMS], row2[:, bank % 2, ft * P:(ft + 1) * P], K.cst[0:STREAMS, 0:STREAMS])
                    mm.then_inc(s["columns"], 1)
                pe.wait_ge(s["silu"], 1)
                pe.wait_ge(s["consts"], 64)
                with pe.Fori(0, N_ADA // SLOTS) as i:
                    for slot in range(SLOTS):
                        product(i * SLOTS + slot, slot, i)
                        if slot:
                            turn_rows(i * SLOTS + slot - 1, slot - 1)
                    turn_rows(i * SLOTS + SLOTS - 1, SLOTS - 1)
                pe.wait_ge(s["mod"], 1)
                for l in range(DEPTH):
                    for r in range(STREAMS):
                        j = (l * STREAMS + r) * P
                        mm = pe.transpose(K.ps[0:KT, 4 * PIECE + j:4 * PIECE + j + P],
                                          K.ada[:, r, l * 48 + 16:l * 48 + 24], K.c("ident"))
                mm.then_inc(s["turned"], 1)

            @block.vector
            def _(dve):
                dve.sem_inc(s["added"], 2)
                dve.wait_ge(s["par"], 16)
                dve.tensor_copy(cpack[:, :, 0], K.p("c")).then_inc(s["pack"], 1)
                dve.tensor_copy(cpack[:, :, 1], K.p("c_ctx")).then_inc(s["pack"], 1)
                dve.memset(K.eps[:], EPS).then_inc(s["pack"], 1)
                b_ada = PARAMS["b_ada"][0]
                with dve.Fori(0, N_ADA // 2) as i:
                    for par in range(2):
                        q = i * 2 + par
                        dve.wait_ge(s["columns"], q + 1)
                        for r in range(STREAMS):
                            a = (2 + par) * PIECE
                            ins = dve.tensor_tensor(
                                K.ada[:, r, bass.ds(q * 4, 4)],
                                K.ps[:, a:a + 4 * STREAMS].rearrange("p (f r) -> p r f", r=STREAMS)[:, r],
                                K.par[:, bass.ds(q * 4 + b_ada, 4)], ALU.add)
                        ins.then_inc(s["added"], 1)
                dve.wait_ge(s["added"], 2 + N_ADA)
                gn = PARAMS["g_norm"][0]
                for l in range(DEPTH):
                    for j in range(2):
                        for r in range(STREAMS):
                            g0 = gn + (l * 2 + j) * KT
                            c = l * 48 + (3 * j + 1) * KT
                            ins = dve.scalar_tensor_tensor(K.scale[:, l, j, r, :], K.ada[:, r, c:c + KT], 1.0,
                                                           K.par[:, g0:g0 + KT], ALU.add, ALU.mult)
                ins.then_inc(s["mod"], 1)
                dve.wait_ge(s["turned"], 1)
                dve.tensor_copy(rows[:], K.ps[0:KT, 4 * PIECE:4 * PIECE + DEPTH * STREAMS * P]).then_inc(s["rows"], 1)


def over_tiles(eng, body):
    with eng.Fori(0, NS // 2) as i:
        body([(i * 2, 0, i), (i * 2 + 1, 1, i)], 0)
    body([(NS, 0, NS // 2)], 1)


def stage_norm(K, l, j, store):
    nc = K.nc
    with ExitStack() as ctx:
        s = K.sems(f"norm{l}{j}", "x_in0", "x_in1", "xn_ready", "sumsq", "root", "rcp", "turned", "act_evac", "dve_evac", "stored0", "stored1")
        x_in, stored = [s["x_in0"], s["x_in1"]], [s["stored0"], s["stored1"]]
        xt = ctx.enter_context(nc.sbuf_tensor(f"xt{l}{j}", [P, 2, D], F32))
        xn = ctx.enter_context(nc.sbuf_tensor(f"xn{l}{j}", [P, 2, D], F32))
        junk = ctx.enter_context(nc.sbuf_tensor(f"junk{l}{j}", [P, D], F32))
        st = ctx.enter_context(nc.sbuf_tensor(f"stat{l}{j}", [P, 2, 4], F32))
        shift_at = l * 48 + 3 * j * KT
        with nc.Block() as block:
            @block.gpsimd
            def _(pool):
                def body(tiles, r):
                    for t, b, u in tiles:
                        pool.wait_ge(s["xn_ready"], t + 1)
                        pool.dma_start(xt[:, b], K.xres[bass.ds(t * P, P), :]).then_inc(x_in[b], 16)
                over_tiles(pool, body)

            @block.sync
            def _(sp):
                if store:
                    sp.sem_inc(stored[0], 16)
                    sp.sem_inc(stored[1], 16)

                    def body(tiles, r):
                        for t, b, u in tiles:
                            sp.wait_ge(s["xn_ready"], t + 3)
                            sp.dma_start(K.xnorm[bass.ds(t * P, P), :], xn[:, b]).then_inc(stored[b], 16)
                    over_tiles(sp, body)
                    sp.wait_ge(stored[0], 16 + 16 * 5)
                    sp.wait_ge(stored[1], 16 + 16 * 4)

            @block.scalar
            def _(act):
                def body(tiles, r):
                    for t, b, u in tiles:
                        act.wait_ge(x_in[b], u * 16 + 16)
                        act.activation(junk[:], xt[:, b], ACT.Square, accum_out=st[:, b, 0:1]).then_inc(s["sumsq"], 1)
                        act.wait_ge(s["sumsq"], t + 1)
                        act.activation(st[:, b, 1:2], st[:, b, 0:1], ACT.Sqrt, bias=K.eps[:], scale=1.0 / D).then_inc(s["root"], 1)
                    for t, b, u in tiles:
                        act.wait_ge(s["turned"], t + 3)
                        for k in range(KT // 2):
                            ins = act.activation(K.hT[:, k, bass.ds(t * P, P)], K.ps[:, b * D + k * P:b * D + (k + 1) * P],
                                                 ACT.Identity, bias=K.ada[:, r, shift_at + k:shift_at + k + 1],
                                                 scale=K.scale[:, l, j, r, k:k + 1])
                        ins.then_inc(s["act_evac"], 1)
                act.sem_inc(s["act_evac"], 2)
                over_tiles(act, body)

            @block.tensor
            def _(pe):
                def body(tiles, r):
                    for t, b, u in tiles:
                        pe.wait_ge(s["xn_ready"], t + 3)
                        pe.wait_ge(s["act_evac"], t + 1)
                        pe.wait_ge(s["dve_evac"], t + 1)
                        for k in range(KT):
                            mm = pe.transpose(K.ps[:, b * D + k * P:b * D + (k + 1) * P],
                                              xn[:, b, k * P:(k + 1) * P], K.c("ident"))
                        mm.then_inc(s["turned"], 1)
                pe.sem_inc(s["turned"], 2)
                over_tiles(pe, body)

            @block.vector
            def _(dve):
                def body(tiles, r):
                    for t, b, u in tiles:
                        dve.wait_ge(s["root"], t + 1)
                        dve.reciprocal(st[:, b, 2:3], st[:, b, 1:2]).then_inc(s["rcp"], 1)
                        dve.wait_ge(s["rcp"], t + 1)
                        dve.wait_ge(s["turned"], t + 1)
                        if store:
                            dve.wait_ge(stored[b], u * 16 + 16)
                        dve.tensor_scalar(xn[:, b], xt[:, b], st[:, b, 2:3], None, ALU.mult).then_inc(s["xn_ready"], 1)
                    for t, b, u in tiles:
                        dve.wait_ge(s["turned"], t + 3)
                        for k in range(KT // 2, KT):
                            ins = dve.tensor_scalar(K.hT[:, k, bass.ds(t * P, P)], K.ps[:, b * D + k * P:b * D + (k + 1) * P],
                                                    K.scale[:, l, j, r, k:k + 1],
                                                    K.ada[:, r, shift_at + k:shift_at + k + 1], ALU.mult, ALU.add)
                        ins.then_inc(s["dve_evac"], 1)
                dve.sem_inc(s["xn_ready"], 2)
                dve.sem_inc(s["dve_evac"], 2)
                over_tiles(dve, body)


def stage_project(K, name, at, n_feature, n_token, gates):
    nc, d = K.nc, K.d
    TC = T // 3
    n_groups = n_feature * 12 + n_token * NT
    with ExitStack() as ctx:
        s = K.sems(name, "group", "even_out", "odd_out", "stored0", "stored1", "stored2", "stored3",
                   "wg_in", "gates", "round_out", "gates_out", "gates_stored")
        stored = [s["stored0"], s["stored1"], s["stored2"], s["stored3"]]
        stg = ctx.enter_context(nc.sbuf_tensor(f"{name}_stage", [P, 4, PIECE], F32))
        if gates:
            wg = ctx.enter_context(nc.sbuf_tensor("w_gates", [P, KT, 16], F32))
            gsb = ctx.enter_context(nc.sbuf_tensor("gates_sb", [4, 4, T], F32))

        def groups():
            for f in range(n_feature):
                yield "feature", f, f * 12
            for t in range(n_token):
                yield "token", t, n_feature * 12 + t * NT

        def take_out(eng, copy, mine, out_sem):
            def one(g, bank, width, use):
                eng.wait_ge(s["group"], g + 1)
                eng.wait_ge(stored[bank], use * 16 + 16)
                copy(stg[:, bank, 0:width], K.ps[:, bank * PIECE:bank * PIECE + width]).then_inc(out_sem, 1)
            for kind, n, g0 in groups():
                if kind == "feature":
                    with eng.Fori(0, 3) as c:
                        for ft in range(mine, 4, 2):
                            one(c * 4 + (g0 + ft), ft, TC, c + g0 // 4)
                else:
                    for t in range(NT):
                        g = g0 + t
                        if g % 2 == mine:
                            one(g, g % 4, PIECE, g // 4)

        with nc.Block() as block:
            @block.sync
            def _(sp):
                for sem in stored:
                    sp.sem_inc(sem, 16)

                def out(g):
                    return s["even_out"] if g % 2 == 0 else s["odd_out"]
                for kind, n, g0 in groups():
                    if kind == "feature":
                        with sp.Fori(0, 3) as c:
                            for ft in range(4):
                                sp.wait_ge(out(ft), c * 2 + ((g0 + ft) // 2 + 1))
                                sp.dma_start(K.featT[n * 4 + ft, :, bass.ds(c * TC, TC)],
                                             stg[:, ft, 0:TC]).then_inc(stored[ft], 16)
                    else:
                        for t in range(NT):
                            g = g0 + t
                            sp.wait_ge(out(g), g // 2 + 1)
                            sp.dma_start(K.tok[n, t], stg[:, g % 4, :]).then_inc(stored[g % 4], 16)
                    load_piece(K, sp, at + SLOTS + (n if kind == "feature" else n_feature + n))
                for b in range(4):
                    sp.wait_ge(stored[b], 16 + 16 * len(range(b, n_groups, 4)))

            @block.gpsimd
            def _(pool):
                if gates:
                    pool.dma_start(wg[:], d["w_in_ab"][0].rearrange("(k p) f -> p k f", p=P)[:, :, 3584:3600]).then_inc(s["wg_in"], 16)
                    pool.wait_ge(s["gates_out"], 1)
                    pool.dma_start(K.gate_rows.rearrange("k h t -> h k t"), gsb[:]).then_inc(s["gates_stored"], 16)
                    pool.wait_ge(s["gates_stored"], 16)

            @block.scalar
            def _(act):
                take_out(act, act.copy, 1, s["odd_out"])

            @block.vector
            def _(dve):
                take_out(dve, dve.tensor_copy, 0, s["even_out"])
                if gates:
                    for rnd in range(2):
                        dve.wait_ge(s["gates"], rnd + 1)
                        ins = dve.tensor_copy(gsb[:, 2 * rnd:2 * rnd + 2, :],
                                              K.ps[0:4, 0:2 * T].rearrange("h (k t) -> h k t", k=2))
                        ins.then_inc(s["gates_out"] if rnd else s["round_out"], 1)

            @block.tensor
            def _(pe):
                def bank_free(g_mod, count):
                    pe.wait_ge(s["even_out"] if g_mod % 2 == 0 else s["odd_out"], count)
                for kind, n, g0 in groups():
                    piece = at + (n if kind == "feature" else n_feature + n)
                    wait_piece(K, pe, piece)
                    w = K.W[:, piece % SLOTS]
                    if kind == "feature":
                        def chunk(c, first):
                            for ft in range(4):
                                if not first:
                                    bank_free(ft, c * 2 + ((g0 + ft - 4) // 2 + 1))
                                for k in range(KT):
                                    mm = pe.matmul(K.ps[:, ft * PIECE:ft * PIECE + TC], w[:, k, ft * P:(ft + 1) * P],
                                                   K.hT[:, k, bass.ds(c * TC, TC)], start=(k == 0), stop=(k == KT - 1))
                                mm.then_inc(s["group"], 1)
                        if g0 == 0:
                            chunk(0, True)
                            with pe.Fori(1, 3) as c:
                                chunk(c, False)
                        else:
                            with pe.Fori(0, 3) as c:
                                chunk(c, False)
                    else:
                        for t in range(NT):
                            g = g0 + t
                            bank_free(g, (g - 4) // 2 + 1)
                            for k in range(KT):
                                mm = pe.matmul(K.ps[:, g % 4 * PIECE:(g % 4 + 1) * PIECE],
                                               K.hT[:, k, t * P:(t + 1) * P], w[:, k, :], start=(k == 0), stop=(k == KT - 1))
                            mm.then_inc(s["group"], 1)
                    pe.drain().then_inc(K.w_used, 1)
                if gates:
                    pe.wait_ge(s["wg_in"], 16)
                    bank_free(0, len(range(0, n_groups, 2)))
                    bank_free(1, len(range(1, n_groups, 2)))
                    for rnd in range(2):
                        if rnd:
                            pe.wait_ge(s["round_out"], 1)
                        for q in range(2):
                            kind = 2 * rnd + q
                            for c0, n in [(q * T + a, b) for a, b in ((0, 384), (384, 384), (768, 384))]:
                                cut = min(n, PIECE - c0 % PIECE)
                                for a, m in ((c0, cut), (c0 + cut, n - cut)):
                                    if m:
                                        for k in range(KT):
                                            mm = pe.matmul(K.ps[0:4, a:a + m], wg[:, k, kind * 4:kind * 4 + 4],
                                                           K.hT[:, k, a - q * T:a - q * T + m], start=(k == 0), stop=(k == KT - 1))
                        mm.then_inc(s["gates"], 1)


def stage_attention(K):
    nc, d = K.nc, K.d
    NK = NT + 1
    KEYS = T
    SC = float(DQK) ** -0.5
    CH = KEYS // 3
    PER_TILE = 6
    with ExitStack() as ctx:
        def sb(name, shape):
            return ctx.enter_context(nc.sbuf_tensor(f"att_{name}", shape, F32))
        s = K.sems("att", "q_in", "k_in", "v_in", "rope_in", "steps", "roped", "turned", "qkT", "scored",
                   "bias", "expd", "mixed", "aT", "aT_out", "av", "av_out", "squared", "summed", "root", "act_steps",
                   "lam_steps", "lam_e", "lam_ps", "kept")
        q, k, v = sb("q", [P, NT, P]), sb("k", [P, NK, P]), sb("v", [P, NK, P])
        qr, tmp = sb("qr", [P, NS, P]), sb("tmp", [P, NS, P])
        kr = sb("kr", [P, NS, P])
        rope = sb("rope", [P, 2, NS, P])
        qT, kT = sb("qT", [P, T]), sb("kT", [P, NK * P])
        p0, p1 = sb("p0", [P, KEYS]), sb("p1", [P, KEYS])
        aT = sb("aT", [P, KEYS])
        oT, sq = sb("oT", [P, T]), aT
        st = sb("stat", [P, 2, 8])
        lam = sb("lam", [1, 4 * DQK])
        nlam = sb("nlam", [P, 1])
        gs = sb("g_scaled", [P, HEADS_A])
        S0 = 0
        TR, AV = 6 * PIECE, 7 * PIECE

        def q_cols(i):
            return slice(i * P, (i + 1) * P)

        def keys_of(i):
            return (0, NT) if i < NS else (KEYS, 1)

        def chunks(n_tiles):
            return [(c, CH) for c in range(3)] if n_tiles == NT else [(0, P)]

        def scores_ps(j, n_tiles):
            a = S0 + j * 3 * PIECE
            if n_tiles == 1:
                return K.ps[:, a:a + P].rearrange("p (c n) -> p c n", c=1)
            return K.ps[:, a:a + 3 * PIECE].rearrange("p (c n) -> p c n", c=3)[:, :, 0:CH]

        def rounds(n_tiles):
            return [(a, min(4, n_tiles - a)) for a in range(0, n_tiles, 4)]
        ROUNDS = [sum(len(rounds(keys_of(j)[1])) for j in range(i)) for i in range(NT + 1)]

        with nc.Block() as block:
            @block.sync
            def _(sp):
                sp.dma_start(d["o_new_k"][0, 0].rearrange("t h f -> t (h f)"), K.tok[1, NS]).then_inc(s["kept"], 16)
                sp.dma_start(d["o_new_v"][0, 0].rearrange("t h f -> t (h f)"), K.tok[2, NS]).then_inc(s["kept"], 16)
                sp.wait_ge(s["kept"], 32)

            @block.gpsimd
            def _(pool):
                pool.dma_start(rope[:], d["rope"]).then_inc(s["rope_in"], 16)
                tok = K.tok.rearrange("n t p f -> n p t f")
                with pool.Fori(0, HEADS_A) as h:
                    pool.wait_ge(s["turned"], h * 2 + 1)
                    pool.dma_start(q[:], tok[0, :, :, bass.ds(h * P, P)]).then_inc(s["q_in"], 16)
                    pool.dma_start(k[:, 1:NK], tok[1, :, :, bass.ds(h * P, P)]).then_inc(s["k_in"], 16)
                    pool.dma_start(k[:, 0], d["cache_dattn_k"][0, 0, :, bass.ds(h, 1), :].rearrange("t a f -> t (a f)")).then_inc(s["k_in"], 16)
                    pool.wait_ge(s["av"], h * NT + 1)
                    pool.dma_start(v[:, 1:NK], tok[2, :, :, bass.ds(h * P, P)]).then_inc(s["v_in"], 16)
                    pool.dma_start(v[:, 0], d["cache_dattn_v"][0, 0, :, bass.ds(h, 1), :].rearrange("t a f -> t (a f)")).then_inc(s["v_in"], 16)

            @block.tensor
            def _(pe):
                pe.sem_inc(s["av"], 1)
                pe.sem_inc(s["turned"], 1)
                pe.wait_ge(s["lam_steps"], 6)
                pe.matmul(K.ps[:, AV:AV + 1], K.cst[0:1, P:2 * P], lam[0:1, 8:9], start=True, stop=True).then_inc(s["lam_ps"], 1)
                with pe.Fori(0, HEADS_A) as h:
                    pe.wait_ge(s["roped"], h * 2 + 1)
                    pe.wait_ge(s["root"], h + 1)
                    for i in range(NT):
                        src = qr[:, i] if i < NS else q[:, i]
                        mm = pe.transpose(K.ps[:, i * P:(i + 1) * P], src, K.c("ident"))
                    mm.then_inc(s["turned"], 1)
                    pe.wait_ge(s["roped"], h * 2 + 2)
                    for i in range(NK):
                        src = kr[:, i - 1] if 1 <= i <= NS else k[:, i]
                        mm = pe.transpose(K.ps[:, 3 * PIECE + i * P:3 * PIECE + (i + 1) * P], src, K.c("ident"))
                    mm.then_inc(s["turned"], 1)
                    pe.wait_ge(s["qkT"], h * 2 + 2)

                    def score(i):
                        k0, n = keys_of(i)
                        for j in range(2):
                            if i > 0:
                                pe.wait_ge(s["expd"], h * 2 * NT + (2 * (i - 1) + j + 1))
                            rows = slice(j * DQK, (j + 1) * DQK)
                            for c, w in chunks(n):
                                a = S0 + (3 * j + c) * PIECE
                                mm = pe.matmul(K.ps[:, a:a + w], qT[rows, q_cols(i)],
                                               kT[rows, k0 + c * CH:k0 + c * CH + w], start=True, stop=True)
                            mm.then_inc(s["scored"], 1)

                    def turn_and_product(i):
                        k0, n = keys_of(i)
                        pe.wait_ge(s["mixed"], h * NT + (i + 1))
                        for r, (a, m) in enumerate(rounds(n)):
                            done = ROUNDS[i] + r
                            pe.wait_ge(s["aT_out"], h * ROUNDS[NT] + done + 1)
                            for y in range(m):
                                mm = pe.transpose(K.ps[:, TR + y * P:TR + (y + 1) * P],
                                                  p0[:, (a + y) * P:(a + y + 1) * P], K.c("ident"))
                            mm.then_inc(s["aT"], 1)
                        pe.wait_ge(s["aT_out"], h * ROUNDS[NT] + ROUNDS[i + 1] + 1)
                        pe.wait_ge(s["v_in"], h * 32 + 32)
                        pe.wait_ge(s["av_out"], h * NT + i + 1)
                        for y in range(n):
                            mm = pe.matmul(K.ps[:, AV:AV + P], v[:, k0 // P + y], aT[:, y * P:(y + 1) * P],
                                           start=(y == 0), stop=(y == n - 1))
                        mm.then_inc(s["av"], 1)

                    score(0)
                    for i in range(NT):
                        if i + 1 < NT:
                            score(i + 1)
                        turn_and_product(i)
                    pe.wait_ge(s["squared"], h + 1)
                    for c in range(3):
                        mm = pe.matmul(K.ps[:, c * PIECE:c * PIECE + CH], K.c("ones"), sq[:, c * CH:(c + 1) * CH],
                                       start=True, stop=True)
                    mm.then_inc(s["summed"], 1)

            @block.scalar
            def _(act):
                act.sem_inc(s["av_out"], 1)
                act.sem_inc(s["aT_out"], 1)
                act.sem_inc(s["root"], 1)
                act.wait_ge(s["lam_steps"], 4)
                act.activation(lam[0:1, 4:6], lam[0:1, 0:2], ACT.Exp).then_inc(s["lam_e"], 1)
                with act.Fori(0, HEADS_A) as h:
                    act.wait_ge(s["turned"], h * 2 + 1 + 1)
                    act.copy(qT[:], K.ps[:, 0:T]).then_inc(s["qkT"], 1)
                    act.wait_ge(s["turned"], h * 2 + 2 + 1)
                    act.copy(kT[:], K.ps[:, 3 * PIECE:3 * PIECE + NK * P]).then_inc(s["qkT"], 1)

                    def exps(i):
                        k0, n = keys_of(i)
                        for j, p in enumerate((p0, p1)):
                            act.wait_ge(s["bias"], h * 2 * NT + (2 * i + j + 1))
                            if i > 0:
                                if j == 0:
                                    act.wait_ge(s["aT"], h * ROUNDS[NT] + ROUNDS[i])
                                else:
                                    act.wait_ge(s["mixed"], h * NT + i)
                            act.activation(p[:, 0:n * P].rearrange("p (c n) -> p c n", c=len(chunks(n))), scores_ps(j, n),
                                           ACT.Exp, bias=st[:, i % 2, 2 + j:3 + j], scale=SC,
                                           accum_out=st[:, i % 2, 4 + j:5 + j]).then_inc(s["expd"], 1)

                    exps(0)
                    for i in range(NT):
                        k0, n = keys_of(i)
                        for r, (a, m) in enumerate(rounds(n)):
                            act.wait_ge(s["aT"], h * ROUNDS[NT] + (ROUNDS[i] + r + 1))
                            if i > 0:
                                act.wait_ge(s["av"], h * NT + i + 1)
                            act.copy(aT[:, a * P:(a + m) * P], K.ps[:, TR:TR + m * P]).then_inc(s["aT_out"], 1)
                        if i + 1 < NT:
                            exps(i + 1)
                        act.wait_ge(s["av"], h * NT + (i + 1) + 1)
                        act.copy(oT[:, q_cols(i)], K.ps[:, AV:AV + P]).then_inc(s["av_out"], 1)
                    act.wait_ge(s["av_out"], h * NT + NT + 1)
                    act.activation(sq[:], oT[:], ACT.Square).then_inc(s["squared"], 1)
                    act.wait_ge(s["summed"], h + 1)
                    act.activation(sq[:].rearrange("p (c n) -> p c n", c=3), scores_ps(0, NT), ACT.Sqrt,
                                   bias=K.eps[:], scale=1.0 / P).then_inc(s["root"], 1)
                    act.wait_ge(s["act_steps"], h + 1)

            @block.vector
            def _(dve):
                one = Steps(dve, s["lam_steps"])
                one.did(dve.tensor_tensor(lam[0:1, 16:16 + DQK], K.lam_row[0:1, 0:DQK], K.lam_row[0:1, DQK:2 * DQK], ALU.mult))
                one.did(dve.tensor_tensor(lam[0:1, 96:96 + DQK], K.lam_row[0:1, 2 * DQK:3 * DQK], K.lam_row[0:1, 3 * DQK:4 * DQK], ALU.mult))
                one.wait()
                one.did(dve.tensor_reduce(lam[0:1, 0:1], lam[0:1, 16:16 + DQK], AX_X, ALU.add))
                one.did(dve.tensor_reduce(lam[0:1, 1:2], lam[0:1, 96:96 + DQK], AX_X, ALU.add))
                dve.wait_ge(s["lam_e"], 1)
                one.did(dve.tensor_tensor(lam[0:1, 6:7], lam[0:1, 5:6], lam[0:1, 4:5], ALU.subtract))
                one.wait()
                one.did(dve.tensor_scalar(lam[0:1, 8:9], lam[0:1, 6:7], -LAM_INIT, None, ALU.add))
                dve.wait_ge(s["lam_ps"], 1)
                one.did(dve.tensor_copy(nlam[:], K.ps[:, AV:AV + 1]))
                one.did(dve.tensor_scalar(gs[:], K.p("g_attn"), 1.0 - LAM_INIT, None, ALU.mult))
                one.wait()
                dve.wait_ge(s["rope_in"], 16)
                with dve.Fori(0, HEADS_A) as h:
                    step = Steps(dve, s["steps"], h, 8 + NT * PER_TILE + 1)
                    for src, out, off, sem, per in ((q, qr, 0, s["q_in"], 16), (k, kr, 1, s["k_in"], 32)):
                        x = src[:, off:off + NS].rearrange("p t (j a f) -> p (t j) a f", j=2, a=2)
                        tp = tmp[:].rearrange("p t (j a f) -> p (t j) a f", j=2, a=2)
                        sn = rope[:, 1].rearrange("p t (j a f) -> p (t j) a f", j=2, a=2)
                        dve.wait_ge(sem, h * per + per)
                        step.did(dve.tensor_tensor(out[:], src[:, off:off + NS], rope[:, 0], ALU.mult))
                        step.did(dve.tensor_tensor(tp[:, :, 0], x[:, :, 1], sn[:, :, 0], ALU.mult))
                        step.did(dve.tensor_tensor(tp[:, :, 1], x[:, :, 0], sn[:, :, 1], ALU.mult))
                        step.wait()
                        step.did(dve.tensor_tensor(out[:], out[:], tmp[:], ALU.add))
                        step.wait()
                        dve.sem_inc(s["roped"], 1)

                    def softmax_bias(i):
                        k0, n = keys_of(i)
                        b = i % 2
                        for j in range(2):
                            dve.wait_ge(s["scored"], h * 2 * NT + (2 * i + j + 1))
                            axis = mybir.AxisListType.XY
                            step.did(dve.tensor_reduce(st[:, b, j:j + 1], scores_ps(j, n), axis, ALU.max))
                            step.wait()
                            dve.tensor_scalar(st[:, b, 2 + j:3 + j], st[:, b, j:j + 1], -SC, None, ALU.mult).then_inc(s["bias"], 1)

                    softmax_bias(0)
                    for i in range(NT):
                        b = i % 2
                        k0, n = keys_of(i)
                        if i + 1 < NT:
                            softmax_bias(i + 1)
                        dve.wait_ge(s["expd"], h * 2 * NT + 2 * (i + 1))
                        step.did(dve.reciprocal(st[:, b, 6:8], st[:, b, 4:6]))
                        step.wait()
                        step.did(dve.tensor_scalar(p0[:, 0:n * P], p0[:, 0:n * P], st[:, b, 6:7], None, ALU.mult))
                        step.did(dve.tensor_tensor(st[:, b, 7:8], st[:, b, 7:8], nlam[:], ALU.mult))
                        step.wait()
                        step.did(dve.scalar_tensor_tensor(p0[:, 0:n * P], p1[:, 0:n * P], st[:, b, 7:8], p0[:, 0:n * P],
                                                          ALU.mult, ALU.add))
                        step.wait()
                        dve.sem_inc(s["mixed"], 1)
                    dve.wait_ge(s["root"], h + 1 + 1)
                    step.did(dve.reciprocal(sq[:], sq[:]))
                    step.wait()
                    dve.scalar_tensor_tensor(K.hT[:, bass.ds(h, 1), :].rearrange("p a t -> p (a t)"), oT[:],
                                             gs[:, bass.ds(h, 1)], sq[:], ALU.mult, ALU.mult).then_inc(s["act_steps"], 1)
                    step.close()


def stage_gates(K):
    nc, d = K.nc, K.d
    with ExitStack() as ctx:
        def sb(name, shape):
            return ctx.enter_context(nc.sbuf_tensor(f"gate_{name}", shape, F32))
        s = K.sems("gate", "rows_in", "par_in", "steps", "abs", "exped", "log", "em", "rows_ready", "rows_out", "small", "small_out",
                   "wold", "turned", "cols", "m_out")
        g = sb("in", [4, 4, T])
        li, x = g[:, 0:2], g[:, 2:4]
        a, b, m = sb("a", [4, 2, T]), sb("b", [4, 2, T]), sb("m", [4, 2, T])
        resets = sb("resets", [4, 2, T])
        bias = sb("bias", [4, 3, 2])
        sm = sb("small", [4, 2, 2, NT])
        e = sb("end", [4, 3, 2, NT])

        def ends(t, r):
            return t[:, r].rearrange("h (c p) -> h c p", p=P)[:, :, (P - 1) if r == 0 else 0]

        def along(t, r, lo, hi):
            if r == 0:
                return t[:, 0, lo:hi]
            return t[:, 1, lo:hi][:, ::-1]

        with nc.Block() as block:
            @block.sync
            def _(sp):
                sp.dma_start(g[:], K.gate_rows.rearrange("k h t -> h k t")).then_inc(s["rows_in"], 16)
                sp.dma_start(resets[:], d["resets"]).then_inc(s["rows_in"], 16)
                with nc.allow_non_contiguous_dma("a few words"):
                    sp.dma_start(bias[:, 0], d["b_ig_ab"][0].rearrange("r h -> h r")).then_inc(s["par_in"], 16)
                    sp.dma_start(bias[:, 1], d["b_fg_ab"][0].rearrange("r h -> h r")).then_inc(s["par_in"], 16)
                    sp.dma_start(bias[:, 2], d["state_mlstm_m"][0, 0].rearrange("r h -> h r")).then_inc(s["par_in"], 16)
                    sp.wait_ge(s["rows_ready"], 1)
                    sp.dma_start(K.mrows[0].rearrange("r h t -> h r t"), x).then_inc(s["rows_out"], 16)
                    sp.wait_ge(s["em"], 1)
                    sp.dma_start(K.mrows[1].rearrange("r h t -> h r t"), a[:]).then_inc(s["rows_out"], 16)
                    sp.wait_ge(s["wold"], 1)
                    sp.dma_start(K.msmall.rearrange("k r h c -> h k r c"), sm[:]).then_inc(s["small_out"], 16)
                    sp.dma_start(d["o_new_m"][0, 0].rearrange("r h -> h r"), e[:, 1, :, NS]).then_inc(s["m_out"], 16)
                sp.wait_ge(s["rows_out"], 32)
                sp.wait_ge(s["small_out"], 16)
                sp.wait_ge(s["m_out"], 16)

            @block.scalar
            def _(act):
                act.wait_ge(s["abs"], 1)
                act.activation(a[:], a[:], ACT.Exp, scale=-1.0).then_inc(s["exped"], 1)
                act.wait_ge(s["exped"], 1)
                act.activation(a[:], a[:], ACT.Ln, bias=1.0).then_inc(s["log"], 1)
                act.wait_ge(s["rows_ready"], 1)
                act.activation(a[:], m[:], ACT.Exp, scale=-1.0).then_inc(s["em"], 1)
                act.wait_ge(s["small"], 1)
                act.activation(sm[:, 1], sm[:, 1], ACT.Exp).then_inc(s["wold"], 1)
                act.wait_ge(s["turned"], 1)
                act.activation(K.w_state[:], K.ps[:, PIECE:PIECE + 72].rearrange("p (r c h) -> p r c h", r=2, c=NT),
                               ACT.Exp).then_inc(s["cols"], 1)

            @block.tensor
            def _(pe):
                pe.wait_ge(s["small"], 1)
                for kind, src in ((0, b), (1, m)):
                    for r in range(2):
                        for c in range(NT):
                            at = kind * PIECE + (r * NT + c) * 4
                            mm = pe.transpose(K.ps[:, at:at + 4], src[:, r, c * P:(c + 1) * P], K.cst[0:4, 0:4])
                mm.then_inc(s["turned"], 1)

            @block.vector
            def _(dve):
                step = Steps(dve, s["steps"])
                dve.wait_ge(s["rows_in"], 32)
                dve.wait_ge(s["par_in"], 48)
                for r in range(2):
                    step.did(dve.tensor_scalar(li[:, r], li[:, r], bias[:, 0, r:r + 1], None, ALU.add))
                    step.did(dve.tensor_scalar(x[:, r], x[:, r], bias[:, 1, r:r + 1], None, ALU.add))
                step.wait()
                dve.scalar_tensor_tensor(a[:], x, -1.0, x, ALU.mult, ALU.max).then_inc(s["abs"], 1)
                dve.wait_ge(s["log"], 1)
                step.did(dve.scalar_tensor_tensor(x, x, 0.0, a[:], ALU.min, ALU.subtract))
                step.wait()
                for r in range(2):
                    step.did(dve.tensor_tensor_scan(along(b, r, 0, T), along(resets, r, 0, T), along(x, r, 0, T), 0.0,
                                                    ALU.mult, ALU.add))
                    step.did(dve.tensor_tensor_scan(along(m, r, 0, T_S), along(x, r, 0, T_S), along(li, r, 0, T_S),
                                                    bias[:, 2, r:r + 1], ALU.add, ALU.max))
                    step.did(dve.tensor_tensor_scan(along(m, r, T_S, T), along(x, r, T_S, T), along(li, r, T_S, T),
                                                    0.0, ALU.add, ALU.max))
                step.wait()
                step.did(dve.tensor_tensor(x, b[:], m[:], ALU.subtract))
                for r in range(2):
                    step.did(dve.tensor_copy(e[:, 0, r], ends(b, r)))
                    step.did(dve.tensor_copy(e[:, 1, r], ends(m, r)))
                step.did(dve.memset(sm[:, 0, :, NS:NT], 0.0))
                step.did(dve.tensor_copy(sm[:, 0, 0, 0:1], bias[:, 2, 0:1]))
                step.did(dve.tensor_copy(sm[:, 0, 1, NS - 1:NS], bias[:, 2, 1:2]))
                step.wait()
                step.did(dve.tensor_copy(sm[:, 0, 0, 1:NS], e[:, 1, 0, 0:NS - 1]))
                step.did(dve.tensor_copy(sm[:, 0, 1, 0:NS - 1], e[:, 1, 1, 1:NS]))
                step.did(dve.tensor_tensor(e[:, 2], e[:, 0], e[:, 1], ALU.subtract))
                step.wait()
                dve.sem_inc(s["rows_ready"], 1)
                step.did(dve.tensor_tensor(sm[:, 1], e[:, 2], sm[:, 0], ALU.add))
                step.did(dve.tensor_tensor(b[:], li, b[:], ALU.subtract))
                step.wait()
                dve.wait_ge(s["em"], 1)
                for r in range(2):
                    step.did(dve.tensor_tensor(m[:, r].rearrange("h (c p) -> h c p", p=P),
                                               b[:, r].rearrange("h (c p) -> h c p", p=P),
                                               e[:, 2, r].unsqueeze(2).to_broadcast([4, NT, P]), ALU.add))
                step.wait()
                dve.sem_inc(s["small"], 1)
                dve.wait_ge(s["turned"], 1)
                dve.tensor_copy(K.w_arg[:], K.ps[:, 0:72].rearrange("p (r c h) -> p r c h", r=2, c=NT)).then_inc(s["cols"], 1)


def stage_mlstm(K):
    nc, d = K.nc, K.d
    NSTATE = NS + 2
    with ExitStack() as ctx:
        def sb(name, shape):
            return ctx.enter_context(nc.sbuf_tensor(f"ml_{name}", shape, F32))
        s = K.sems("ml", "x_in", "v_in", "o_in", "row_in", "small_in", "st_in", "steps", "conv", "act_silu", "kscaled", "kT",
                   "k_used", "scT", "sc_out", "arg", "exped", "att", "kv", "upd", "num", "num_read", "C_out", "sq", "ssum",
                   "root", "sig", "done")
        qx, kx, ox = sb("qx", [P, T]), sb("kx", [P, T]), sb("ox", [P, T])
        v = sb("v", [P, NT, P + 1])
        qc, kc, sc = sb("qc", [P, T]), sb("kc", [P, T]), sb("sc", [P, T])
        ub, em = sb("ub", [P, T]), sb("em", [P, T])
        att, qw, hs, tmp = sb("att", [P, T]), sb("qw", [P, T]), sb("hs", [P, T]), sb("tmp", [P, T])
        small = sb("small", [P, 2, 2, NT])
        C = sb("C", [P, NSTATE, P + 1])
        kw = [qx, kx]
        chunk = lambda t: t.rearrange("p (c n) -> p c n", n=P)
        KV = [6 * PIECE, 7 * PIECE]
        N_DVE = 2 * 5 + 1 + 2 + (3 + 2 + 5) + (3 + 2 + 6) + 3

        def order(r):
            lat = range(NS) if r == 0 else range(NS - 1, -1, -1)
            return [(c, i, i + 1) for i, c in enumerate(lat)] + [(NS, None, NS + 1)]

        with nc.Block() as block:
            @block.gpsimd
            def _(pool):
                with pool.Fori(0, HEADS_B) as h:
                    pool.wait_ge(s["done"], h + 1)
                    pool.dma_start(qx[:], K.featT[bass.ds(h, 1)].rearrange("a p t -> (a p) t")).then_inc(s["x_in"], 16)
                    pool.dma_start(kx[:], K.featT[bass.ds(h + 4, 1)].rearrange("a p t -> (a p) t")).then_inc(s["x_in"], 16)
                    pool.dma_start(ox[:], K.featT[bass.ds(h + 8, 1)].rearrange("a p t -> (a p) t")).then_inc(s["o_in"], 16)
                    pool.dma_start(v[:, :, 0:P], K.tok.rearrange("n t p f -> n p t f")[3, :, :, bass.ds(h * P, P)]).then_inc(s["v_in"], 16)

            @block.sync
            def _(sp):
                sp.sem_inc(s["C_out"], 32)
                def row(kind, r, h):
                    return K.mrows[kind, r, bass.ds(h, 1), :].to_broadcast([P, T])
                with sp.Fori(0, HEADS_B) as h, nc.allow_non_contiguous_dma("a state's normaliser column"):
                    for r in range(2):
                        sp.wait_ge(s["num_read"], h * 2 + r + 1)
                        if r == 0:
                            sp.dma_start(small[:], K.msmall[:, :, bass.ds(h, 1), :].rearrange("k r a c -> a k r c")
                                         .to_broadcast([P, 2, 2, NT])).then_inc(s["small_in"], 16)
                        sp.dma_start(ub[:], row(0, r, h)).then_inc(s["row_in"], 16)
                        sp.dma_start(em[:], row(1, r, h)).then_inc(s["row_in"], 16)
                        sp.wait_ge(s["C_out"], (h * 2 + r) * 32 + 32)
                        sp.dma_start(C[:, 0, 0:P], d["state_mlstm_C"][0, 0, r, bass.ds(h, 1)].rearrange("a k v -> (a k) v")).then_inc(s["st_in"], 16)
                        sp.dma_start(C[:, 0, P:P + 1], d["state_mlstm_n"][0, 0, r, bass.ds(h, 1)].rearrange("a k -> k a")).then_inc(s["st_in"], 16)
                        sp.wait_ge(s["upd"], (h * 2 + r + 1) * NT + 1)
                        sp.dma_start(d["o_new_C"][0, 0, r, bass.ds(h, 1)].rearrange("a k v -> (a k) v"), C[:, NS + 1, 0:P]).then_inc(s["C_out"], 16)
                        sp.dma_start(d["o_new_n"][0, 0, r, bass.ds(h, 1)].rearrange("a k -> k a"), C[:, NS + 1, P:P + 1]).then_inc(s["C_out"], 16)
                sp.wait_ge(s["C_out"], 32 * 2 * HEADS_B + 32)

            @block.scalar
            def _(act):
                act.sem_inc(s["root"], 1)
                with act.Fori(0, HEADS_B) as h:
                    for j, t in enumerate((qc, kc)):
                        act.wait_ge(s["conv"], h * 2 + j + 1)
                        act.activation(t[:], t[:], ACT.Silu).then_inc(s["act_silu"], 1)
                    act.wait_ge(s["o_in"], h * 16 + 16)
                    act.activation(ox[:], ox[:], ACT.Sigmoid).then_inc(s["sig"], 1)
                    act.wait_ge(s["scT"], h + 1)
                    act.copy(sc[:], K.ps[:, 3 * PIECE:3 * PIECE + T]).then_inc(s["sc_out"], 1)
                    for r in range(2):
                        for j, t in enumerate((att, qw)):
                            act.wait_ge(s["arg"], h * 4 + (2 * r + j + 1))
                            act.activation(t[:], t[:], ACT.Exp).then_inc(s["exped"], 1)
                    act.wait_ge(s["num_read"], h * 2 + 2 + 1)
                    act.activation(att[:], hs[:], ACT.Square).then_inc(s["sq"], 1)
                    act.wait_ge(s["ssum"], h + 1)
                    act.activation(chunk(tmp[:]), chunk(K.ps[:, 0:T]), ACT.Sqrt, bias=K.eps[:], scale=1.0 / P).then_inc(s["root"], 1)

            @block.tensor
            def _(pe):
                pe.sem_inc(s["num"], 1)
                with pe.Fori(0, HEADS_B) as h:
                    pe.wait_ge(s["kscaled"], h + 1)
                    pe.wait_ge(s["root"], h + 1)
                    for c in range(NT):
                        mm = pe.transpose(K.ps[:, c * P:(c + 1) * P], kc[:, c * P:(c + 1) * P], K.c("ident"))
                    mm.then_inc(s["kT"], 1)
                    for c in range(NT):
                        mm = pe.matmul(K.ps[:, 3 * PIECE + c * P:3 * PIECE + (c + 1) * P], kc[:, c * P:(c + 1) * P],
                                       qc[:, c * P:(c + 1) * P], start=True, stop=True)
                    mm.then_inc(s["scT"], 1)
                    pe.wait_ge(s["v_in"], h * 16 + 16)
                    pe.wait_ge(s["k_used"], h + 1)
                    pe.wait_ge(s["sc_out"], h + 1)
                    for r in range(2):
                        base = (h * 2 + r) * NT
                        for n, (c, before, after) in enumerate(order(r)):
                            if n >= 2:
                                pe.wait_ge(s["upd"], base + n - 1 + 1)
                            elif r == 1:
                                pe.wait_ge(s["upd"], base + 1)
                            else:
                                pe.wait_ge(s["upd"], base + 1)
                            pe.matmul(K.ps[:, KV[n % 2]:KV[n % 2] + P + 1], kw[r][:, c * P:(c + 1) * P], v[:, c, :],
                                      start=True, stop=True).then_inc(s["kv"], 1)
                        pe.wait_ge(s["att"], h * 2 + r + 1)
                        pe.wait_ge(s["upd"], base + NT + 1)
                        if r == 1:
                            pe.wait_ge(s["num_read"], h * 2 + 1 + 1)
                        for c, before, after in sorted(order(r)):
                            num, den = K.ps[:, c * P:(c + 1) * P], K.ps[:, 3 * PIECE + c * P:3 * PIECE + (c + 1) * P]
                            cc = slice(c * P, (c + 1) * P)
                            first = before is None
                            if not first:
                                pe.matmul(num, C[:, before, 0:P], qw[:, cc], start=True, stop=False)
                            pe.matmul(num, v[:, c, 0:P], att[:, cc], start=first, stop=True)
                            if not first:
                                pe.matmul(den, C[:, before, P:P + 1].to_broadcast([P, P]), qw[:, cc], start=True, stop=False)
                            mm = pe.matmul(den, K.c("ones"), att[:, cc], start=first, stop=True)
                        mm.then_inc(s["num"], 1)
                    pe.wait_ge(s["sq"], h + 1)
                    for c in range(3):
                        w = min(PIECE, T - c * PIECE)
                        mm = pe.matmul(K.ps[:, c * PIECE:c * PIECE + w], K.c("ones"), att[:, c * PIECE:c * PIECE + w], start=True, stop=True)
                    mm.then_inc(s["ssum"], 1)

            @block.vector
            def _(dve):
                dve.sem_inc(s["upd"], 1)
                dve.sem_inc(s["num_read"], 1)
                dve.sem_inc(s["done"], 1)
                dve.memset(v[:, :, P:P + 1], 1.0).then_inc(s["steps"], 1)
                conv_at = PARAMS["conv"][0]
                with dve.Fori(0, HEADS_B) as h:
                    step = Steps(dve, s["steps"], h, N_DVE)
                    step.base = step.base + 1
                    dve.wait_ge(s["x_in"], h * 32 + 32)
                    for j, (x, y) in enumerate(((qx, qc), (kx, kc))):
                        def w(i):
                            return K.par[:, bass.ds(h + (conv_at + i * 8 + j * 4), 1)]
                        step.did(dve.tensor_scalar(y[:], x[:], w(1), None, ALU.mult))
                        step.wait()
                        for lo, hi in ((0, T_S), (T_S, T)):
                            step.did(dve.scalar_tensor_tensor(y[:, lo + 1:hi], x[:, lo:hi - 1], w(0), y[:, lo + 1:hi], ALU.mult, ALU.add))
                        step.wait()
                        for lo, hi in ((0, T_S), (T_S, T)):
                            step.did(dve.scalar_tensor_tensor(y[:, lo:hi - 1], x[:, lo + 1:hi], w(2), y[:, lo:hi - 1], ALU.mult, ALU.add))
                        step.wait()
                        dve.sem_inc(s["conv"], 1)
                    dve.wait_ge(s["act_silu"], h * 2 + 2)
                    step.did(dve.tensor_scalar(kc[:], kc[:], float(P) ** -0.5, None, ALU.mult))
                    step.wait()
                    dve.sem_inc(s["kscaled"], 1)
                    dve.wait_ge(s["kT"], h + 1)
                    for r in range(2):
                        step.did(dve.tensor_tensor(chunk(kw[r][:]), chunk(K.ps[:, 0:T]),
                                                   K.w_state[:, r, :, bass.ds(h, 1)].to_broadcast([P, NT, P]), ALU.mult))
                    step.wait()
                    dve.sem_inc(s["k_used"], 1)
                    for r in range(2):
                        n_dir = h * 2 + r
                        neg = K.c("neg_fwd" if r == 0 else "neg_bwd").unsqueeze(1).to_broadcast([P, NT, P])
                        dve.wait_ge(s["row_in"], (n_dir + 1) * 32)
                        dve.wait_ge(s["small_in"], h * 16 + 16)
                        dve.wait_ge(s["num"], n_dir + 1)
                        step.did(dve.tensor_tensor(chunk(att[:]), chunk(ub[:]),
                                                   K.w_arg[:, r, :, bass.ds(h, 1)].to_broadcast([P, NT, P]), ALU.add))
                        step.wait()
                        step.did(dve.tensor_tensor(chunk(att[:]), chunk(att[:]), neg, ALU.min))
                        step.did(dve.tensor_tensor(chunk(qw[:]), chunk(ub[:]), small[:, 0, r].unsqueeze(2).to_broadcast([P, NT, P]), ALU.add))
                        step.wait()
                        dve.sem_inc(s["arg"], 2)
                        dve.wait_ge(s["st_in"], (n_dir + 1) * 32)
                        for n, (c, before, after) in enumerate(order(r)):
                            dve.wait_ge(s["kv"], n_dir * NT + n + 1)
                            kv = K.ps[:, KV[n % 2]:KV[n % 2] + P + 1]
                            if before is None:
                                ins = dve.tensor_copy(C[:, after], kv)
                            else:
                                ins = dve.scalar_tensor_tensor(C[:, after], C[:, before], small[:, 1, r, c:c + 1], kv, ALU.mult, ALU.add)
                            ins.then_inc(s["upd"], 1)
                            dve.wait_ge(s["upd"], n_dir * NT + n + 1 + 1)
                            pass
                        dve.wait_ge(s["exped"], n_dir * 2 + 2)
                        dve.wait_ge(s["sc_out"], h + 1)
                        step.did(dve.tensor_tensor(att[:], att[:], sc[:], ALU.mult))
                        step.did(dve.tensor_tensor(qw[:], qw[:], qc[:], ALU.mult))
                        step.wait()
                        dve.sem_inc(s["att"], 1)
                        dve.wait_ge(s["num"], n_dir + 1 + 1)
                        den = K.ps[:, 3 * PIECE:3 * PIECE + T]
                        step.did(dve.tensor_copy(tmp[:], den))
                        step.wait()
                        step.did(dve.scalar_tensor_tensor(tmp[:], tmp[:], -1.0, tmp[:], ALU.mult, ALU.max))
                        step.wait()
                        step.did(dve.tensor_tensor(tmp[:], tmp[:], em[:], ALU.max))
                        step.wait()
                        step.did(dve.reciprocal(tmp[:], tmp[:]))
                        step.wait()
                        if r == 0:
                            step.did(dve.tensor_tensor(hs[:], K.ps[:, 0:T], tmp[:], ALU.mult))
                            step.wait()
                        else:
                            step.did(dve.tensor_tensor(tmp[:], K.ps[:, 0:T], tmp[:], ALU.mult))
                            step.wait()
                            step.did(dve.tensor_tensor(hs[:], hs[:], tmp[:], ALU.add))
                            step.wait()
                        dve.sem_inc(s["num_read"], 1)
                    dve.wait_ge(s["root"], h + 1 + 1)
                    step.did(dve.reciprocal(tmp[:], tmp[:]))
                    step.wait()
                    step.did(dve.scalar_tensor_tensor(hs[:], hs[:], K.par[:, bass.ds(h + PARAMS["g_mlstm"][0], 1)], tmp[:], ALU.mult, ALU.mult))
                    step.wait()
                    dve.wait_ge(s["sig"], h + 1)
                    step.did(dve.tensor_tensor(K.hT[:, bass.ds(h + 4, 1), :].rearrange("p a t -> p (a t)"), hs[:], ox[:], ALU.mult))
                    step.wait()
                    dve.sem_inc(s["done"], 1)
                    step.close()


def stage_out(K, l):
    nc = K.nc
    at = AT_OUT[l]
    with ExitStack() as ctx:
        def sb(name, shape):
            return ctx.enter_context(nc.sbuf_tensor(f"out{l}_{name}", shape, F32))
        s = K.sems(f"out{l}", "x_in0", "x_in1", "gate_in", "product", "gated", "x_new", "x_stored0", "x_stored1", "sumsq",
                   "root", "rcp", "xn_ready", "turned", "act_evac", "dve_evac", "xn_stored0", "xn_stored1")
        x_in, x_stored, xn_stored = [s["x_in0"], s["x_in1"]], [s["x_stored0"], s["x_stored1"]], [s["xn_stored0"], s["xn_stored1"]]
        xt, xn = sb("x", [P, 2, D]), sb("xn", [P, 2, D])
        tmp, junk = sb("tmp", [P, 2, D]), sb("junk", [P, D])
        gate = sb("gate", [P, STREAMS, D])
        st = sb("stat", [P, 2, 4])
        TURN = 4 * PIECE
        shift_at = l * 48 + 3 * KT
        with nc.Block() as block:
            @block.gpsimd
            def _(pool):
                for r in range(STREAMS):
                    pool.dma_start(gate[:, r], K.gate1_rows[l, r:r + 1].to_broadcast([P, D])).then_inc(s["gate_in"], 16)

                def body(tiles, r):
                    for t, b, u in tiles:
                        pool.wait_ge(s["xn_ready"], t + 1)
                        pool.wait_ge(x_stored[b], u * 16 + 16)
                        pool.dma_start(xt[:, b], K.xres[bass.ds(t * P, P), :]).then_inc(x_in[b], 16)
                over_tiles(pool, body)

            @block.sync
            def _(sp):
                def body(tiles, r):
                    for t, b, u in tiles:
                        sp.wait_ge(s["x_new"], t + 1)
                        sp.dma_start(K.xres[bass.ds(t * P, P), :], xt[:, b]).then_inc(x_stored[b], 16)
                    for t, b, u in tiles:
                        sp.wait_ge(s["xn_ready"], t + 3)
                        sp.dma_start(K.xnorm[bass.ds(t * P, P), :], xn[:, b]).then_inc(xn_stored[b], 16)
                for sem in x_stored + xn_stored:
                    sp.sem_inc(sem, 16)
                over_tiles(sp, body)
                for i in range(2):
                    load_piece(K, sp, at + SLOTS + i)
                for sems in (x_stored, xn_stored):
                    sp.wait_ge(sems[0], 16 + 16 * 5)
                    sp.wait_ge(sems[1], 16 + 16 * 4)

            @block.scalar
            def _(act):
                def body(tiles, r):
                    for t, b, u in tiles:
                        act.wait_ge(s["x_new"], t + 1)
                        act.activation(junk[:], xt[:, b], ACT.Square, accum_out=st[:, b, 0:1]).then_inc(s["sumsq"], 1)
                        act.wait_ge(s["sumsq"], t + 1)
                        act.activation(st[:, b, 1:2], st[:, b, 0:1], ACT.Sqrt, bias=K.eps[:], scale=1.0 / D).then_inc(s["root"], 1)
                    for t, b, u in tiles:
                        act.wait_ge(s["turned"], t + 3)
                        for k in range(KT // 2):
                            a = TURN + b * D + k * P
                            ins = act.activation(K.hT[:, k, bass.ds(t * P, P)], K.ps[:, a:a + P], ACT.Identity,
                                                 bias=K.ada[:, r, shift_at + k:shift_at + k + 1], scale=K.scale[:, l, 1, r, k:k + 1])
                        ins.then_inc(s["act_evac"], 1)
                act.sem_inc(s["act_evac"], 2)
                over_tiles(act, body)

            @block.tensor
            def _(pe):
                pe.sem_inc(s["turned"], 2)

                def product(t):
                    b = t % 2
                    pe.wait_ge(s["gated"], t + 1)
                    for c in range(2):
                        if t == 0:
                            wait_piece(K, pe, at + c)
                        for k in range(KT):
                            mm = pe.matmul(K.ps[:, b * D + c * PIECE:b * D + (c + 1) * PIECE], K.hT[:, k, t * P:(t + 1) * P],
                                           K.W[:, (at + c) % SLOTS, k], start=(k == 0), stop=(k == KT - 1))
                    mm.then_inc(s["product"], 1)

                def turn(t):
                    b = t % 2
                    pe.wait_ge(s["xn_ready"], t + 3)
                    pe.wait_ge(s["act_evac"], t + 1)
                    pe.wait_ge(s["dve_evac"], t + 1)
                    for k in range(KT):
                        a = TURN + b * D + k * P
                        mm = pe.transpose(K.ps[:, a:a + P], xn[:, b, k * P:(k + 1) * P], K.c("ident"))
                    mm.then_inc(s["turned"], 1)
                product(0)
                product(1)
                for t in range(NT):
                    if t + 2 < NT:
                        product(t + 2)
                    if t + 2 == NT:
                        pe.drain().then_inc(K.w_used, 2)
                    turn(t)

            @block.vector
            def _(dve):
                def body(tiles, r):
                    for t, b, u in tiles:
                        dve.wait_ge(s["product"], t + 1)
                        dve.tensor_tensor(tmp[:, b], K.ps[:, b * D:(b + 1) * D], gate[:, r], ALU.mult).then_inc(s["gated"], 1)
                        dve.wait_ge(s["gated"], t + 3)
                        dve.wait_ge(x_in[b], u * 16 + 16)
                        dve.tensor_tensor(xt[:, b], xt[:, b], tmp[:, b], ALU.add).then_inc(s["x_new"], 1)
                    for t, b, u in tiles:
                        dve.wait_ge(s["root"], t + 1)
                        dve.reciprocal(st[:, b, 2:3], st[:, b, 1:2]).then_inc(s["rcp"], 1)
                        dve.wait_ge(s["rcp"], t + 1)
                        dve.wait_ge(s["turned"], t + 1)
                        dve.wait_ge(xn_stored[b], u * 16 + 16)
                        dve.tensor_scalar(xn[:, b], xt[:, b], st[:, b, 2:3], None, ALU.mult).then_inc(s["xn_ready"], 1)
                    for t, b, u in tiles:
                        dve.wait_ge(s["turned"], t + 3)
                        for k in range(KT // 2, KT):
                            a = TURN + b * D + k * P
                            ins = dve.tensor_scalar(K.hT[:, k, bass.ds(t * P, P)], K.ps[:, a:a + P], K.scale[:, l, 1, r, k:k + 1],
                                                    K.ada[:, r, shift_at + k:shift_at + k + 1], ALU.mult, ALU.add)
                        ins.then_inc(s["dve_evac"], 1)
                dve.sem_inc(s["xn_ready"], 2)
                dve.sem_inc(s["dve_evac"], 2)
                dve.sem_inc(s["gated"], 2)
                dve.wait_ge(s["gate_in"], 32)
                over_tiles(dve, body)


def stage_route(K, l):
    nc = K.nc
    E = EXPERTS
    with ExitStack() as ctx:
        def sb(name, shape, dt=F32):
            return ctx.enter_context(nc.sbuf_tensor(f"route{l}_{name}", shape, dt))
        s = K.sems(f"route{l}", "logits", "steps", "less_max", "exped", "aff", "affT", "picked", "columns")
        e, st = sb("e", [P, NT, E]), sb("stat", [P, 3, NT])
        aff = sb("aff", [E, T])
        val, idx = sb("val", [E, CAP]), sb("idx", [E, CAP], U32)
        idxf = sb("idxf", [E, CAP])
        with nc.Block() as block:
            @block.tensor
            def _(pe):
                for t in range(NT):
                    for k in range(KT):
                        mm = pe.matmul(K.ps[:, t * E:(t + 1) * E], K.hT[:, k, t * P:(t + 1) * P], K.w_router[:, l, k],
                                       start=(k == 0), stop=(k == KT - 1))
                mm.then_inc(s["logits"], 1)
                pe.wait_ge(s["aff"], 1)
                for t in range(NT):
                    mm = pe.transpose(K.ps[0:E, PIECE + t * P:PIECE + (t + 1) * P], e[:, t], K.c("ident"))
                mm.then_inc(s["affT"], 1)
                pe.wait_ge(s["picked"], 1)
                idn = K.cst[0:E, 0:E]
                for n, src in enumerate((idxf, val)):
                    pe.transpose(K.ps[:, n * E:(n + 1) * E], src[:, 0:CAP_S], idn)
                    mm = pe.transpose(K.ps[0:CAP_P, 64 + n * E:64 + (n + 1) * E], src[:, CAP_S:CAP], idn)
                mm.then_inc(s["columns"], 1)

            @block.scalar
            def _(act):
                act.wait_ge(s["less_max"], 1)
                act.activation(e[:], e[:], ACT.Exp).then_inc(s["exped"], 1)

            @block.vector
            def _(dve):
                step = Steps(dve, s["steps"])
                logits = K.ps[:, 0:NT * E].rearrange("p (t e) -> p t e", e=E)

                def wide(i):
                    return st[:, i].unsqueeze(2).to_broadcast([P, NT, E])
                dve.wait_ge(s["logits"], 1)
                step.did(dve.tensor_reduce(st[:, 0], logits, AX_X, ALU.max))
                step.wait()
                dve.tensor_tensor(e[:], logits, wide(0), ALU.subtract).then_inc(s["less_max"], 1)
                dve.wait_ge(s["exped"], 1)
                step.did(dve.tensor_reduce(st[:, 1], e[:], AX_X, ALU.add))
                step.wait()
                step.did(dve.reciprocal(st[:, 2], st[:, 1]))
                step.wait()
                dve.tensor_tensor(e[:], e[:], wide(2), ALU.mult).then_inc(s["aff"], 1)
                dve.wait_ge(s["affT"], 1)
                step.did(dve.tensor_copy(aff[:], K.ps[0:E, PIECE:PIECE + T]))
                step.wait()
                for at, cap, lo, hi in ((0, CAP_S, 0, T_S), (CAP_S, CAP_P, T_S, T)):
                    for n in range(at, at + cap, 8):
                        step.did(dve.max(val[:, n:n + 8], aff[:, lo:hi]))
                        step.wait()
                        step.did(dve.max_index(idx[:, n:n + 8], val[:, n:n + 8], aff[:, lo:hi]))
                        step.wait()
                        if n + 8 < at + cap:
                            step.did(dve.match_replace(aff[:, lo:hi], val[:, n:n + 8], aff[:, lo:hi], -1.0))
                            step.wait()
                step.did(dve.tensor_copy(idxf[:, 0:CAP_S], idx[:, 0:CAP_S]))
                step.did(dve.tensor_scalar(idxf[:, CAP_S:CAP], idx[:, CAP_S:CAP], float(T_S), None, ALU.add))
                step.wait()
                dve.sem_inc(s["picked"], 1)
                dve.wait_ge(s["columns"], 1)
                step.did(dve.tensor_copy(K.idx_s[:], K.ps[:, 0:E]))
                step.did(dve.tensor_copy(K.gate_s[:], K.ps[:, E:2 * E]))
                step.did(dve.tensor_copy(K.idx_p[:], K.ps[0:CAP_P, 64:64 + E]))
                step.did(dve.tensor_copy(K.gate_p[:], K.ps[0:CAP_P, 64 + E:64 + 2 * E]))
                step.wait()


def stage_experts(K, l):
    nc = K.nc
    at = AT_EXPERTS[l]
    E = EXPERTS
    GU = [0, PIECE]
    DN = [2 * PIECE, 3 * PIECE]
    TR = 4 * PIECE
    with ExitStack() as ctx:
        def sb(name, shape, dt=F32):
            return ctx.enter_context(nc.sbuf_tensor(f"moe{l}_{name}", shape, dt))
        s = K.sems(f"moe{l}", "idx_g", "idx_s", "xs_in", "xp_in", "x_turned", "xT", "xT2", "gate", "up", "silu", "hid",
                   "down", "y_act", "y_dve", "y_turned", "ys_out", "yp_out", "ys_added", "yp_added", "added", "order")
        xs, xp = sb("xs", [CAP_S, D]), sb("xp", [CAP_P, D])
        xT, hid, yT = sb("xT", [P, KT, CAP]), sb("hid", [P, KT, CAP]), sb("yT", [P, KT, CAP])
        sg = sb("silu", [P, 2, CAP])
        ys, yp = sb("ys", [CAP_S, D]), sb("yp", [CAP_P, D])
        ig, ipg = sb("ig", [P, 1], I32), sb("ipg", [CAP_P, 1], I32)
        isc, ips = sb("is", [P, 1], I32), sb("ips", [CAP_P, 1], I32)
        shift_at, gate2_at = l * 48 + 3 * KT, l * 48 + 5 * KT

        def turned_x(k):
            return TR + (k // 3) * PIECE + (k % 3) * CAP

        def turn_x(pe, e):
            pe.wait_ge(s["xs_in"], e * 16 + 16)
            pe.wait_ge(s["xp_in"], e * 16 + 16)
            for k in range(KT):
                a = turned_x(k)
                pe.transpose(K.ps[:, a:a + CAP_S], xs[:, k * P:(k + 1) * P], K.c("ident"))
                mm = pe.transpose(K.ps[:, a + CAP_S:a + CAP], xp[:, k * P:(k + 1) * P], K.cst[0:CAP_P, 0:CAP_P])
            mm.then_inc(s["x_turned"], 1)

        def turn_y(pe, e):
            pe.wait_ge(s["y_act"], e * KT + KT)
            for k in range(KT):
                pe.transpose(K.ps[:, TR + k * P:TR + (k + 1) * P], yT[:, k, 0:CAP_S], K.c("ident"))
            for k in range(KT):
                mm = pe.transpose(K.ps[0:CAP_P, TR + D + k * P:TR + D + (k + 1) * P], yT[:, k, CAP_S:CAP], K.c("ident"))
            mm.then_inc(s["y_turned"], 1)

        def experts(eng, body):
            body(0, False, True)
            with eng.Fori(1, E - 1) as e:
                body(e, True, True)
            body(E - 1, True, False)

        with nc.Block() as block:
            @block.sync
            def _(sp):
                def used(i, e):
                    if i < 4:
                        sp.wait_ge(s["up"], e * KT + 4 * (i // 2 + 1))
                    else:
                        sp.wait_ge(s["down"], e * KT + 4 * (i - 3))
                with sp.Fori(0, E - 1) as e:
                    for i in range(SLOTS):
                        used(i, e)
                        w = (K.d["w_gate_e"], K.d["w_up_e"], K.d["w_gate_e"], K.d["w_up_e"], K.d["w_down_e"], K.d["w_down_e"])[i]
                        c = (0, 0, 1, 1, 0, 1)[i]
                        src = w[l, bass.ds(e + 1, 1)].rearrange("a (k p) f -> p (a k) f", p=P)[:, :, c * PIECE:(c + 1) * PIECE]
                        sp.dma_start(K.W[:, (at + i) % SLOTS], src).then_inc(K.w_loaded[(at + i) % SLOTS], 16)
                for i in range(SLOTS):
                    n = at + E * SLOTS + i
                    if n < len(K.pieces):
                        used(i, E - 1)
                        sp.dma_start(K.W[:, n % SLOTS], K.pieces[n]).then_inc(K.w_loaded[n % SLOTS], 16)

            @block.gpsimd
            def _(pool):
                pool.sem_inc(s["added"], 1)

                def gather(e):
                    pool.tensor_copy(ig[:], K.idx_s[:, bass.ds(e, 1)]).then_inc(s["idx_g"], 1)
                    pool.tensor_copy(ipg[:], K.idx_p[:, bass.ds(e, 1)]).then_inc(s["idx_g"], 1)
                    pool.wait_ge(s["idx_g"], e * 2 + 2)
                    pool.sem_inc(s["order"], 1)
                    pool.indirect_dma_start(xs[:], None, K.xnorm, bass.IndirectOffsetOnAxis(ig[:, 0:1], 0)).then_inc(s["xs_in"], 16)
                    pool.indirect_dma_start(xp[:], None, K.xnorm, bass.IndirectOffsetOnAxis(ipg[:, 0:1], 0)).then_inc(s["xp_in"], 16)

                def add(e):
                    pool.tensor_copy(isc[:], K.idx_s[:, bass.ds(e, 1)]).then_inc(s["idx_s"], 1)
                    pool.tensor_copy(ips[:], K.idx_p[:, bass.ds(e, 1)]).then_inc(s["idx_s"], 1)
                    pool.wait_ge(s["idx_s"], e * 2 + 2)
                    pool.wait_ge(s["ys_out"], e + 1 + 1)
                    pool.sem_inc(s["order"], 1)
                    pool.indirect_dma_start(K.xres, bass.IndirectOffsetOnAxis(isc[:, 0:1], 0), ys[:], None,
                                            compute_op=ALU.add).then_inc(s["ys_added"], 16)
                    pool.wait_ge(s["yp_out"], e + 1 + 1)
                    pool.sem_inc(s["order"], 1)
                    pool.indirect_dma_start(K.xres, bass.IndirectOffsetOnAxis(ips[:, 0:1], 0), yp[:], None,
                                            compute_op=ALU.add).then_inc(s["yp_added"], 16)
                    pool.wait_ge(s["ys_added"], e * 16 + 16)
                    pool.wait_ge(s["yp_added"], e * 16 + 16)
                    pool.sem_inc(s["added"], 1)

                def body(e, before, after):
                    if after:
                        pool.wait_ge(s["x_turned"], e + 1)
                        gather(e + 1)
                    if before:
                        add(e - 1)
                gather(0)
                experts(pool, body)
                add(E - 1)

            @block.tensor
            def _(pe):
                def column_tile(e, ft):
                    half, col = ft // 4, (ft % 4) * P
                    pe.wait_ge(s["hid"], e * KT + max(ft - 1, 0) + 1)
                    for j in range(2):
                        n = at + 2 * half + j
                        slot = n % SLOTS
                        if ft % 4 == 0:
                            pe.wait_ge(K.w_loaded[slot], e * 16 + 16 * (n // SLOTS + 1))
                        a = GU[ft % 2] + j * CAP
                        for k in range(KT):
                            mm = pe.matmul(K.ps[:, a:a + CAP], K.W[:, slot, k, col:col + P], xT[:, k, :],
                                           start=(k == 0), stop=(k == KT - 1))
                    mm.then_inc(s["up"], 1)

                def body(e, before, after):
                    pe.wait_ge(s["xT"], e + 1)
                    pe.wait_ge(s["xT2"], e + 1)
                    column_tile(e, 0)
                    if before:
                        turn_y(pe, e - 1)
                    for ft in range(1, KT):
                        column_tile(e, ft)
                    if after:
                        pe.wait_ge(s["ys_out"], e + 1)
                        pe.wait_ge(s["yp_out"], e + 1)
                        turn_x(pe, e + 1)
                    pe.wait_ge(s["hid"], e * KT + KT + 1)
                    for dt in range(KT):
                        n = at + 4 + dt // 4
                        slot, col = n % SLOTS, (dt % 4) * P
                        if dt % 4 == 0:
                            pe.wait_ge(K.w_loaded[slot], e * 16 + 16 * (n // SLOTS + 1))
                        if dt >= 2:
                            pe.wait_ge(s["y_act"], e * KT + dt - 1)
                        for k in range(KT):
                            mm = pe.matmul(K.ps[:, DN[dt % 2]:DN[dt % 2] + CAP], K.W[:, slot, k, col:col + P], hid[:, k, :],
                                           start=(k == 0), stop=(k == KT - 1))
                        mm.then_inc(s["down"], 1)
                turn_x(pe, 0)
                experts(pe, body)
                turn_y(pe, E - 1)
                pe.drain().then_inc(K.w_used, E * SLOTS)

            @block.scalar
            def _(act):
                act.sem_inc(s["ys_out"], 1)

                def modulate(e):
                    act.wait_ge(s["x_turned"], e + 1)
                    for k in range(3, 6):
                        for r, (lo, hi) in enumerate(((0, CAP_S), (CAP_S, CAP))):
                            a = turned_x(k)
                            ins = act.activation(xT[:, k, lo:hi], K.ps[:, a + lo:a + hi], ACT.Identity,
                                                 bias=K.ada[:, r, shift_at + k:shift_at + k + 1], scale=K.scale[:, l, 1, r, k:k + 1])
                    ins.then_inc(s["xT"], 1)

                def weighted(e):
                    act.wait_ge(s["y_turned"], e + 1)
                    act.wait_ge(s["added"], e + 1)
                    act.activation(ys[:], K.ps[:, TR:TR + D], ACT.Copy, scale=K.gate_s[:, bass.ds(e, 1)]).then_inc(s["ys_out"], 1)

                def body(e, before, after):
                    for ft in range(KT):
                        act.wait_ge(s["up"], e * KT + (ft + 1))
                        if ft >= 2:
                            act.wait_ge(s["hid"], e * KT + (ft - 1) + 1)
                        act.activation(sg[:, ft % 2], K.ps[:, GU[ft % 2]:GU[ft % 2] + CAP], ACT.Silu).then_inc(s["silu"], 1)
                        if ft == 1 and before:
                            weighted(e - 1)
                    if after:
                        modulate(e + 1)
                    for dt in range(KT):
                        act.wait_ge(s["down"], e * KT + (dt + 1))
                        for r, (lo, hi) in enumerate(((0, CAP_S), (CAP_S, CAP))):
                            ins = act.activation(yT[:, dt, lo:hi], K.ps[:, DN[dt % 2] + lo:DN[dt % 2] + hi], ACT.Copy,
                                                 scale=K.ada[:, r, gate2_at + dt:gate2_at + dt + 1])
                        ins.then_inc(s["y_act"], 1)
                modulate(0)
                experts(act, body)
                weighted(E - 1)

            @block.vector
            def _(dve):
                dve.sem_inc(s["hid"], 1)
                dve.sem_inc(s["yp_out"], 1)

                def modulate(e):
                    dve.wait_ge(s["x_turned"], e + 1)
                    for k in (0, 1, 2, 6, 7):
                        for r, (lo, hi) in enumerate(((0, CAP_S), (CAP_S, CAP))):
                            a = turned_x(k)
                            ins = dve.tensor_scalar(xT[:, k, lo:hi], K.ps[:, a + lo:a + hi], K.scale[:, l, 1, r, k:k + 1],
                                                    K.ada[:, r, shift_at + k:shift_at + k + 1], ALU.mult, ALU.add)
                    ins.then_inc(s["xT2"], 1)

                def weighted(e):
                    dve.wait_ge(s["y_turned"], e + 1)
                    dve.wait_ge(s["added"], e + 1)
                    dve.tensor_scalar(yp[:], K.ps[0:CAP_P, TR + D:TR + 2 * D], K.gate_p[:, bass.ds(e, 1)], None,
                                      ALU.mult).then_inc(s["yp_out"], 1)

                def body(e, before, after):
                    for ft in range(KT):
                        dve.wait_ge(s["silu"], e * KT + (ft + 1))
                        a = GU[ft % 2] + CAP
                        dve.tensor_tensor(hid[:, ft], sg[:, ft % 2], K.ps[:, a:a + CAP], ALU.mult).then_inc(s["hid"], 1)
                        if ft == 1 and before:
                            weighted(e - 1)
                    if after:
                        modulate(e + 1)
                modulate(0)
                experts(dve, body)
                weighted(E - 1)


def stage_final(K):
    nc, d = K.nc, K.d
    with ExitStack() as ctx:
        def sb(name, shape):
            return ctx.enter_context(nc.sbuf_tensor(f"fin_{name}", shape, F32))
        s = K.sems("fin", "x_in0", "x_in1", "g_in", "sumsq", "root", "rcp", "y", "stored0", "stored1")
        x_in, stored = [s["x_in0"], s["x_in1"]], [s["stored0"], s["stored1"]]
        xt, y, g = sb("x", [P, 2, D]), sb("y", [P, 2, D]), sb("g", [P, D])
        junk, st = sb("junk", [P, D]), sb("stat", [P, 2, 4])
        with nc.Block() as block:
            @block.gpsimd
            def _(pool):
                pool.dma_start(g[:], d["g_final"].unsqueeze(0).to_broadcast([P, D])).then_inc(s["g_in"], 16)

                def body(tiles, r):
                    for t, b, u in tiles:
                        pool.wait_ge(s["y"], t + 1)
                        pool.dma_start(xt[:, b], K.xres[bass.ds(t * P, P), :]).then_inc(x_in[b], 16)
                over_tiles(pool, body)

            @block.sync
            def _(sp):
                for sem in stored:
                    sp.sem_inc(sem, 16)

                def body(tiles, r):
                    for t, b, u in tiles:
                        sp.wait_ge(s["y"], t + 3)
                        dst = d["o_y_prompt"][0] if r else d["o_y_sample"][0, bass.ds(t * P, P), :]
                        sp.dma_start(dst, y[:, b]).then_inc(stored[b], 16)
                over_tiles(sp, body)
                sp.wait_ge(stored[0], 16 + 16 * 5)
                sp.wait_ge(stored[1], 16 + 16 * 4)

            @block.scalar
            def _(act):
                def body(tiles, r):
                    for t, b, u in tiles:
                        act.wait_ge(x_in[b], u * 16 + 16)
                        act.activation(junk[:], xt[:, b], ACT.Square, accum_out=st[:, b, 0:1]).then_inc(s["sumsq"], 1)
                        act.wait_ge(s["sumsq"], t + 1)
                        act.activation(st[:, b, 1:2], st[:, b, 0:1], ACT.Sqrt, bias=K.eps[:], scale=1.0 / D).then_inc(s["root"], 1)
                over_tiles(act, body)

            @block.vector
            def _(dve):
                dve.sem_inc(s["y"], 2)
                dve.wait_ge(s["g_in"], 16)

                def body(tiles, r):
                    for t, b, u in tiles:
                        dve.wait_ge(s["root"], t + 1)
                        dve.reciprocal(st[:, b, 2:3], st[:, b, 1:2]).then_inc(s["rcp"], 1)
                        dve.wait_ge(s["rcp"], t + 1)
                        dve.wait_ge(stored[b], u * 16 + 16)
                        dve.scalar_tensor_tensor(y[:, b], xt[:, b], st[:, b, 2:3], g[:], ALU.mult, ALU.mult).then_inc(s["y"], 1)
                over_tiles(dve, body)


def stage_hgrn(K):
    nc, d = K.nc, K.d
    NSTATE = NS + 2
    N_DVE = 2 + 2 + 2 + 1 + LEVELS * 4 + 2 * NT + 3
    with ExitStack() as ctx:
        def sb(name, shape):
            return ctx.enter_context(nc.sbuf_tensor(f"hg_{name}", shape, F32))
        s = K.sems("hg", "f_in", "q_in", "v_in", "g_in", "st_in", "steps", "lb", "sig", "ready", "level", "next", "merged",
                   "kT", "ktok", "kv", "state", "S_out", "out", "o_out", "sq", "ssum", "root", "silu", "done", "asm")
        G = sb("G", [P, 2, T])
        Kx, Qx = sb("K", [P, 2, T]), sb("Q", [P, 2, T])
        q, v = sb("q", [P, T]), sb("v", [P, NT, P])
        g = q
        att, A = sb("att", [P, T]), sb("A", [P, T])
        S = sb("S", [P, 2, NSTATE, P])
        lens = [T >> i for i in range(LEVELS + 1)]
        Tl = [G] + [sb(f"T{i}", [P, 2, lens[i]]) for i in range(1, LEVELS + 1)]
        lb = sb("lb", [P, 4, HEADS_C])
        nbf = sb("nbf", [P, 2 * HEADS_C])
        R = [0, 3 * PIECE]
        bf_at = PARAMS["b_f"][0]

        def blocks(t, m, lo, n):
            full = t[:]
            return bass.AP(full.tensor, full.offset + lo, [list(full.ap[0]), [2 * m, n // (2 * m)], [T + m, 2], [1, m]])

        def factors(i, start, pair_step, j_step):
            full = Tl[i][:]
            m = 1 << i
            return bass.AP(full.tensor, full.offset + start, [list(full.ap[0]), [pair_step, T // (2 * m)], [j_step, 2], [0, m]])

        def order(r):
            lat = range(NS) if r == 0 else range(NS - 1, -1, -1)
            return [(c, i, i + 1) for i, c in enumerate(lat)] + [(NS, None, NS + 1)]

        def before(r, c):
            return c if r == 0 else NS - 1 - c

        def heads(eng, body):
            with eng.Fori(0, HEADS_C // 2) as i:
                for half in range(2):
                    body(i * 2 + half, i + 4 * half, half)

        with nc.Block() as block:
            @block.gpsimd
            def _(pool):
                def body(n, h, half):
                    pool.wait_ge(s["kv"], n * 2 + 1)
                    for r in range(2):
                        pool.dma_start(G[:, r], K.featT[bass.ds(h + (16 + 8 * r), 1)].rearrange("a p t -> (a p) t")).then_inc(s["f_in"], 16)
                    pool.wait_ge(s["out"], n + 1)
                    pool.dma_start(v[:], K.tok.rearrange("n t p f -> n p t f")[half, :, :, bass.ds((h - 4 * half) * P, P)]).then_inc(s["v_in"], 16)
                    pool.wait_ge(s["done"], n + 1)
                    pool.dma_start(q[:], K.featT[bass.ds(h, 1)].rearrange("a p t -> (a p) t")).then_inc(s["q_in"], 16)
                    pool.wait_ge(s["level"], n * (LEVELS + 1) + 1)
                    pool.dma_start(g[:], K.featT[bass.ds(h + 8, 1)].rearrange("a p t -> (a p) t")).then_inc(s["g_in"], 16)
                heads(pool, body)

            @block.sync
            def _(sp):
                sp.sem_inc(s["S_out"], 32)
                def body(n, h, half):
                    sp.wait_ge(s["out"], n + 1)
                    for r in range(2):
                        sp.dma_start(S[:, r, 0], d["state_hgrn_S"][0, 0, r, bass.ds(h, 1)].rearrange("a k v -> (a k) v")).then_inc(s["st_in"], 16)
                    sp.wait_ge(s["state"], n + 1)
                    for r in range(2):
                        sp.dma_start(d["o_new_S"][0, 0, r, bass.ds(h, 1)].rearrange("a k v -> (a k) v"), S[:, r, NS + 1]).then_inc(s["S_out"], 16)
                heads(sp, body)
                sp.wait_ge(s["S_out"], 32 * HEADS_C + 32)

            @block.scalar
            def _(act):
                act.sem_inc(s["root"], 1)
                act.wait_ge(s["lb"], 1)
                act.activation(lb[:, 1], lb[:, 0], ACT.Sigmoid).then_inc(s["lb"], 1)

                def body(n, h, half):
                    act.wait_ge(s["f_in"], n * 32 + 32)
                    act.wait_ge(s["done"], n + 1)
                    act.wait_ge(s["lb"], 3)
                    for r in range(2):
                        act.activation(Kx[:, r], G[:, r], ACT.Sigmoid, scale=-1.0, bias=nbf[:, bass.ds(h + 8 * r, 1)])
                        act.activation(G[:, r], G[:, r], ACT.Sigmoid, bias=K.par[:, bass.ds(h + (bf_at + 8 * r), 1)]).then_inc(s["sig"], 1)
                    act.wait_ge(s["ready"], n + 1)
                    for i in range(LEVELS):
                        if i:
                            act.wait_ge(s["next"], n * LEVELS + i)
                        act.copy(A[:].rearrange("p (b j m) -> p b j m", j=2, m=1 << i), blocks(Kx, 1 << i, 0, T)).then_inc(s["asm"], 1)
                    act.wait_ge(s["g_in"], n * 16 + 16)
                    act.activation(g[:], g[:], ACT.Silu).then_inc(s["silu"], 1)
                    for r in range(2):
                        act.wait_ge(s["kT"], n * 2 + r + 1)
                        act.copy(G[:, r], K.ps[:, R[r]:R[r] + T]).then_inc(s["ktok"], 1)
                    act.wait_ge(s["out"], n + 1 + 1)
                    act.copy(Kx[:, 0], K.ps[:, 0:T]).then_inc(s["o_out"], 1)
                    act.wait_ge(s["o_out"], n * 2 + 1)
                    act.activation(Kx[:, 1], Kx[:, 0], ACT.Square).then_inc(s["sq"], 1)
                    act.wait_ge(s["ssum"], n + 1)
                    act.activation(Kx[:, 1], K.ps[:, R[1]:R[1] + T], ACT.Sqrt, bias=K.eps[:], scale=1.0 / P).then_inc(s["root"], 1)
                    act.sem_inc(s["o_out"], 1)
                heads(act, body)

            @block.tensor
            def _(pe):
                pe.sem_inc(s["out"], 1)
                pe.sem_inc(s["kv"], 1)
                def body(n, h, half):
                    cols = lambda c: slice(c * P, (c + 1) * P)
                    pe.wait_ge(s["ready"], n + 1)
                    pe.wait_ge(s["root"], n + 1)
                    for c in range(NT):
                        a = R[0] + c * P
                        pe.matmul(K.ps[:, a:a + P], Kx[:, 0, cols(c)], q[:, cols(c)], start=True, stop=False)
                        mm = pe.matmul(K.ps[:, a:a + P], Kx[:, 1, cols(c)], q[:, cols(c)], start=False, stop=True)
                    mm.then_inc(s["level"], 1)
                    for i in range(LEVELS):
                        pe.wait_ge(s["asm"], n * LEVELS + i + 1)
                        pe.wait_ge(s["merged"], n * (LEVELS + 1) + i + 1)
                        for c in range(NT):
                            a = R[(i + 1) % 2] + c * P
                            mm = pe.matmul(K.ps[:, a:a + P], A[:, cols(c)], blocks(Qx, 1 << i, c * P, P),
                                           start=True, stop=True)
                        mm.then_inc(s["level"], 1)
                    pe.wait_ge(s["next"], (n + 1) * LEVELS)
                    for r in range(2):
                        pe.wait_ge(s["merged"], (n + 1) * (LEVELS + 1) + 1)
                        for c in range(NT):
                            mm = pe.transpose(K.ps[:, R[r] + c * P:R[r] + (c + 1) * P], Kx[:, r, cols(c)], K.c("ident"))
                        mm.then_inc(s["kT"], 1)
                    pe.wait_ge(s["v_in"], n * 16 + 16)
                    for r in range(2):
                        pe.wait_ge(s["ktok"], n * 2 + r + 1)
                        for c in range(NT):
                            mm = pe.matmul(K.ps[:, R[r] + c * P:R[r] + (c + 1) * P], G[:, r, cols(c)], v[:, c], start=True, stop=True)
                        mm.then_inc(s["kv"], 1)
                    pe.wait_ge(s["state"], n + 1)
                    for c in range(NT):
                        o = K.ps[:, c * P:(c + 1) * P]
                        if c < NS:
                            pe.matmul(o, S[:, 0, before(0, c)], Qx[:, 1, cols(c)], start=True, stop=False)
                            pe.matmul(o, S[:, 1, before(1, c)], Qx[:, 0, cols(c)], start=False, stop=False)
                        mm = pe.matmul(o, v[:, c], att[:, cols(c)], start=(c == NS), stop=True)
                    mm.then_inc(s["out"], 1)
                    pe.wait_ge(s["sq"], n + 1)
                    for c in range(3):
                        w = min(PIECE, T - c * PIECE)
                        mm = pe.matmul(K.ps[:, R[1] + c * PIECE:R[1] + c * PIECE + w], K.c("ones"), Kx[:, 1, c * PIECE:c * PIECE + w],
                                       start=True, stop=True)
                    mm.then_inc(s["ssum"], 1)
                heads(pe, body)

            @block.vector
            def _(dve):
                dve.sem_inc(s["merged"], 1)
                dve.sem_inc(s["done"], 1)
                gm = PARAMS["gamma"][0]
                dve.tensor_tensor(lb[:, 0], K.par[:, gm + 8:gm + 16], K.par[:, gm:gm + 8], ALU.subtract).then_inc(s["lb"], 1)
                dve.tensor_scalar(nbf[:], K.p("b_f"), -1.0, None, ALU.mult).then_inc(s["steps"], 1)
                dve.wait_ge(s["steps"], 1)
                dve.wait_ge(s["lb"], 2)
                dve.tensor_scalar(lb[:, 2], lb[:, 1], -1.0, 1.0, ALU.mult, ALU.add).then_inc(s["lb"], 1)
                dve.wait_ge(s["lb"], 3)

                def body(n, h, half):
                    step = Steps(dve, s["steps"], n, N_DVE)
                    step.base = step.base + 1
                    lbh, oml = lb[:, 1, bass.ds(h, 1)], lb[:, 2, bass.ds(h, 1)]
                    dve.wait_ge(s["sig"], n * 2 + 2)
                    for r in range(2):
                        step.did(dve.tensor_scalar(G[:, r], G[:, r], oml, lbh, ALU.mult, ALU.add))
                        step.did(dve.tensor_scalar(Kx[:, r], Kx[:, r], oml, None, ALU.mult))
                    step.wait()
                    dve.wait_ge(s["q_in"], n * 16 + 16)
                    for r in range(2):
                        step.did(dve.tensor_tensor(Qx[:, 1 - r], q[:], G[:, r], ALU.mult))
                    step.wait()
                    dve.sem_inc(s["ready"], 1)
                    ident = K.c("ident").unsqueeze(1).to_broadcast([P, NT, P])
                    chunked = att[:].rearrange("p (c n) -> p c n", n=P)
                    dve.wait_ge(s["level"], n * (LEVELS + 1) + 1)
                    step.did(dve.tensor_tensor(chunked, K.ps[:, R[0]:R[0] + T].rearrange("p (c n) -> p c n", n=P), ident, ALU.mult))
                    step.wait()
                    dve.sem_inc(s["merged"], 1)
                    for i in range(LEVELS):
                        m = 1 << i
                        L = lens[i]
                        dve.wait_ge(s["level"], n * (LEVELS + 1) + (i + 2))
                        dve.wait_ge(s["asm"], n * LEVELS + i + 1)
                        kb, qb = blocks(Kx, m, 0, T), blocks(Qx, m, 0, T)
                        step.did(dve.tensor_tensor(kb, kb, factors(i, 1, 2, L - 1), ALU.mult))
                        step.did(dve.tensor_tensor(qb, qb, factors(i, L + 1, 2, -(L + 1)), ALU.mult))
                        pair = Tl[i][:].rearrange("p r (n two) -> p r n two", two=2)
                        step.did(dve.tensor_tensor(Tl[i + 1][:], pair[:, :, :, 0], pair[:, :, :, 1], ALU.mult))
                        step.wait()
                        dve.sem_inc(s["next"], 1)
                        region = K.ps[:, R[(i + 1) % 2]:R[(i + 1) % 2] + T].rearrange("p (c n) -> p c n", n=P)
                        mask = K.level_masks[:, i].unsqueeze(1).to_broadcast([P, NT, P])
                        step.did(dve.copy_predicated(chunked, mask, region))
                        step.wait()
                        dve.sem_inc(s["merged"], 1)
                    dve.wait_ge(s["st_in"], n * 32 + 32)
                    dve.wait_ge(s["S_out"], n * 32 + 32)
                    for r in range(2):
                        dve.wait_ge(s["kv"], n * 2 + r + 1 + 1)
                        for c, i0, i1 in order(r):
                            kv = K.ps[:, R[r] + c * P:R[r] + (c + 1) * P]
                            if i0 is None:
                                ins = dve.tensor_copy(S[:, r, i1], kv)
                                step.did(ins)
                            else:
                                ins = dve.scalar_tensor_tensor(S[:, r, i1], S[:, r, i0], Tl[LEVELS][:, r, c:c + 1], kv, ALU.mult, ALU.add)
                                ins.then_inc(s["steps"], 1)
                                step.k += 1
                                step.wait()
                    step.wait()
                    dve.sem_inc(s["state"], 1)
                    dve.wait_ge(s["root"], n + 1 + 1)
                    step.did(dve.reciprocal(Kx[:, 1], Kx[:, 1]))
                    step.wait()
                    step.did(dve.scalar_tensor_tensor(Kx[:, 0], Kx[:, 0], K.par[:, bass.ds(h + PARAMS["g_hgrn"][0], 1)],
                                                      Kx[:, 1], ALU.mult, ALU.mult))
                    step.wait()
                    dve.wait_ge(s["silu"], n + 1)
                    step.did(dve.tensor_tensor(K.hT[:, bass.ds(h, 1), :].rearrange("p a t -> p (a t)"), Kx[:, 0], g[:], ALU.mult))
                    step.wait()
                    dve.sem_inc(s["done"], 1)
                    step.close()
                heads(dve, body)


def build(nc, d, stages=None):
    ctx = ExitStack()
    in_stage = []
    with ctx:
        def sb(name, shape, dt=F32):
            return ctx.enter_context(nc.sbuf_tensor(name, shape, dt))

        def dram(name, shape):
            return nc.dram_tensor(name, shape, F32).ap()

        def sems(stage, *names):
            held = {n: nc.alloc_semaphore(name=f"{stage}_{n}") for n in names}
            in_stage.extend(held.values())
            return held

        K = Shared(nc, d, ctx, sb, dram, sems)
        for n, stage in enumerate([
            lambda: stage_adaln(K),
            lambda: stage_norm(K, 0, 0, False),
            lambda: stage_project(K, "in_ab", AT_IN_AB, 3, 4, True),
            lambda: stage_attention(K),
            lambda: stage_gates(K),
            lambda: stage_mlstm(K),
            lambda: stage_out(K, 0),
            lambda: stage_route(K, 0),
            lambda: stage_experts(K, 0),
            lambda: stage_norm(K, 1, 0, False),
            lambda: stage_project(K, "in_c", AT_IN_C, 8, 2, False),
            lambda: stage_hgrn(K),
            lambda: stage_out(K, 1),
            lambda: stage_route(K, 1),
            lambda: stage_experts(K, 1),
            lambda: stage_final(K),
        ]):
            if stages is None or n < stages:
                stage()
                nc.clear_and_free_semaphores(list(in_stage))
                in_stage.clear()
                nc.all_engine_barrier()
        if stages is not None and stages < 99:
            total = K.loaded_after[stages]
            with nc.Block() as block:
                @block.sync
                def _(sp):
                    for i in range(SLOTS):
                        sp.wait_ge(K.w_loaded[i], 16 * len(range(i, total, SLOTS)))


_OUTS = [("y_prompt", (1, T_P, D)), ("y_sample", (1, T_S, D)),
         ("new_k", (1, 1, P, HEADS_A, 2 * DQK)), ("new_v", (1, 1, P, HEADS_A, P)),
         ("new_C", (1, 1, 2, HEADS_B, P, P)), ("new_n", (1, 1, 2, HEADS_B, P)), ("new_m", (1, 1, 2, HEADS_B)),
         ("new_S", (1, 1, 2, HEADS_C, P, P))]


def columns(v):
    return np.ascontiguousarray(v).reshape(-1, P).T


def shape_constants():
    c = np.zeros((P, N_CONSTS), np.float32)

    def put(name, a):
        c[:a.shape[0], CONSTS[name][0]:CONSTS[name][0] + CONSTS[name][1]] = a
    i, j = np.arange(P)[:, None], np.arange(P)[None, :]
    put("ident", np.eye(P))
    put("ones", np.ones((P, P)))
    put("neg_fwd", np.where(i <= j, 0.0, NEG))
    put("neg_bwd", np.where(i >= j, 0.0, NEG))
    n_freq = DQK // 4
    inv = np.power(np.float32(10000.0), -np.arange(n_freq, dtype=np.float32) / n_freq).astype(np.float32)
    t = np.arange(T_S)
    ang = np.concatenate([(t // GRID_W).astype(np.float32)[:, None] * inv,
                          (t % GRID_W).astype(np.float32)[:, None] * inv], axis=1).astype(np.float32)
    cos, sin = np.cos(ang), np.sin(ang)
    rope = np.stack([np.concatenate(x, 1).reshape(NS, P, P).transpose(1, 0, 2)
                     for x in ([cos] * 4, [-sin, sin] * 2)], 1)
    k = np.arange(T)
    resets = np.tile(np.stack([k % P != 0, k % P != P - 1]).astype(np.float32), (4, 1, 1))
    masks = np.stack([((i >> (m + 1)) == (j >> (m + 1))) & ((i >> m) != (j >> m)) for m in range(LEVELS)], 1)
    return c, masks.astype(np.uint32), np.ascontiguousarray(rope, np.float32), resets


_DIRECT = ["x_prompt", "x_sample", "cache_dattn_k", "cache_dattn_v", "state_mlstm_C", "state_mlstm_n",
           "state_mlstm_m", "state_hgrn_S", "w_ada", "g_final", "w_in_ab", "b_ig_ab", "b_fg_ab", "w_out_ab",
           "w_in_c", "w_out_c", "w_router", "w_gate_e", "w_up_e", "w_down_e"]


def laid_out(inputs):
    a = {n: np.ascontiguousarray(inputs[n]) for n in _DIRECT}
    a["params"] = np.concatenate([columns(np.asarray(inputs[n])) for n in (
        "c", "c_ctx", "b_ada", "g_norm", "g_attn_ab", "g_mlstm_ab", "conv_ab", "b_f_c", "gamma_lb", "g_hgrn_c")], axis=1)
    a["lam_ab"] = np.ascontiguousarray(inputs["lam_ab"]).reshape(1, -1)
    a["consts"], a["level_masks"], a["rope"], a["resets"] = shape_constants()
    return a


def declare(nc, arrays):
    d = {n: nc.dram_tensor(f"in_{n}", a.shape, mybir.dt.from_np(a.dtype), kind="ExternalInput").ap()
         for n, a in arrays.items()}
    d.update({f"o_{n}": nc.dram_tensor(f"out_{n}", shape, F32, kind="ExternalOutput").ap() for n, shape in _OUTS})
    return d


def kernel(**inputs):
    import concourse.bacc as _bacc
    from concourse.bass_utils import run_bass_kernel_spmd as _run

    nc = _bacc.Bacc("TRN2", target_bir_lowering=False, num_devices=1)
    arrays = laid_out(inputs)
    build(nc, declare(nc, arrays))
    r = _run(nc, [{f"in_{n}": a for n, a in arrays.items()}], core_ids=[0])
    return tuple(r.results[0][f"out_{n}"] for n, _ in _OUTS)
```

```python
from contextlib import ExitStack

import numpy as np
import concourse.bass as bass
from concourse import mybir

P = 128
D = 1024
KT = D // P
T_S, T_P = 1024, 128
T = T_S + T_P
NT = T // P
NS = T_S // P
STREAMS = 2
DEPTH = 2
HEADS_A = HEADS_B = 4
HEADS_C = 8
DQK = 64
GRID_W = 64
EXPERTS = 16
CAP_S, CAP_P = 2 * T_S // EXPERTS, 2 * T_P // EXPERTS
CAP = CAP_S + CAP_P
PIECE = 512
SLOTS = 6
EPS = 1e-6
LAM_INIT = float(0.8 - 0.6 * np.exp(-0.3 * 0))
NEG = -1e30
LEVELS = 7

F32 = mybir.dt.float32
U32 = mybir.dt.uint32
I32 = mybir.dt.int32
ALU = mybir.AluOpType
ACT = mybir.ActivationFunctionType
AX_X = mybir.AxisListType.X


def fields(sizes):
    out, at = {}, 0
    for name, n in sizes:
        out[name] = (at, n)
        at += n
    return out, at


PARAMS, N_PARAMS = fields([
    ("c", KT), ("c_ctx", KT), ("b_ada", DEPTH * 6 * KT), ("g_norm", DEPTH * 2 * KT),
    ("g_attn", 4), ("g_mlstm", 4), ("conv", 3 * 8), ("b_f", 16), ("gamma", 16), ("g_hgrn", 8)])
CONSTS, N_CONSTS = fields([
    ("ident", P), ("ones", P), ("neg_fwd", P), ("neg_bwd", P)])


def weight_pieces(d):
    def cols(w, c):
        return w.rearrange("(k p) f -> p k f", p=P)[:, :, c * PIECE:(c + 1) * PIECE]

    out = [cols(d["w_ada"][l], c) for l in range(DEPTH) for c in range(12)]
    out += [cols(d["w_in_ab"][0], c) for c in AB_FEATURE + AB_TOKEN]
    for l in range(DEPTH):
        if l == 1:
            out += [cols(d["w_in_c"][0], c) for c in C_FEATURE + C_TOKEN]
        w_out = d["w_out_ab"][0] if l == 0 else d["w_out_c"][0]
        out += [cols(w_out, c) for c in range(2)]
        for e in range(EXPERTS):
            out += [cols(w, c) for c in range(2) for w in (d["w_gate_e"][l, e], d["w_up_e"][l, e])]
            out += [cols(d["w_down_e"][l, e], c) for c in range(2)]
    return out


AB_FEATURE, AB_TOKEN = [3, 4, 6], [0, 1, 2, 5]
C_FEATURE, C_TOKEN = [0, 1, 4, 5, 6, 7, 8, 9], [2, 3]
N_ADA = 24
AT_IN_AB = N_ADA
AT_OUT = [AT_IN_AB + 7, AT_IN_AB + 7 + 2 + 6 * EXPERTS + 10]
AT_EXPERTS = [a + 2 for a in AT_OUT]
AT_IN_C = AT_EXPERTS[0] + 6 * EXPERTS


class Shared:

    def __init__(self, nc, d, ctx, sb, dram, sems):
        self.nc, self.d, self.sems = nc, d, sems
        self.W = sb("weights", [P, SLOTS, KT, PIECE])
        self.pieces = weight_pieces(d)
        self.w_used = ctx.enter_context(nc.semaphore("w_used"))
        self.w_loaded = [ctx.enter_context(nc.semaphore(f"w_loaded{i}")) for i in range(SLOTS)]
        self.loaded_after = [0, 30, 30, 37, 37, 37, 37, 39, 39, 135, 135, 141, 141, 147, 147, 237, 237]
        self.ps = ctx.enter_context(nc.psum_tensor("ps", [P, 8 * PIECE], F32))
        self.par, self.cst = sb("params_sb", [P, N_PARAMS]), sb("consts_sb", [P, N_CONSTS])
        self.eps = sb("eps", [P, 1])
        self.level_masks = sb("level_masks_sb", [P, LEVELS, P], U32)
        self.w_router = sb("w_router_sb", [P, DEPTH, KT, EXPERTS])
        self.lam_row = sb("lam_row", [1, 4 * DQK])
        self.hT = sb("hT", [P, KT, T])
        self.ada, self.scale = sb("ada", [P, STREAMS, DEPTH * 6 * KT]), sb("scale", [P, DEPTH, 2, STREAMS, KT])
        self.idx_s, self.gate_s = sb("idx_s", [P, EXPERTS], I32), sb("gate_s", [P, EXPERTS])
        self.idx_p, self.gate_p = sb("idx_p", [CAP_P, EXPERTS], I32), sb("gate_p", [CAP_P, EXPERTS])
        self.w_arg, self.w_state = sb("w_arg", [P, 2, NT, HEADS_B]), sb("w_state", [P, 2, NT, HEADS_B])
        self.xres, self.xnorm = dram("x_residual", [T, D]), dram("x_norm", [T, D])
        self.gate1_rows = dram("gate1_rows", [DEPTH, STREAMS, D])
        self.featT, self.tok = dram("feature_rows", [32, P, T]), dram("token_rows", [4, NT, P, PIECE])
        self.gate_rows, self.mrows = dram("mlstm_gate_rows", [4, 4, T]), dram("mlstm_rows", [2, 2, 4, T])
        self.msmall = dram("mlstm_chunks", [2, 2, 4, NT])

    def p(self, name):
        at, n = PARAMS[name]
        return self.par[:, at:at + n]

    def c(self, name):
        at, n = CONSTS[name]
        return self.cst[:, at:at + n]


class Steps:

    def __init__(self, eng, sem, turn=0, per=0):
        self.eng, self.sem, self.base, self.k, self.per = eng, sem, turn * per, 0, per

    def did(self, ins):
        ins.then_inc(self.sem, 1)
        self.k += 1

    def wait(self):
        self.eng.wait_ge(self.sem, self.base + self.k)

    def close(self):
        assert self.k == self.per, self.k


def load_piece(K, sp, n, src=None):
    if n >= SLOTS:
        sp.wait_ge(K.w_used, n - SLOTS + 1)
    sp.dma_start(K.W[:, n % SLOTS], K.pieces[n] if src is None else src).then_inc(K.w_loaded[n % SLOTS], 16)


def wait_piece(K, pe, n):
    pe.wait_ge(K.w_loaded[n % SLOTS], 16 * (n // SLOTS + 1))


def stage_adaln(K):
    nc, d = K.nc, K.d
    with ExitStack() as ctx:
        s = K.sems("ada", "par", "silu", "added", "mod", "turned", "rows", "rows_out", "x_copied", "consts", "pack", "copied", "columns", "turning")
        condT = ctx.enter_context(nc.sbuf_tensor("condT", [P, KT, STREAMS], F32))
        cpack = ctx.enter_context(nc.sbuf_tensor("cpack", [P, KT, STREAMS], F32))
        row2 = ctx.enter_context(nc.sbuf_tensor("ada_rows", [STREAMS, 2, PIECE], F32))
        rows = ctx.enter_context(nc.sbuf_tensor("gate_rows", [KT, DEPTH * STREAMS * P], F32))
        with nc.Block() as block:
            @block.sync
            def _(sp):
                for n in range(SLOTS):
                    load_piece(K, sp, n)
                for n in range(SLOTS, N_ADA + SLOTS):
                    load_piece(K, sp, n)

            @block.gpsimd
            def _(pool):
                pool.dma_start(K.xres[0:T_S, :], d["x_sample"][0]).then_inc(s["x_copied"], 16)
                pool.dma_start(K.xres[T_S:T, :], d["x_prompt"][0]).then_inc(s["x_copied"], 16)
                pool.wait_ge(s["rows"], 1)
                for l in range(DEPTH):
                    for r in range(STREAMS):
                        j = (l * STREAMS + r) * P
                        pool.dma_start(K.gate1_rows[l, r].rearrange("(k p) -> k p", p=P),
                                       rows[:, j:j + P]).then_inc(s["rows_out"], 16)
                pool.wait_ge(s["rows_out"], 16 * DEPTH * STREAMS)
                pool.wait_ge(s["x_copied"], 32)

            @block.scalar
            def _(act):
                act.dma_start(K.par[:], d["params"]).then_inc(s["par"], 16)
                act.dma_start(K.cst[:], d["consts"]).then_inc(s["consts"], 16)
                act.dma_start(K.level_masks[:], d["level_masks"]).then_inc(s["consts"], 16)
                act.dma_start(K.w_router[:], d["w_router"].rearrange("l (k p) e -> p l k e", p=P)).then_inc(s["consts"], 16)
                act.dma_start(K.lam_row[:], d["lam_ab"]).then_inc(s["consts"], 16)
                act.wait_ge(s["pack"], 3)
                act.activation(condT[:], cpack[:], ACT.Silu).then_inc(s["silu"], 1)
                act.sem_inc(s["copied"], 2)
                with act.Fori(0, N_ADA // 2) as i:
                    for par in range(2):
                        q = i * 2 + par
                        act.wait_ge(K.w_used, q + 1)
                        act.wait_ge(s["added"], q + 1)
                        act.copy(row2[:, par], K.ps[0:STREAMS, par * PIECE:(par + 1) * PIECE]).then_inc(s["copied"], 1)
                act.wait_ge(s["consts"], 64)

            @block.tensor
            def _(pe):
                def product(q, bank, turn):
                    pe.wait_ge(s["copied"], q + 1)
                    pe.wait_ge(K.w_loaded[bank], turn * 16 + 16)
                    for k in range(KT):
                        mm = pe.matmul(K.ps[0:STREAMS, bank % 2 * PIECE:(bank % 2 + 1) * PIECE], condT[:, k, :], K.W[:, bank, k],
                                       start=(k == 0), stop=(k == KT - 1))
                    mm.then_inc(K.w_used, 1)

                def turn_rows(q, bank):
                    pe.wait_ge(s["copied"], q + 3)
                    pe.wait_ge(s["added"], q + 1)
                    pe.sem_inc(s["turning"], 1)
                    for ft in range(4):
                        a = (2 + bank % 2) * PIECE + ft * STREAMS
                        mm = pe.transpose(K.ps[:, a:a + STREAMS], row2[:, bank % 2, ft * P:(ft + 1) * P], K.cst[0:STREAMS, 0:STREAMS])
                    mm.then_inc(s["columns"], 1)
                pe.wait_ge(s["silu"], 1)
                pe.wait_ge(s["consts"], 64)
                with pe.Fori(0, N_ADA // SLOTS) as i:
                    for slot in range(SLOTS):
                        product(i * SLOTS + slot, slot, i)
                        if slot:
                            turn_rows(i * SLOTS + slot - 1, slot - 1)
                    turn_rows(i * SLOTS + SLOTS - 1, SLOTS - 1)
                pe.wait_ge(s["mod"], 1)
                for l in range(DEPTH):
                    for r in range(STREAMS):
                        j = (l * STREAMS + r) * P
                        mm = pe.transpose(K.ps[0:KT, 4 * PIECE + j:4 * PIECE + j + P],
                                          K.ada[:, r, l * 48 + 16:l * 48 + 24], K.c("ident"))
                mm.then_inc(s["turned"], 1)

            @block.vector
            def _(dve):
                dve.sem_inc(s["added"], 2)
                dve.wait_ge(s["par"], 16)
                dve.tensor_copy(cpack[:, :, 0], K.p("c")).then_inc(s["pack"], 1)
                dve.tensor_copy(cpack[:, :, 1], K.p("c_ctx")).then_inc(s["pack"], 1)
                dve.memset(K.eps[:], EPS).then_inc(s["pack"], 1)
                b_ada = PARAMS["b_ada"][0]
                with dve.Fori(0, N_ADA // 2) as i:
                    for par in range(2):
                        q = i * 2 + par
                        dve.wait_ge(s["columns"], q + 1)
                        for r in range(STREAMS):
                            a = (2 + par) * PIECE
                            ins = dve.tensor_tensor(
                                K.ada[:, r, bass.ds(q * 4, 4)],
                                K.ps[:, a:a + 4 * STREAMS].rearrange("p (f r) -> p r f", r=STREAMS)[:, r],
                                K.par[:, bass.ds(q * 4 + b_ada, 4)], ALU.add)
                        ins.then_inc(s["added"], 1)
                dve.wait_ge(s["added"], 2 + N_ADA)
                gn = PARAMS["g_norm"][0]
                for l in range(DEPTH):
                    for j in range(2):
                        for r in range(STREAMS):
                            g0 = gn + (l * 2 + j) * KT
                            c = l * 48 + (3 * j + 1) * KT
                            ins = dve.scalar_tensor_tensor(K.scale[:, l, j, r, :], K.ada[:, r, c:c + KT], 1.0,
                                                           K.par[:, g0:g0 + KT], ALU.add, ALU.mult)
                ins.then_inc(s["mod"], 1)
                dve.wait_ge(s["turned"], 1)
                dve.tensor_copy(rows[:], K.ps[0:KT, 4 * PIECE:4 * PIECE + DEPTH * STREAMS * P]).then_inc(s["rows"], 1)


def over_tiles(eng, body):
    with eng.Fori(0, NS // 2) as i:
        body([(i * 2, 0, i), (i * 2 + 1, 1, i)], 0)
    body([(NS, 0, NS // 2)], 1)


def stage_norm(K, l, j, store):
    nc = K.nc
    with ExitStack() as ctx:
        s = K.sems(f"norm{l}{j}", "x_in0", "x_in1", "xn_ready", "sumsq", "root", "rcp", "turned", "act_evac", "dve_evac", "stored0", "stored1")
        x_in, stored = [s["x_in0"], s["x_in1"]], [s["stored0"], s["stored1"]]
        xt = ctx.enter_context(nc.sbuf_tensor(f"xt{l}{j}", [P, 2, D], F32))
        xn = ctx.enter_context(nc.sbuf_tensor(f"xn{l}{j}", [P, 2, D], F32))
        junk = ctx.enter_context(nc.sbuf_tensor(f"junk{l}{j}", [P, D], F32))
        st = ctx.enter_context(nc.sbuf_tensor(f"stat{l}{j}", [P, 2, 4], F32))
        shift_at = l * 48 + 3 * j * KT
        with nc.Block() as block:
            @block.gpsimd
            def _(pool):
                def body(tiles, r):
                    for t, b, u in tiles:
                        pool.wait_ge(s["xn_ready"], t + 1)
                        pool.dma_start(xt[:, b], K.xres[bass.ds(t * P, P), :]).then_inc(x_in[b], 16)
                over_tiles(pool, body)

            @block.sync
            def _(sp):
                if store:
                    sp.sem_inc(stored[0], 16)
                    sp.sem_inc(stored[1], 16)

                    def body(tiles, r):
                        for t, b, u in tiles:
                            sp.wait_ge(s["xn_ready"], t + 3)
                            sp.dma_start(K.xnorm[bass.ds(t * P, P), :], xn[:, b]).then_inc(stored[b], 16)
                    over_tiles(sp, body)
                    sp.wait_ge(stored[0], 16 + 16 * 5)
                    sp.wait_ge(stored[1], 16 + 16 * 4)

            @block.scalar
            def _(act):
                def body(tiles, r):
                    for t, b, u in tiles:
                        act.wait_ge(x_in[b], u * 16 + 16)
                        act.activation(junk[:], xt[:, b], ACT.Square, accum_out=st[:, b, 0:1]).then_inc(s["sumsq"], 1)
                        act.wait_ge(s["sumsq"], t + 1)
                        act.activation(st[:, b, 1:2], st[:, b, 0:1], ACT.Sqrt, bias=K.eps[:], scale=1.0 / D).then_inc(s["root"], 1)
                    for t, b, u in tiles:
                        act.wait_ge(s["turned"], t + 3)
                        for k in range(KT // 2):
                            ins = act.activation(K.hT[:, k, bass.ds(t * P, P)], K.ps[:, b * D + k * P:b * D + (k + 1) * P],
                                                 ACT.Identity, bias=K.ada[:, r, shift_at + k:shift_at + k + 1],
                                                 scale=K.scale[:, l, j, r, k:k + 1])
                        ins.then_inc(s["act_evac"], 1)
                act.sem_inc(s["act_evac"], 2)
                over_tiles(act, body)

            @block.tensor
            def _(pe):
                def body(tiles, r):
                    for t, b, u in tiles:
                        pe.wait_ge(s["xn_ready"], t + 3)
                        pe.wait_ge(s["act_evac"], t + 1)
                        pe.wait_ge(s["dve_evac"], t + 1)
                        for k in range(KT):
                            mm = pe.transpose(K.ps[:, b * D + k * P:b * D + (k + 1) * P],
                                              xn[:, b, k * P:(k + 1) * P], K.c("ident"))
                        mm.then_inc(s["turned"], 1)
                pe.sem_inc(s["turned"], 2)
                over_tiles(pe, body)

            @block.vector
            def _(dve):
                def body(tiles, r):
                    for t, b, u in tiles:
                        dve.wait_ge(s["root"], t + 1)
                        dve.reciprocal(st[:, b, 2:3], st[:, b, 1:2]).then_inc(s["rcp"], 1)
                        dve.wait_ge(s["rcp"], t + 1)
                        dve.wait_ge(s["turned"], t + 1)
                        if store:
                            dve.wait_ge(stored[b], u * 16 + 16)
                        dve.tensor_scalar(xn[:, b], xt[:, b], st[:, b, 2:3], None, ALU.mult).then_inc(s["xn_ready"], 1)
                    for t, b, u in tiles:
                        dve.wait_ge(s["turned"], t + 3)
                        for k in range(KT // 2, KT):
                            ins = dve.tensor_scalar(K.hT[:, k, bass.ds(t * P, P)], K.ps[:, b * D + k * P:b * D + (k + 1) * P],
                                                    K.scale[:, l, j, r, k:k + 1],
                                                    K.ada[:, r, shift_at + k:shift_at + k + 1], ALU.mult, ALU.add)
                        ins.then_inc(s["dve_evac"], 1)
                dve.sem_inc(s["xn_ready"], 2)
                dve.sem_inc(s["dve_evac"], 2)
                over_tiles(dve, body)


def stage_project(K, name, at, n_feature, n_token, gates):
    nc, d = K.nc, K.d
    TC = T // 3
    n_groups = n_feature * 12 + n_token * NT
    with ExitStack() as ctx:
        s = K.sems(name, "group", "even_out", "odd_out", "stored0", "stored1", "stored2", "stored3",
                   "wg_in", "gates", "round_out", "gates_out", "gates_stored")
        stored = [s["stored0"], s["stored1"], s["stored2"], s["stored3"]]
        stg = ctx.enter_context(nc.sbuf_tensor(f"{name}_stage", [P, 4, PIECE], F32))
        if gates:
            wg = ctx.enter_context(nc.sbuf_tensor("w_gates", [P, KT, 16], F32))
            gsb = ctx.enter_context(nc.sbuf_tensor("gates_sb", [4, 4, T], F32))

        def groups():
            for f in range(n_feature):
                yield "feature", f, f * 12
            for t in range(n_token):
                yield "token", t, n_feature * 12 + t * NT

        def take_out(eng, copy, mine, out_sem):
            def one(g, bank, width, use):
                eng.wait_ge(s["group"], g + 1)
                eng.wait_ge(stored[bank], use * 16 + 16)
                copy(stg[:, bank, 0:width], K.ps[:, bank * PIECE:bank * PIECE + width]).then_inc(out_sem, 1)
            for kind, n, g0 in groups():
                if kind == "feature":
                    with eng.Fori(0, 3) as c:
                        for ft in range(mine, 4, 2):
                            one(c * 4 + (g0 + ft), ft, TC, c + g0 // 4)
                else:
                    for t in range(NT):
                        g = g0 + t
                        if g % 2 == mine:
                            one(g, g % 4, PIECE, g // 4)

        with nc.Block() as block:
            @block.sync
            def _(sp):
                for sem in stored:
                    sp.sem_inc(sem, 16)

                def out(g):
                    return s["even_out"] if g % 2 == 0 else s["odd_out"]
                for kind, n, g0 in groups():
                    if kind == "feature":
                        with sp.Fori(0, 3) as c:
                            for ft in range(4):
                                sp.wait_ge(out(ft), c * 2 + ((g0 + ft) // 2 + 1))
                                sp.dma_start(K.featT[n * 4 + ft, :, bass.ds(c * TC, TC)],
                                             stg[:, ft, 0:TC]).then_inc(stored[ft], 16)
                    else:
                        for t in range(NT):
                            g = g0 + t
                            sp.wait_ge(out(g), g // 2 + 1)
                            sp.dma_start(K.tok[n, t], stg[:, g % 4, :]).then_inc(stored[g % 4], 16)
                    ahead = at + SLOTS + (n if kind == "feature" else n_feature + n)
                    if not AT_EXPERTS[1] <= ahead < AT_EXPERTS[1] + SLOTS:
                        load_piece(K, sp, ahead)
                for b in range(4):
                    sp.wait_ge(stored[b], 16 + 16 * len(range(b, n_groups, 4)))

            @block.gpsimd
            def _(pool):
                if gates:
                    pool.dma_start(wg[:], d["w_in_ab"][0].rearrange("(k p) f -> p k f", p=P)[:, :, 3584:3600]).then_inc(s["wg_in"], 16)
                    pool.wait_ge(s["gates_out"], 1)
                    pool.dma_start(K.gate_rows.rearrange("k h t -> h k t"), gsb[:]).then_inc(s["gates_stored"], 16)
                    pool.wait_ge(s["gates_stored"], 16)

            @block.scalar
            def _(act):
                take_out(act, act.copy, 1, s["odd_out"])

            @block.vector
            def _(dve):
                take_out(dve, dve.tensor_copy, 0, s["even_out"])
                if gates:
                    for rnd in range(2):
                        dve.wait_ge(s["gates"], rnd + 1)
                        ins = dve.tensor_copy(gsb[:, 2 * rnd:2 * rnd + 2, :],
                                              K.ps[0:4, 0:2 * T].rearrange("h (k t) -> h k t", k=2))
                        ins.then_inc(s["gates_out"] if rnd else s["round_out"], 1)

            @block.tensor
            def _(pe):
                def bank_free(g_mod, count):
                    pe.wait_ge(s["even_out"] if g_mod % 2 == 0 else s["odd_out"], count)
                for kind, n, g0 in groups():
                    piece = at + (n if kind == "feature" else n_feature + n)
                    wait_piece(K, pe, piece)
                    w = K.W[:, piece % SLOTS]
                    if kind == "feature":
                        def chunk(c, first):
                            for ft in range(4):
                                if not first:
                                    bank_free(ft, c * 2 + ((g0 + ft - 4) // 2 + 1))
                                for k in range(KT):
                                    mm = pe.matmul(K.ps[:, ft * PIECE:ft * PIECE + TC], w[:, k, ft * P:(ft + 1) * P],
                                                   K.hT[:, k, bass.ds(c * TC, TC)], start=(k == 0), stop=(k == KT - 1))
                                mm.then_inc(s["group"], 1)
                        if g0 == 0:
                            chunk(0, True)
                            with pe.Fori(1, 3) as c:
                                chunk(c, False)
                        else:
                            with pe.Fori(0, 3) as c:
                                chunk(c, False)
                    else:
                        for t in range(NT):
                            g = g0 + t
                            bank_free(g, (g - 4) // 2 + 1)
                            for k in range(KT):
                                mm = pe.matmul(K.ps[:, g % 4 * PIECE:(g % 4 + 1) * PIECE],
                                               K.hT[:, k, t * P:(t + 1) * P], w[:, k, :], start=(k == 0), stop=(k == KT - 1))
                            mm.then_inc(s["group"], 1)
                    pe.drain().then_inc(K.w_used, 1)
                if gates:
                    pe.wait_ge(s["wg_in"], 16)
                    bank_free(0, len(range(0, n_groups, 2)))
                    bank_free(1, len(range(1, n_groups, 2)))
                    for rnd in range(2):
                        if rnd:
                            pe.wait_ge(s["round_out"], 1)
                        for q in range(2):
                            kind = 2 * rnd + q
                            for c0, n in [(q * T + a, b) for a, b in ((0, 384), (384, 384), (768, 384))]:
                                cut = min(n, PIECE - c0 % PIECE)
                                for a, m in ((c0, cut), (c0 + cut, n - cut)):
                                    if m:
                                        for k in range(KT):
                                            mm = pe.matmul(K.ps[0:4, a:a + m], wg[:, k, kind * 4:kind * 4 + 4],
                                                           K.hT[:, k, a - q * T:a - q * T + m], start=(k == 0), stop=(k == KT - 1))
                        mm.then_inc(s["gates"], 1)


def stage_attention(K):
    nc, d = K.nc, K.d
    NK = NT + 1
    KEYS = T
    SC = float(DQK) ** -0.5
    CH = KEYS // 3
    PER_TILE = 6
    with ExitStack() as ctx:
        def sb(name, shape):
            return ctx.enter_context(nc.sbuf_tensor(f"att_{name}", shape, F32))
        s = K.sems("att", "q_in", "k_in", "v_in", "rope_in", "rope_steps", "steps", "roped", "k_turned", "q_turned", "kT_out",
                   "qT_out", "scored", "bias", "expd", "mixed", "aT", "aT_out", "av", "av_out", "root", "normed", "o_turned",
                   "o_out", "lam_steps", "lam_e", "lam_ps", "kept")
        q, k, v = sb("q", [P, NT, P]), sb("k", [P, NK, P]), sb("v", [P, NK, P])
        qr, tmp = sb("qr", [P, NS, P]), sb("tmp", [P, NS, P])
        kr = sb("kr", [P, NS, P])
        rope = sb("rope", [P, 2, NS, P])
        qT, kT = sb("qT", [P, T]), sb("kT", [P, NK * P])
        assert KEYS == T
        p0, p1 = K.hT[:, 4:6], sb("p1", [P, 2, KEYS])
        aT = K.hT[:, 6]
        o, sq = K.hT[:, 7].rearrange("p (t f) -> p t f", f=P), sb("sq", [P, P])
        rms = sb("rms", [P, 3, NT])
        st = sb("stat", [P, 2, 8])
        lam = sb("lam", [1, 4 * DQK])
        nlam = sb("nlam", [P, 1])
        gs = sb("g_scaled", [P, HEADS_A])
        S0 = 0
        TR, AV = 6 * PIECE, 7 * PIECE

        def q_cols(i):
            return slice(i * P, (i + 1) * P)

        def keys_of(i):
            return (0, NT) if i < NS else (KEYS, 1)

        def chunks(n_tiles):
            return [(c, CH) for c in range(3)] if n_tiles == NT else [(0, P)]

        def scores_ps(j, n_tiles):
            a = S0 + j * 3 * PIECE
            if n_tiles == 1:
                return K.ps[:, a:a + P].rearrange("p (c n) -> p c n", c=1)
            return K.ps[:, a:a + 3 * PIECE].rearrange("p (c n) -> p c n", c=3)[:, :, 0:CH]

        def rounds(n_tiles):
            return [(a, min(4, n_tiles - a)) for a in range(0, n_tiles, 4)]
        ROUNDS = [sum(len(rounds(keys_of(j)[1])) for j in range(i)) for i in range(NT + 1)]

        with nc.Block() as block:
            @block.sync
            def _(sp):
                sp.dma_start(d["o_new_k"][0, 0].rearrange("t h f -> t (h f)"), K.tok[1, NS]).then_inc(s["kept"], 16)
                sp.dma_start(d["o_new_v"][0, 0].rearrange("t h f -> t (h f)"), K.tok[2, NS]).then_inc(s["kept"], 16)
                sp.wait_ge(s["kept"], 32)

            @block.gpsimd
            def _(pool):
                pool.dma_start(rope[:], d["rope"]).then_inc(s["rope_in"], 16)
                tok = K.tok.rearrange("n t p f -> n p t f")

                def load_q(h):
                    pool.dma_start(q[:], tok[0, :, :, bass.ds(h * P, P)]).then_inc(s["q_in"], 16)

                def load_k(h):
                    pool.dma_start(k[:, 1:NK], tok[1, :, :, bass.ds(h * P, P)]).then_inc(s["k_in"], 16)
                    pool.dma_start(k[:, 0], d["cache_dattn_k"][0, 0, :, bass.ds(h, 1), :].rearrange("t a f -> t (a f)")).then_inc(s["k_in"], 16)

                def load_v(h):
                    pool.dma_start(v[:, 1:NK], tok[2, :, :, bass.ds(h * P, P)]).then_inc(s["v_in"], 16)
                    pool.dma_start(v[:, 0], d["cache_dattn_v"][0, 0, :, bass.ds(h, 1), :].rearrange("t a f -> t (a f)")).then_inc(s["v_in"], 16)
                load_q(0)
                load_k(0)
                load_v(0)
                with pool.Fori(1, HEADS_A) as h:
                    pool.wait_ge(s["k_turned"], h)
                    pool.wait_ge(s["q_turned"], h)
                    load_q(h)
                    load_k(h)
                    pool.wait_ge(s["av"], h * NT)
                    load_v(h)

            def over_heads(eng, body):
                with eng.Fori(0, HEADS_A - 1) as h:
                    body(h, True)
                body(HEADS_A - 1, False)

            @block.tensor
            def _(pe):
                pe.wait_ge(s["lam_steps"], 6)
                pe.matmul(K.ps[:, AV:AV + 1], K.cst[0:1, P:2 * P], lam[0:1, 8:9], start=True, stop=True).then_inc(s["lam_ps"], 1)

                def turn_k(h):
                    pe.wait_ge(s["roped"], h * 2 + 2)
                    for i in range(NK):
                        src = kr[:, i - 1] if 1 <= i <= NS else k[:, i]
                        mm = pe.transpose(K.ps[:, 3 * PIECE + i * P:3 * PIECE + (i + 1) * P], src, K.c("ident"))
                    mm.then_inc(s["k_turned"], 1)

                def turn_q(h):
                    pe.wait_ge(s["roped"], h * 2 + 1)
                    for i in range(NT):
                        src = qr[:, i] if i < NS else q[:, i]
                        mm = pe.transpose(K.ps[:, i * P:(i + 1) * P], src, K.c("ident"))
                    mm.then_inc(s["q_turned"], 1)
                turn_k(0)
                turn_q(0)

                def head(h, more):
                    pe.wait_ge(s["kT_out"], h + 1)
                    pe.wait_ge(s["qT_out"], h + 1)

                    def score(i):
                        k0, n = keys_of(i)
                        for j in range(2):
                            if i > 0:
                                pe.wait_ge(s["expd"], h * 2 * NT + (2 * (i - 1) + j + 1))
                            rows = slice(j * DQK, (j + 1) * DQK)
                            for c, w in chunks(n):
                                a = S0 + (3 * j + c) * PIECE
                                mm = pe.matmul(K.ps[:, a:a + w], qT[rows, q_cols(i)],
                                               kT[rows, k0 + c * CH:k0 + c * CH + w], start=True, stop=True)
                            mm.then_inc(s["scored"], 1)

                    def turn_and_product(i):
                        k0, n = keys_of(i)
                        pe.wait_ge(s["mixed"], h * NT + (i + 1))
                        for r, (a, m) in enumerate(rounds(n)):
                            done = ROUNDS[i] + r
                            pe.wait_ge(s["aT_out"], h * ROUNDS[NT] + done + 1)
                            for y in range(m):
                                mm = pe.transpose(K.ps[:, TR + y * P:TR + (y + 1) * P],
                                                  p0[:, i % 2, (a + y) * P:(a + y + 1) * P], K.c("ident"))
                            mm.then_inc(s["aT"], 1)
                        pe.wait_ge(s["aT_out"], h * ROUNDS[NT] + ROUNDS[i + 1] + 1)
                        pe.wait_ge(s["v_in"], h * 32 + 32)
                        pe.wait_ge(s["av_out"], h * NT + i + 1)
                        for y in range(n):
                            mm = pe.matmul(K.ps[:, AV:AV + P], aT[:, y * P:(y + 1) * P], v[:, k0 // P + y],
                                           start=(y == 0), stop=(y == n - 1))
                        mm.then_inc(s["av"], 1)

                    score(0)
                    for i in range(NT):
                        if i + 1 < NT:
                            score(i + 1)
                        turn_and_product(i)
                    if more:
                        turn_k(h + 1)
                    pe.wait_ge(s["normed"], h + 1)
                    for i in range(NT):
                        mm = pe.transpose(K.ps[:, i * P:(i + 1) * P], o[:, i], K.c("ident"))
                    mm.then_inc(s["o_turned"], 1)
                    if more:
                        pe.wait_ge(s["o_out"], h + 1)
                        turn_q(h + 1)
                over_heads(pe, head)

            @block.scalar
            def _(act):
                act.sem_inc(s["av_out"], 1)
                act.sem_inc(s["aT_out"], 1)
                act.wait_ge(s["lam_steps"], 4)
                act.activation(lam[0:1, 4:6], lam[0:1, 0:2], ACT.Exp).then_inc(s["lam_e"], 1)

                def copy_k(h):
                    act.wait_ge(s["k_turned"], h + 1)
                    act.copy(kT[:], K.ps[:, 3 * PIECE:3 * PIECE + NK * P]).then_inc(s["kT_out"], 1)

                def copy_q(h):
                    act.wait_ge(s["q_turned"], h + 1)
                    act.copy(qT[:], K.ps[:, 0:T]).then_inc(s["qT_out"], 1)
                copy_k(0)
                copy_q(0)

                def head(h, more):
                    def exp(i, j):
                        k0, n = keys_of(i)
                        act.wait_ge(s["bias"], h * 2 * NT + (2 * i + j + 1))
                        act.activation((p0, p1)[j][:, i % 2, 0:n * P].rearrange("p (c n) -> p c n", c=len(chunks(n))), scores_ps(j, n),
                                       ACT.Exp, bias=st[:, i % 2, 2 + j:3 + j], scale=SC,
                                       accum_out=st[:, i % 2, 4 + j:5 + j]).then_inc(s["expd"], 1)

                    exp(0, 0)
                    exp(0, 1)
                    for i in range(NT):
                        k0, n = keys_of(i)
                        for r, (a, m) in enumerate(rounds(n)):
                            act.wait_ge(s["aT"], h * ROUNDS[NT] + (ROUNDS[i] + r + 1))
                            if i > 0:
                                act.wait_ge(s["av"], h * NT + i)
                            act.copy(aT[:, a * P:(a + m) * P], K.ps[:, TR:TR + m * P]).then_inc(s["aT_out"], 1)
                            if i + 1 < NT and r < 2:
                                exp(i + 1, r)
                        act.wait_ge(s["av"], h * NT + (i + 1))
                        act.activation(sq[:], K.ps[:, AV:AV + P], ACT.Square, accum_out=rms[:, 0, i:i + 1])
                        act.copy(o[:, i], K.ps[:, AV:AV + P]).then_inc(s["av_out"], 1)
                    act.wait_ge(s["av_out"], h * NT + NT + 1)
                    act.activation(rms[:, 1], rms[:, 0], ACT.Sqrt, bias=K.eps[:], scale=1.0 / P).then_inc(s["root"], 1)
                    if more:
                        copy_k(h + 1)
                        copy_q(h + 1)
                over_heads(act, head)

            @block.vector
            def _(dve):
                one = Steps(dve, s["lam_steps"])
                one.did(dve.tensor_tensor(lam[0:1, 16:16 + DQK], K.lam_row[0:1, 0:DQK], K.lam_row[0:1, DQK:2 * DQK], ALU.mult))
                one.did(dve.tensor_tensor(lam[0:1, 96:96 + DQK], K.lam_row[0:1, 2 * DQK:3 * DQK], K.lam_row[0:1, 3 * DQK:4 * DQK], ALU.mult))
                one.wait()
                one.did(dve.tensor_reduce(lam[0:1, 0:1], lam[0:1, 16:16 + DQK], AX_X, ALU.add))
                one.did(dve.tensor_reduce(lam[0:1, 1:2], lam[0:1, 96:96 + DQK], AX_X, ALU.add))
                dve.wait_ge(s["lam_e"], 1)
                one.did(dve.tensor_tensor(lam[0:1, 6:7], lam[0:1, 5:6], lam[0:1, 4:5], ALU.subtract))
                one.wait()
                one.did(dve.tensor_scalar(lam[0:1, 8:9], lam[0:1, 6:7], -LAM_INIT, None, ALU.add))
                dve.wait_ge(s["lam_ps"], 1)
                one.did(dve.tensor_copy(nlam[:], K.ps[:, AV:AV + 1]))
                one.did(dve.tensor_scalar(gs[:], K.p("g_attn"), 1.0 - LAM_INIT, None, ALU.mult))
                one.wait()
                dve.wait_ge(s["rope_in"], 16)

                def rotate(which, h):
                    src, out, off, sem, per = ((q, qr, 0, s["q_in"], 16), (k, kr, 1, s["k_in"], 32))[which]
                    turn = Steps(dve, s["rope_steps"], h, 8)
                    turn.k = 4 * which
                    x = src[:, off:off + NS].rearrange("p t (j a f) -> p (t j) a f", j=2, a=2)
                    tp = tmp[:].rearrange("p t (j a f) -> p (t j) a f", j=2, a=2)
                    sn = rope[:, 1].rearrange("p t (j a f) -> p (t j) a f", j=2, a=2)
                    dve.wait_ge(sem, h * per + per)
                    turn.did(dve.tensor_tensor(out[:], src[:, off:off + NS], rope[:, 0], ALU.mult))
                    turn.did(dve.tensor_tensor(tp[:, :, 0], x[:, :, 1], sn[:, :, 0], ALU.mult))
                    turn.did(dve.tensor_tensor(tp[:, :, 1], x[:, :, 0], sn[:, :, 1], ALU.mult))
                    turn.wait()
                    turn.did(dve.tensor_tensor(out[:], out[:], tmp[:], ALU.add))
                    turn.wait()
                    dve.sem_inc(s["roped"], 1)
                rotate(0, 0)
                rotate(1, 0)

                def head(h, more):
                    step = Steps(dve, s["steps"], h, NT * PER_TILE + 2)

                    def softmax_bias(i):
                        k0, n = keys_of(i)
                        b = i % 2
                        for j in range(2):
                            dve.wait_ge(s["scored"], h * 2 * NT + (2 * i + j + 1))
                            axis = mybir.AxisListType.XY
                            step.did(dve.tensor_reduce(st[:, b, j:j + 1], scores_ps(j, n), axis, ALU.max))
                            step.wait()
                            dve.tensor_scalar(st[:, b, 2 + j:3 + j], st[:, b, j:j + 1], -SC, None, ALU.mult).then_inc(s["bias"], 1)

                    softmax_bias(0)
                    for i in range(NT):
                        b = i % 2
                        k0, n = keys_of(i)
                        dve.wait_ge(s["expd"], h * 2 * NT + 2 * (i + 1))
                        step.did(dve.reciprocal(st[:, b, 6:8], st[:, b, 4:6]))
                        step.wait()
                        step.did(dve.tensor_scalar(p0[:, b, 0:n * P], p0[:, b, 0:n * P], st[:, b, 6:7], None, ALU.mult))
                        step.did(dve.tensor_tensor(st[:, b, 7:8], st[:, b, 7:8], nlam[:], ALU.mult))
                        step.wait()
                        step.did(dve.scalar_tensor_tensor(p0[:, b, 0:n * P], p1[:, b, 0:n * P], st[:, b, 7:8], p0[:, b, 0:n * P],
                                                          ALU.mult, ALU.add))
                        step.wait()
                        dve.sem_inc(s["mixed"], 1)
                        if i + 1 < NT:
                            softmax_bias(i + 1)
                        if more and i in (3, 5):
                            rotate(i // 4, h + 1)
                    dve.wait_ge(s["root"], h + 1)
                    step.did(dve.reciprocal(rms[:, 2], rms[:, 1]))
                    step.wait()
                    step.did(dve.tensor_tensor(o, o, rms[:, 2].unsqueeze(2).to_broadcast([P, NT, P]), ALU.mult))
                    step.wait()
                    step.close()
                    dve.sem_inc(s["normed"], 1)
                    dve.wait_ge(s["o_turned"], h + 1)
                    dve.tensor_scalar(K.hT[:, bass.ds(h, 1), :].rearrange("p a t -> p (a t)"), K.ps[:, 0:T],
                                      gs[:, bass.ds(h, 1)], None, ALU.mult).then_inc(s["o_out"], 1)
                over_heads(dve, head)


def stage_gates(K):
    nc, d = K.nc, K.d
    with ExitStack() as ctx:
        def sb(name, shape):
            return ctx.enter_context(nc.sbuf_tensor(f"gate_{name}", shape, F32))
        s = K.sems("gate", "rows_in", "par_in", "steps", "abs", "exped", "log", "em", "rows_ready", "rows_out", "small", "small_out",
                   "wold", "turned", "cols", "m_out")
        g = sb("in", [4, 4, T])
        li, x = g[:, 0:2], g[:, 2:4]
        a, b, m = sb("a", [4, 2, T]), sb("b", [4, 2, T]), sb("m", [4, 2, T])
        resets = sb("resets", [4, 2, T])
        bias = sb("bias", [4, 3, 2])
        sm = sb("small", [4, 2, 2, NT])
        e = sb("end", [4, 3, 2, NT])

        def ends(t, r):
            return t[:, r].rearrange("h (c p) -> h c p", p=P)[:, :, (P - 1) if r == 0 else 0]

        def along(t, r, lo, hi):
            if r == 0:
                return t[:, 0, lo:hi]
            return t[:, 1, lo:hi][:, ::-1]

        with nc.Block() as block:
            @block.sync
            def _(sp):
                sp.dma_start(g[:], K.gate_rows.rearrange("k h t -> h k t")).then_inc(s["rows_in"], 16)
                sp.dma_start(resets[:], d["resets"]).then_inc(s["rows_in"], 16)
                with nc.allow_non_contiguous_dma("a few words"):
                    sp.dma_start(bias[:, 0], d["b_ig_ab"][0].rearrange("r h -> h r")).then_inc(s["par_in"], 16)
                    sp.dma_start(bias[:, 1], d["b_fg_ab"][0].rearrange("r h -> h r")).then_inc(s["par_in"], 16)
                    sp.dma_start(bias[:, 2], d["state_mlstm_m"][0, 0].rearrange("r h -> h r")).then_inc(s["par_in"], 16)
                    sp.wait_ge(s["rows_ready"], 1)
                    sp.dma_start(K.mrows[0].rearrange("r h t -> h r t"), x).then_inc(s["rows_out"], 16)
                    sp.wait_ge(s["em"], 1)
                    sp.dma_start(K.mrows[1].rearrange("r h t -> h r t"), a[:]).then_inc(s["rows_out"], 16)
                    sp.wait_ge(s["wold"], 1)
                    sp.dma_start(K.msmall.rearrange("k r h c -> h k r c"), sm[:]).then_inc(s["small_out"], 16)
                    sp.dma_start(d["o_new_m"][0, 0].rearrange("r h -> h r"), e[:, 1, :, NS]).then_inc(s["m_out"], 16)
                sp.wait_ge(s["rows_out"], 32)
                sp.wait_ge(s["small_out"], 16)
                sp.wait_ge(s["m_out"], 16)

            @block.scalar
            def _(act):
                act.wait_ge(s["abs"], 1)
                act.activation(a[:], a[:], ACT.Exp, scale=-1.0).then_inc(s["exped"], 1)
                act.wait_ge(s["exped"], 1)
                act.activation(a[:], a[:], ACT.Ln, bias=1.0).then_inc(s["log"], 1)
                act.wait_ge(s["rows_ready"], 1)
                act.activation(a[:], m[:], ACT.Exp, scale=-1.0).then_inc(s["em"], 1)
                act.wait_ge(s["small"], 1)
                act.activation(sm[:, 1], sm[:, 1], ACT.Exp).then_inc(s["wold"], 1)
                act.wait_ge(s["turned"], 1)
                act.activation(K.w_state[:], K.ps[:, PIECE:PIECE + 72].rearrange("p (r c h) -> p r c h", r=2, c=NT),
                               ACT.Exp).then_inc(s["cols"], 1)

            @block.tensor
            def _(pe):
                pe.wait_ge(s["small"], 1)
                for kind, src in ((0, b), (1, m)):
                    for r in range(2):
                        for c in range(NT):
                            at = kind * PIECE + (r * NT + c) * 4
                            mm = pe.transpose(K.ps[:, at:at + 4], src[:, r, c * P:(c + 1) * P], K.cst[0:4, 0:4])
                mm.then_inc(s["turned"], 1)

            @block.vector
            def _(dve):
                step = Steps(dve, s["steps"])
                dve.wait_ge(s["rows_in"], 32)
                dve.wait_ge(s["par_in"], 48)
                for r in range(2):
                    step.did(dve.tensor_scalar(li[:, r], li[:, r], bias[:, 0, r:r + 1], None, ALU.add))
                    step.did(dve.tensor_scalar(x[:, r], x[:, r], bias[:, 1, r:r + 1], None, ALU.add))
                step.wait()
                dve.scalar_tensor_tensor(a[:], x, -1.0, x, ALU.mult, ALU.max).then_inc(s["abs"], 1)
                dve.wait_ge(s["log"], 1)
                step.did(dve.scalar_tensor_tensor(x, x, 0.0, a[:], ALU.min, ALU.subtract))
                step.wait()
                for r in range(2):
                    step.did(dve.tensor_tensor_scan(along(b, r, 0, T), along(resets, r, 0, T), along(x, r, 0, T), 0.0,
                                                    ALU.mult, ALU.add))
                    step.did(dve.tensor_tensor_scan(along(m, r, 0, T_S), along(x, r, 0, T_S), along(li, r, 0, T_S),
                                                    bias[:, 2, r:r + 1], ALU.add, ALU.max))
                    step.did(dve.tensor_tensor_scan(along(m, r, T_S, T), along(x, r, T_S, T), along(li, r, T_S, T),
                                                    0.0, ALU.add, ALU.max))
                step.wait()
                step.did(dve.tensor_tensor(x, b[:], m[:], ALU.subtract))
                for r in range(2):
                    step.did(dve.tensor_copy(e[:, 0, r], ends(b, r)))
                    step.did(dve.tensor_copy(e[:, 1, r], ends(m, r)))
                step.did(dve.memset(sm[:, 0, :, NS:NT], 0.0))
                step.did(dve.tensor_copy(sm[:, 0, 0, 0:1], bias[:, 2, 0:1]))
                step.did(dve.tensor_copy(sm[:, 0, 1, NS - 1:NS], bias[:, 2, 1:2]))
                step.wait()
                step.did(dve.tensor_copy(sm[:, 0, 0, 1:NS], e[:, 1, 0, 0:NS - 1]))
                step.did(dve.tensor_copy(sm[:, 0, 1, 0:NS - 1], e[:, 1, 1, 1:NS]))
                step.did(dve.tensor_tensor(e[:, 2], e[:, 0], e[:, 1], ALU.subtract))
                step.wait()
                dve.sem_inc(s["rows_ready"], 1)
                step.did(dve.tensor_tensor(sm[:, 1], e[:, 2], sm[:, 0], ALU.add))
                step.did(dve.tensor_tensor(b[:], li, b[:], ALU.subtract))
                step.wait()
                dve.wait_ge(s["em"], 1)
                for r in range(2):
                    step.did(dve.tensor_tensor(m[:, r].rearrange("h (c p) -> h c p", p=P),
                                               b[:, r].rearrange("h (c p) -> h c p", p=P),
                                               e[:, 2, r].unsqueeze(2).to_broadcast([4, NT, P]), ALU.add))
                step.wait()
                dve.sem_inc(s["small"], 1)
                dve.wait_ge(s["turned"], 1)
                dve.tensor_copy(K.w_arg[:], K.ps[:, 0:72].rearrange("p (r c h) -> p r c h", r=2, c=NT)).then_inc(s["cols"], 1)


def stage_mlstm(K):
    nc, d = K.nc, K.d
    NSTATE = NS + 2
    with ExitStack() as ctx:
        def sb(name, shape):
            return ctx.enter_context(nc.sbuf_tensor(f"ml_{name}", shape, F32))
        s = K.sems("ml", "x_in", "v_in", "o_in", "row_in", "small_in", "st_in", "steps", "conv", "act_silu", "kscaled", "kT",
                   "k_used", "scT", "sc_out", "arg", "exped", "att", "kv", "upd", "num", "num_read", "C_out", "sq", "ssum",
                   "root", "sig", "done")
        qx, kx, ox = sb("qx", [P, T]), sb("kx", [P, T]), sb("ox", [P, T])
        v = sb("v", [P, NT, P + 1])
        qc, kc, sc = sb("qc", [P, T]), sb("kc", [P, T]), sb("sc", [P, T])
        ub, em = sb("ub", [P, T]), sb("em", [P, T])
        att, qw, hs, tmp = sb("att", [P, T]), sb("qw", [P, T]), sb("hs", [P, T]), sb("tmp", [P, T])
        small = sb("small", [P, 2, 2, NT])
        C = sb("C", [P, NSTATE, P + 1])
        kw = [qx, kx]
        chunk = lambda t: t.rearrange("p (c n) -> p c n", n=P)
        KV = [6 * PIECE, 7 * PIECE]
        N_DVE = 2 * 5 + 1 + 2 + (3 + 2 + 5) + (3 + 2 + 6) + 3

        def order(r):
            lat = range(NS) if r == 0 else range(NS - 1, -1, -1)
            return [(c, i, i + 1) for i, c in enumerate(lat)] + [(NS, None, NS + 1)]

        with nc.Block() as block:
            @block.gpsimd
            def _(pool):
                with pool.Fori(0, HEADS_B) as h:
                    pool.wait_ge(s["done"], h + 1)
                    pool.dma_start(qx[:], K.featT[bass.ds(h, 1)].rearrange("a p t -> (a p) t")).then_inc(s["x_in"], 16)
                    pool.dma_start(kx[:], K.featT[bass.ds(h + 4, 1)].rearrange("a p t -> (a p) t")).then_inc(s["x_in"], 16)
                    pool.dma_start(ox[:], K.featT[bass.ds(h + 8, 1)].rearrange("a p t -> (a p) t")).then_inc(s["o_in"], 16)
                    pool.dma_start(v[:, :, 0:P], K.tok.rearrange("n t p f -> n p t f")[3, :, :, bass.ds(h * P, P)]).then_inc(s["v_in"], 16)

            @block.sync
            def _(sp):
                sp.sem_inc(s["C_out"], 32)
                def row(kind, r, h):
                    return K.mrows[kind, r, bass.ds(h, 1), :].to_broadcast([P, T])
                with sp.Fori(0, HEADS_B) as h, nc.allow_non_contiguous_dma("a state's normaliser column"):
                    for r in range(2):
                        sp.wait_ge(s["num_read"], h * 2 + r + 1)
                        if r == 0:
                            sp.dma_start(small[:], K.msmall[:, :, bass.ds(h, 1), :].rearrange("k r a c -> a k r c")
                                         .to_broadcast([P, 2, 2, NT])).then_inc(s["small_in"], 16)
                        sp.dma_start(ub[:], row(0, r, h)).then_inc(s["row_in"], 16)
                        sp.dma_start(em[:], row(1, r, h)).then_inc(s["row_in"], 16)
                        sp.wait_ge(s["C_out"], (h * 2 + r) * 32 + 32)
                        sp.dma_start(C[:, 0, 0:P], d["state_mlstm_C"][0, 0, r, bass.ds(h, 1)].rearrange("a k v -> (a k) v")).then_inc(s["st_in"], 16)
                        sp.dma_start(C[:, 0, P:P + 1], d["state_mlstm_n"][0, 0, r, bass.ds(h, 1)].rearrange("a k -> k a")).then_inc(s["st_in"], 16)
                        sp.wait_ge(s["upd"], (h * 2 + r + 1) * NT + 1)
                        sp.dma_start(d["o_new_C"][0, 0, r, bass.ds(h, 1)].rearrange("a k v -> (a k) v"), C[:, NS + 1, 0:P]).then_inc(s["C_out"], 16)
                        sp.dma_start(d["o_new_n"][0, 0, r, bass.ds(h, 1)].rearrange("a k -> k a"), C[:, NS + 1, P:P + 1]).then_inc(s["C_out"], 16)
                sp.wait_ge(s["C_out"], 32 * 2 * HEADS_B + 32)

            @block.scalar
            def _(act):
                act.sem_inc(s["root"], 1)
                with act.Fori(0, HEADS_B) as h:
                    for j, t in enumerate((qc, kc)):
                        act.wait_ge(s["conv"], h * 2 + j + 1)
                        act.activation(t[:], t[:], ACT.Silu).then_inc(s["act_silu"], 1)
                    act.wait_ge(s["o_in"], h * 16 + 16)
                    act.activation(ox[:], ox[:], ACT.Sigmoid).then_inc(s["sig"], 1)
                    act.wait_ge(s["scT"], h + 1)
                    act.copy(sc[:], K.ps[:, 3 * PIECE:3 * PIECE + T]).then_inc(s["sc_out"], 1)
                    for r in range(2):
                        for j, t in enumerate((att, qw)):
                            act.wait_ge(s["arg"], h * 4 + (2 * r + j + 1))
                            act.activation(t[:], t[:], ACT.Exp).then_inc(s["exped"], 1)
                    act.wait_ge(s["num_read"], h * 2 + 2 + 1)
                    act.activation(att[:], hs[:], ACT.Square).then_inc(s["sq"], 1)
                    act.wait_ge(s["ssum"], h + 1)
                    act.activation(chunk(tmp[:]), chunk(K.ps[:, 0:T]), ACT.Sqrt, bias=K.eps[:], scale=1.0 / P).then_inc(s["root"], 1)

            @block.tensor
            def _(pe):
                pe.sem_inc(s["num"], 1)
                with pe.Fori(0, HEADS_B) as h:
                    pe.wait_ge(s["kscaled"], h + 1)
                    pe.wait_ge(s["root"], h + 1)
                    for c in range(NT):
                        mm = pe.transpose(K.ps[:, c * P:(c + 1) * P], kc[:, c * P:(c + 1) * P], K.c("ident"))
                    mm.then_inc(s["kT"], 1)
                    for c in range(NT):
                        mm = pe.matmul(K.ps[:, 3 * PIECE + c * P:3 * PIECE + (c + 1) * P], kc[:, c * P:(c + 1) * P],
                                       qc[:, c * P:(c + 1) * P], start=True, stop=True)
                    mm.then_inc(s["scT"], 1)
                    pe.wait_ge(s["v_in"], h * 16 + 16)
                    pe.wait_ge(s["k_used"], h + 1)
                    pe.wait_ge(s["sc_out"], h + 1)
                    for r in range(2):
                        base = (h * 2 + r) * NT
                        for n, (c, before, after) in enumerate(order(r)):
                            if n >= 2:
                                pe.wait_ge(s["upd"], base + n - 1 + 1)
                            elif r == 1:
                                pe.wait_ge(s["upd"], base + 1)
                            else:
                                pe.wait_ge(s["upd"], base + 1)
                            pe.matmul(K.ps[:, KV[n % 2]:KV[n % 2] + P + 1], kw[r][:, c * P:(c + 1) * P], v[:, c, :],
                                      start=True, stop=True).then_inc(s["kv"], 1)
                        pe.wait_ge(s["att"], h * 2 + r + 1)
                        pe.wait_ge(s["upd"], base + NT + 1)
                        if r == 1:
                            pe.wait_ge(s["num_read"], h * 2 + 1 + 1)
                        for c, before, after in sorted(order(r)):
                            num, den = K.ps[:, c * P:(c + 1) * P], K.ps[:, 3 * PIECE + c * P:3 * PIECE + (c + 1) * P]
                            cc = slice(c * P, (c + 1) * P)
                            first = before is None
                            if not first:
                                pe.matmul(num, C[:, before, 0:P], qw[:, cc], start=True, stop=False)
                            pe.matmul(num, v[:, c, 0:P], att[:, cc], start=first, stop=True)
                            if not first:
                                pe.matmul(den, C[:, before, P:P + 1].to_broadcast([P, P]), qw[:, cc], start=True, stop=False)
                            mm = pe.matmul(den, K.c("ones"), att[:, cc], start=first, stop=True)
                        mm.then_inc(s["num"], 1)
                    pe.wait_ge(s["sq"], h + 1)
                    for c in range(3):
                        w = min(PIECE, T - c * PIECE)
                        mm = pe.matmul(K.ps[:, c * PIECE:c * PIECE + w], K.c("ones"), att[:, c * PIECE:c * PIECE + w], start=True, stop=True)
                    mm.then_inc(s["ssum"], 1)

            @block.vector
            def _(dve):
                dve.sem_inc(s["upd"], 1)
                dve.sem_inc(s["num_read"], 1)
                dve.sem_inc(s["done"], 1)
                dve.memset(v[:, :, P:P + 1], 1.0).then_inc(s["steps"], 1)
                conv_at = PARAMS["conv"][0]
                with dve.Fori(0, HEADS_B) as h:
                    step = Steps(dve, s["steps"], h, N_DVE)
                    step.base = step.base + 1
                    dve.wait_ge(s["x_in"], h * 32 + 32)
                    for j, (x, y) in enumerate(((qx, qc), (kx, kc))):
                        def w(i):
                            return K.par[:, bass.ds(h + (conv_at + i * 8 + j * 4), 1)]
                        step.did(dve.tensor_scalar(y[:], x[:], w(1), None, ALU.mult))
                        step.wait()
                        for lo, hi in ((0, T_S), (T_S, T)):
                            step.did(dve.scalar_tensor_tensor(y[:, lo + 1:hi], x[:, lo:hi - 1], w(0), y[:, lo + 1:hi], ALU.mult, ALU.add))
                        step.wait()
                        for lo, hi in ((0, T_S), (T_S, T)):
                            step.did(dve.scalar_tensor_tensor(y[:, lo:hi - 1], x[:, lo + 1:hi], w(2), y[:, lo:hi - 1], ALU.mult, ALU.add))
                        step.wait()
                        dve.sem_inc(s["conv"], 1)
                    dve.wait_ge(s["act_silu"], h * 2 + 2)
                    step.did(dve.tensor_scalar(kc[:], kc[:], float(P) ** -0.5, None, ALU.mult))
                    step.wait()
                    dve.sem_inc(s["kscaled"], 1)
                    dve.wait_ge(s["kT"], h + 1)
                    for r in range(2):
                        step.did(dve.tensor_tensor(chunk(kw[r][:]), chunk(K.ps[:, 0:T]),
                                                   K.w_state[:, r, :, bass.ds(h, 1)].to_broadcast([P, NT, P]), ALU.mult))
                    step.wait()
                    dve.sem_inc(s["k_used"], 1)
                    for r in range(2):
                        n_dir = h * 2 + r
                        neg = K.c("neg_fwd" if r == 0 else "neg_bwd").unsqueeze(1).to_broadcast([P, NT, P])
                        dve.wait_ge(s["row_in"], (n_dir + 1) * 32)
                        dve.wait_ge(s["small_in"], h * 16 + 16)
                        dve.wait_ge(s["num"], n_dir + 1)
                        step.did(dve.tensor_tensor(chunk(att[:]), chunk(ub[:]),
                                                   K.w_arg[:, r, :, bass.ds(h, 1)].to_broadcast([P, NT, P]), ALU.add))
                        step.wait()
                        step.did(dve.tensor_tensor(chunk(att[:]), chunk(att[:]), neg, ALU.min))
                        step.did(dve.tensor_tensor(chunk(qw[:]), chunk(ub[:]), small[:, 0, r].unsqueeze(2).to_broadcast([P, NT, P]), ALU.add))
                        step.wait()
                        dve.sem_inc(s["arg"], 2)
                        dve.wait_ge(s["st_in"], (n_dir + 1) * 32)
                        for n, (c, before, after) in enumerate(order(r)):
                            dve.wait_ge(s["kv"], n_dir * NT + n + 1)
                            kv = K.ps[:, KV[n % 2]:KV[n % 2] + P + 1]
                            if before is None:
                                ins = dve.tensor_copy(C[:, after], kv)
                            else:
                                ins = dve.scalar_tensor_tensor(C[:, after], C[:, before], small[:, 1, r, c:c + 1], kv, ALU.mult, ALU.add)
                            ins.then_inc(s["upd"], 1)
                            dve.wait_ge(s["upd"], n_dir * NT + n + 1 + 1)
                            pass
                        dve.wait_ge(s["exped"], n_dir * 2 + 2)
                        dve.wait_ge(s["sc_out"], h + 1)
                        step.did(dve.tensor_tensor(att[:], att[:], sc[:], ALU.mult))
                        step.did(dve.tensor_tensor(qw[:], qw[:], qc[:], ALU.mult))
                        step.wait()
                        dve.sem_inc(s["att"], 1)
                        dve.wait_ge(s["num"], n_dir + 1 + 1)
                        den = K.ps[:, 3 * PIECE:3 * PIECE + T]
                        step.did(dve.tensor_copy(tmp[:], den))
                        step.wait()
                        step.did(dve.scalar_tensor_tensor(tmp[:], tmp[:], -1.0, tmp[:], ALU.mult, ALU.max))
                        step.wait()
                        step.did(dve.tensor_tensor(tmp[:], tmp[:], em[:], ALU.max))
                        step.wait()
                        step.did(dve.reciprocal(tmp[:], tmp[:]))
                        step.wait()
                        if r == 0:
                            step.did(dve.tensor_tensor(hs[:], K.ps[:, 0:T], tmp[:], ALU.mult))
                            step.wait()
                        else:
                            step.did(dve.tensor_tensor(tmp[:], K.ps[:, 0:T], tmp[:], ALU.mult))
                            step.wait()
                            step.did(dve.tensor_tensor(hs[:], hs[:], tmp[:], ALU.add))
                            step.wait()
                        dve.sem_inc(s["num_read"], 1)
                    dve.wait_ge(s["root"], h + 1 + 1)
                    step.did(dve.reciprocal(tmp[:], tmp[:]))
                    step.wait()
                    step.did(dve.scalar_tensor_tensor(hs[:], hs[:], K.par[:, bass.ds(h + PARAMS["g_mlstm"][0], 1)], tmp[:], ALU.mult, ALU.mult))
                    step.wait()
                    dve.wait_ge(s["sig"], h + 1)
                    step.did(dve.tensor_tensor(K.hT[:, bass.ds(h + 4, 1), :].rearrange("p a t -> p (a t)"), hs[:], ox[:], ALU.mult))
                    step.wait()
                    dve.sem_inc(s["done"], 1)
                    step.close()


def stage_out(K, l):
    nc = K.nc
    at = AT_OUT[l]
    with ExitStack() as ctx:
        def sb(name, shape):
            return ctx.enter_context(nc.sbuf_tensor(f"out{l}_{name}", shape, F32))
        s = K.sems(f"out{l}", "x_in0", "x_in1", "gate_in", "product", "gated", "x_new", "x_stored0", "x_stored1", "sumsq",
                   "root", "rcp", "xn_ready", "turned", "act_evac", "dve_evac", "xn_stored0", "xn_stored1")
        x_in, x_stored, xn_stored = [s["x_in0"], s["x_in1"]], [s["x_stored0"], s["x_stored1"]], [s["xn_stored0"], s["xn_stored1"]]
        xt, xn = sb("x", [P, 2, D]), sb("xn", [P, 2, D])
        tmp, junk = sb("tmp", [P, 2, D]), sb("junk", [P, D])
        gate = sb("gate", [P, STREAMS, D])
        st = sb("stat", [P, 2, 4])
        TURN = 4 * PIECE
        shift_at = l * 48 + 3 * KT
        with nc.Block() as block:
            @block.gpsimd
            def _(pool):
                for r in range(STREAMS):
                    pool.dma_start(gate[:, r], K.gate1_rows[l, r:r + 1].to_broadcast([P, D])).then_inc(s["gate_in"], 16)

                def body(tiles, r):
                    for t, b, u in tiles:
                        pool.wait_ge(s["xn_ready"], t + 1)
                        pool.wait_ge(x_stored[b], u * 16 + 16)
                        pool.dma_start(xt[:, b], K.xres[bass.ds(t * P, P), :]).then_inc(x_in[b], 16)
                over_tiles(pool, body)

            @block.sync
            def _(sp):
                def body(tiles, r):
                    for t, b, u in tiles:
                        sp.wait_ge(s["x_new"], t + 1)
                        sp.dma_start(K.xres[bass.ds(t * P, P), :], xt[:, b]).then_inc(x_stored[b], 16)
                    for t, b, u in tiles:
                        sp.wait_ge(s["xn_ready"], t + 3)
                        sp.dma_start(K.xnorm[bass.ds(t * P, P), :], xn[:, b]).then_inc(xn_stored[b], 16)
                for sem in x_stored + xn_stored:
                    sp.sem_inc(sem, 16)
                if l == 1:
                    for i in range(SLOTS - 2):
                        load_piece(K, sp, AT_EXPERTS[1] + i)
                over_tiles(sp, body)
                for i in range(2):
                    load_piece(K, sp, at + SLOTS + i)
                for sems in (x_stored, xn_stored):
                    sp.wait_ge(sems[0], 16 + 16 * 5)
                    sp.wait_ge(sems[1], 16 + 16 * 4)

            @block.scalar
            def _(act):
                def body(tiles, r):
                    for t, b, u in tiles:
                        act.wait_ge(s["x_new"], t + 1)
                        act.activation(junk[:], xt[:, b], ACT.Square, accum_out=st[:, b, 0:1]).then_inc(s["sumsq"], 1)
                        act.wait_ge(s["sumsq"], t + 1)
                        act.activation(st[:, b, 1:2], st[:, b, 0:1], ACT.Sqrt, bias=K.eps[:], scale=1.0 / D).then_inc(s["root"], 1)
                    for t, b, u in tiles:
                        act.wait_ge(s["turned"], t + 3)
                        for k in range(KT // 2):
                            a = TURN + b * D + k * P
                            ins = act.activation(K.hT[:, k, bass.ds(t * P, P)], K.ps[:, a:a + P], ACT.Identity,
                                                 bias=K.ada[:, r, shift_at + k:shift_at + k + 1], scale=K.scale[:, l, 1, r, k:k + 1])
                        ins.then_inc(s["act_evac"], 1)
                act.sem_inc(s["act_evac"], 2)
                over_tiles(act, body)

            @block.tensor
            def _(pe):
                pe.sem_inc(s["turned"], 2)

                def product(t):
                    b = t % 2
                    pe.wait_ge(s["gated"], t + 1)
                    for c in range(2):
                        if t == 0:
                            wait_piece(K, pe, at + c)
                        for k in range(KT):
                            mm = pe.matmul(K.ps[:, b * D + c * PIECE:b * D + (c + 1) * PIECE], K.hT[:, k, t * P:(t + 1) * P],
                                           K.W[:, (at + c) % SLOTS, k], start=(k == 0), stop=(k == KT - 1))
                    mm.then_inc(s["product"], 1)

                def turn(t):
                    b = t % 2
                    pe.wait_ge(s["xn_ready"], t + 3)
                    pe.wait_ge(s["act_evac"], t + 1)
                    pe.wait_ge(s["dve_evac"], t + 1)
                    for k in range(KT):
                        a = TURN + b * D + k * P
                        mm = pe.transpose(K.ps[:, a:a + P], xn[:, b, k * P:(k + 1) * P], K.c("ident"))
                    mm.then_inc(s["turned"], 1)
                product(0)
                product(1)
                for t in range(NT):
                    if t + 2 < NT:
                        product(t + 2)
                    if t + 2 == NT:
                        pe.drain().then_inc(K.w_used, 2)
                    turn(t)

            @block.vector
            def _(dve):
                def body(tiles, r):
                    for t, b, u in tiles:
                        dve.wait_ge(s["product"], t + 1)
                        dve.tensor_tensor(tmp[:, b], K.ps[:, b * D:(b + 1) * D], gate[:, r], ALU.mult).then_inc(s["gated"], 1)
                        dve.wait_ge(s["gated"], t + 3)
                        dve.wait_ge(x_in[b], u * 16 + 16)
                        dve.tensor_tensor(xt[:, b], xt[:, b], tmp[:, b], ALU.add).then_inc(s["x_new"], 1)
                    for t, b, u in tiles:
                        dve.wait_ge(s["root"], t + 1)
                        dve.reciprocal(st[:, b, 2:3], st[:, b, 1:2]).then_inc(s["rcp"], 1)
                        dve.wait_ge(s["rcp"], t + 1)
                        dve.wait_ge(s["turned"], t + 1)
                        dve.wait_ge(xn_stored[b], u * 16 + 16)
                        dve.tensor_scalar(xn[:, b], xt[:, b], st[:, b, 2:3], None, ALU.mult).then_inc(s["xn_ready"], 1)
                    for t, b, u in tiles:
                        dve.wait_ge(s["turned"], t + 3)
                        for k in range(KT // 2, KT):
                            a = TURN + b * D + k * P
                            ins = dve.tensor_scalar(K.hT[:, k, bass.ds(t * P, P)], K.ps[:, a:a + P], K.scale[:, l, 1, r, k:k + 1],
                                                    K.ada[:, r, shift_at + k:shift_at + k + 1], ALU.mult, ALU.add)
                        ins.then_inc(s["dve_evac"], 1)
                dve.sem_inc(s["xn_ready"], 2)
                dve.sem_inc(s["dve_evac"], 2)
                dve.sem_inc(s["gated"], 2)
                dve.wait_ge(s["gate_in"], 32)
                over_tiles(dve, body)


def stage_route(K, l):
    nc = K.nc
    E = EXPERTS
    with ExitStack() as ctx:
        def sb(name, shape, dt=F32):
            return ctx.enter_context(nc.sbuf_tensor(f"route{l}_{name}", shape, dt))
        s = K.sems(f"route{l}", "logits", "steps", "less_max", "exped", "aff", "affT", "picked", "columns")
        e, st = sb("e", [P, NT, E]), sb("stat", [P, 3, NT])
        aff = sb("aff", [E, T])
        val, idx = sb("val", [E, CAP]), sb("idx", [E, CAP], U32)
        idxf = sb("idxf", [E, CAP])
        with nc.Block() as block:
            @block.tensor
            def _(pe):
                for t in range(NT):
                    for k in range(KT):
                        mm = pe.matmul(K.ps[:, t * E:(t + 1) * E], K.hT[:, k, t * P:(t + 1) * P], K.w_router[:, l, k],
                                       start=(k == 0), stop=(k == KT - 1))
                mm.then_inc(s["logits"], 1)
                pe.wait_ge(s["aff"], 1)
                for t in range(NT):
                    mm = pe.transpose(K.ps[0:E, PIECE + t * P:PIECE + (t + 1) * P], e[:, t], K.c("ident"))
                mm.then_inc(s["affT"], 1)
                pe.wait_ge(s["picked"], 1)
                idn = K.cst[0:E, 0:E]
                for n, src in enumerate((idxf, val)):
                    pe.transpose(K.ps[:, n * E:(n + 1) * E], src[:, 0:CAP_S], idn)
                    mm = pe.transpose(K.ps[0:CAP_P, 64 + n * E:64 + (n + 1) * E], src[:, CAP_S:CAP], idn)
                mm.then_inc(s["columns"], 1)

            @block.scalar
            def _(act):
                act.wait_ge(s["less_max"], 1)
                act.activation(e[:], e[:], ACT.Exp).then_inc(s["exped"], 1)

            @block.vector
            def _(dve):
                step = Steps(dve, s["steps"])
                logits = K.ps[:, 0:NT * E].rearrange("p (t e) -> p t e", e=E)

                def wide(i):
                    return st[:, i].unsqueeze(2).to_broadcast([P, NT, E])
                dve.wait_ge(s["logits"], 1)
                step.did(dve.tensor_reduce(st[:, 0], logits, AX_X, ALU.max))
                step.wait()
                dve.tensor_tensor(e[:], logits, wide(0), ALU.subtract).then_inc(s["less_max"], 1)
                dve.wait_ge(s["exped"], 1)
                step.did(dve.tensor_reduce(st[:, 1], e[:], AX_X, ALU.add))
                step.wait()
                step.did(dve.reciprocal(st[:, 2], st[:, 1]))
                step.wait()
                dve.tensor_tensor(e[:], e[:], wide(2), ALU.mult).then_inc(s["aff"], 1)
                dve.wait_ge(s["affT"], 1)
                step.did(dve.tensor_copy(aff[:], K.ps[0:E, PIECE:PIECE + T]))
                step.wait()
                for at, cap, lo, hi in ((0, CAP_S, 0, T_S), (CAP_S, CAP_P, T_S, T)):
                    for n in range(at, at + cap, 8):
                        step.did(dve.max(val[:, n:n + 8], aff[:, lo:hi]))
                        step.wait()
                        step.did(dve.max_index(idx[:, n:n + 8], val[:, n:n + 8], aff[:, lo:hi]))
                        step.wait()
                        if n + 8 < at + cap:
                            step.did(dve.match_replace(aff[:, lo:hi], val[:, n:n + 8], aff[:, lo:hi], -1.0))
                            step.wait()
                step.did(dve.tensor_copy(idxf[:, 0:CAP_S], idx[:, 0:CAP_S]))
                step.did(dve.tensor_scalar(idxf[:, CAP_S:CAP], idx[:, CAP_S:CAP], float(T_S), None, ALU.add))
                step.wait()
                dve.sem_inc(s["picked"], 1)
                dve.wait_ge(s["columns"], 1)
                step.did(dve.tensor_copy(K.idx_s[:], K.ps[:, 0:E]))
                step.did(dve.tensor_copy(K.gate_s[:], K.ps[:, E:2 * E]))
                step.did(dve.tensor_copy(K.idx_p[:], K.ps[0:CAP_P, 64:64 + E]))
                step.did(dve.tensor_copy(K.gate_p[:], K.ps[0:CAP_P, 64 + E:64 + 2 * E]))
                step.wait()


def stage_experts(K, l):
    nc = K.nc
    at = AT_EXPERTS[l]
    E = EXPERTS
    GU = [0, PIECE]
    DN = [2 * PIECE, 3 * PIECE]
    TR = 4 * PIECE
    with ExitStack() as ctx:
        def sb(name, shape, dt=F32):
            return ctx.enter_context(nc.sbuf_tensor(f"moe{l}_{name}", shape, dt))
        s = K.sems(f"moe{l}", "idx_g", "idx_s", "xs_in", "xp_in", "x_turned", "xT", "xT2", "gate", "up", "silu", "hid",
                   "down", "y_act", "y_dve", "y_turned", "ys_out", "yp_out", "ys_added", "yp_added", "added", "order")
        xs, xp = sb("xs", [CAP_S, D]), sb("xp", [CAP_P, D])
        xT, hid, yT = sb("xT", [P, KT, CAP]), sb("hid", [P, KT, CAP]), sb("yT", [P, KT, CAP])
        sg = sb("silu", [P, 2, CAP])
        ys, yp = sb("ys", [CAP_S, D]), sb("yp", [CAP_P, D])
        ig, ipg = sb("ig", [P, 1], I32), sb("ipg", [CAP_P, 1], I32)
        isc, ips = sb("is", [P, 1], I32), sb("ips", [CAP_P, 1], I32)
        shift_at, gate2_at = l * 48 + 3 * KT, l * 48 + 5 * KT

        def turned_x(k):
            return TR + (k // 3) * PIECE + (k % 3) * CAP

        def turn_x(pe, e):
            pe.wait_ge(s["xs_in"], e * 16 + 16)
            pe.wait_ge(s["xp_in"], e * 16 + 16)
            for k in range(KT):
                a = turned_x(k)
                pe.transpose(K.ps[:, a:a + CAP_S], xs[:, k * P:(k + 1) * P], K.c("ident"))
                mm = pe.transpose(K.ps[:, a + CAP_S:a + CAP], xp[:, k * P:(k + 1) * P], K.cst[0:CAP_P, 0:CAP_P])
            mm.then_inc(s["x_turned"], 1)

        def turn_y(pe, e):
            pe.wait_ge(s["y_act"], e * KT + KT)
            for k in range(KT):
                pe.transpose(K.ps[:, TR + k * P:TR + (k + 1) * P], yT[:, k, 0:CAP_S], K.c("ident"))
            for k in range(KT):
                mm = pe.transpose(K.ps[0:CAP_P, TR + D + k * P:TR + D + (k + 1) * P], yT[:, k, CAP_S:CAP], K.c("ident"))
            mm.then_inc(s["y_turned"], 1)

        def experts(eng, body):
            body(0, False, True)
            with eng.Fori(1, E - 1) as e:
                body(e, True, True)
            body(E - 1, True, False)

        with nc.Block() as block:
            @block.sync
            def _(sp):
                def used(i, e):
                    if i < 4:
                        sp.wait_ge(s["up"], e * KT + 4 * (i // 2 + 1))
                    else:
                        sp.wait_ge(s["down"], e * KT + 4 * (i - 3))
                with sp.Fori(0, E - 1) as e:
                    for i in range(SLOTS):
                        used(i, e)
                        w = (K.d["w_gate_e"], K.d["w_up_e"], K.d["w_gate_e"], K.d["w_up_e"], K.d["w_down_e"], K.d["w_down_e"])[i]
                        c = (0, 0, 1, 1, 0, 1)[i]
                        src = w[l, bass.ds(e + 1, 1)].rearrange("a (k p) f -> p (a k) f", p=P)[:, :, c * PIECE:(c + 1) * PIECE]
                        sp.dma_start(K.W[:, (at + i) % SLOTS], src).then_inc(K.w_loaded[(at + i) % SLOTS], 16)
                for i in range(SLOTS):
                    n = at + E * SLOTS + i
                    if n < len(K.pieces):
                        used(i, E - 1)
                        sp.dma_start(K.W[:, n % SLOTS], K.pieces[n]).then_inc(K.w_loaded[n % SLOTS], 16)

            @block.gpsimd
            def _(pool):
                pool.sem_inc(s["added"], 1)

                def gather(e):
                    pool.tensor_copy(ig[:], K.idx_s[:, bass.ds(e, 1)]).then_inc(s["idx_g"], 1)
                    pool.tensor_copy(ipg[:], K.idx_p[:, bass.ds(e, 1)]).then_inc(s["idx_g"], 1)
                    pool.wait_ge(s["idx_g"], e * 2 + 2)
                    pool.sem_inc(s["order"], 1)
                    pool.indirect_dma_start(xs[:], None, K.xnorm, bass.IndirectOffsetOnAxis(ig[:, 0:1], 0)).then_inc(s["xs_in"], 16)
                    pool.indirect_dma_start(xp[:], None, K.xnorm, bass.IndirectOffsetOnAxis(ipg[:, 0:1], 0)).then_inc(s["xp_in"], 16)

                def add(e):
                    pool.tensor_copy(isc[:], K.idx_s[:, bass.ds(e, 1)]).then_inc(s["idx_s"], 1)
                    pool.tensor_copy(ips[:], K.idx_p[:, bass.ds(e, 1)]).then_inc(s["idx_s"], 1)
                    pool.wait_ge(s["idx_s"], e * 2 + 2)
                    pool.wait_ge(s["ys_out"], e + 1 + 1)
                    pool.sem_inc(s["order"], 1)
                    pool.indirect_dma_start(K.xres, bass.IndirectOffsetOnAxis(isc[:, 0:1], 0), ys[:], None,
                                            compute_op=ALU.add).then_inc(s["ys_added"], 16)
                    pool.wait_ge(s["yp_out"], e + 1 + 1)
                    pool.sem_inc(s["order"], 1)
                    pool.indirect_dma_start(K.xres, bass.IndirectOffsetOnAxis(ips[:, 0:1], 0), yp[:], None,
                                            compute_op=ALU.add).then_inc(s["yp_added"], 16)
                    pool.wait_ge(s["ys_added"], e * 16 + 16)
                    pool.wait_ge(s["yp_added"], e * 16 + 16)
                    pool.sem_inc(s["added"], 1)

                def body(e, before, after):
                    if after:
                        pool.wait_ge(s["x_turned"], e + 1)
                        gather(e + 1)
                    if before:
                        add(e - 1)
                gather(0)
                experts(pool, body)
                add(E - 1)

            @block.tensor
            def _(pe):
                def column_tile(e, ft):
                    half, col = ft // 4, (ft % 4) * P
                    pe.wait_ge(s["hid"], e * KT + max(ft - 1, 0) + 1)
                    for j in range(2):
                        n = at + 2 * half + j
                        slot = n % SLOTS
                        if ft % 4 == 0:
                            pe.wait_ge(K.w_loaded[slot], e * 16 + 16 * (n // SLOTS + 1))
                        a = GU[ft % 2] + j * CAP
                        for k in range(KT):
                            mm = pe.matmul(K.ps[:, a:a + CAP], K.W[:, slot, k, col:col + P], xT[:, k, :],
                                           start=(k == 0), stop=(k == KT - 1))
                    mm.then_inc(s["up"], 1)

                def body(e, before, after):
                    pe.wait_ge(s["xT"], e + 1)
                    pe.wait_ge(s["xT2"], e + 1)
                    column_tile(e, 0)
                    if before:
                        turn_y(pe, e - 1)
                    for ft in range(1, KT):
                        column_tile(e, ft)
                    if after:
                        pe.wait_ge(s["ys_out"], e + 1)
                        pe.wait_ge(s["yp_out"], e + 1)
                        turn_x(pe, e + 1)
                    pe.wait_ge(s["hid"], e * KT + KT + 1)
                    for dt in range(KT):
                        n = at + 4 + dt // 4
                        slot, col = n % SLOTS, (dt % 4) * P
                        if dt % 4 == 0:
                            pe.wait_ge(K.w_loaded[slot], e * 16 + 16 * (n // SLOTS + 1))
                        if dt >= 2:
                            pe.wait_ge(s["y_act"], e * KT + dt - 1)
                        for k in range(KT):
                            mm = pe.matmul(K.ps[:, DN[dt % 2]:DN[dt % 2] + CAP], K.W[:, slot, k, col:col + P], hid[:, k, :],
                                           start=(k == 0), stop=(k == KT - 1))
                        mm.then_inc(s["down"], 1)
                turn_x(pe, 0)
                experts(pe, body)
                turn_y(pe, E - 1)
                pe.drain().then_inc(K.w_used, E * SLOTS)

            @block.scalar
            def _(act):
                act.sem_inc(s["ys_out"], 1)

                def modulate(e):
                    act.wait_ge(s["x_turned"], e + 1)
                    for k in range(3, 6):
                        for r, (lo, hi) in enumerate(((0, CAP_S), (CAP_S, CAP))):
                            a = turned_x(k)
                            ins = act.activation(xT[:, k, lo:hi], K.ps[:, a + lo:a + hi], ACT.Identity,
                                                 bias=K.ada[:, r, shift_at + k:shift_at + k + 1], scale=K.scale[:, l, 1, r, k:k + 1])
                    ins.then_inc(s["xT"], 1)

                def weighted(e):
                    act.wait_ge(s["y_turned"], e + 1)
                    act.wait_ge(s["added"], e + 1)
                    act.activation(ys[:], K.ps[:, TR:TR + D], ACT.Copy, scale=K.gate_s[:, bass.ds(e, 1)]).then_inc(s["ys_out"], 1)

                def body(e, before, after):
                    for ft in range(KT):
                        act.wait_ge(s["up"], e * KT + (ft + 1))
                        if ft >= 2:
                            act.wait_ge(s["hid"], e * KT + (ft - 1) + 1)
                        act.activation(sg[:, ft % 2], K.ps[:, GU[ft % 2]:GU[ft % 2] + CAP], ACT.Silu).then_inc(s["silu"], 1)
                        if ft == 1 and before:
                            weighted(e - 1)
                    if after:
                        modulate(e + 1)
                    for dt in range(KT):
                        act.wait_ge(s["down"], e * KT + (dt + 1))
                        for r, (lo, hi) in enumerate(((0, CAP_S), (CAP_S, CAP))):
                            ins = act.activation(yT[:, dt, lo:hi], K.ps[:, DN[dt % 2] + lo:DN[dt % 2] + hi], ACT.Copy,
                                                 scale=K.ada[:, r, gate2_at + dt:gate2_at + dt + 1])
                        ins.then_inc(s["y_act"], 1)
                modulate(0)
                experts(act, body)
                weighted(E - 1)

            @block.vector
            def _(dve):
                dve.sem_inc(s["hid"], 1)
                dve.sem_inc(s["yp_out"], 1)

                def modulate(e):
                    dve.wait_ge(s["x_turned"], e + 1)
                    for k in (0, 1, 2, 6, 7):
                        for r, (lo, hi) in enumerate(((0, CAP_S), (CAP_S, CAP))):
                            a = turned_x(k)
                            ins = dve.tensor_scalar(xT[:, k, lo:hi], K.ps[:, a + lo:a + hi], K.scale[:, l, 1, r, k:k + 1],
                                                    K.ada[:, r, shift_at + k:shift_at + k + 1], ALU.mult, ALU.add)
                    ins.then_inc(s["xT2"], 1)

                def weighted(e):
                    dve.wait_ge(s["y_turned"], e + 1)
                    dve.wait_ge(s["added"], e + 1)
                    dve.tensor_scalar(yp[:], K.ps[0:CAP_P, TR + D:TR + 2 * D], K.gate_p[:, bass.ds(e, 1)], None,
                                      ALU.mult).then_inc(s["yp_out"], 1)

                def body(e, before, after):
                    for ft in range(KT):
                        dve.wait_ge(s["silu"], e * KT + (ft + 1))
                        a = GU[ft % 2] + CAP
                        dve.tensor_tensor(hid[:, ft], sg[:, ft % 2], K.ps[:, a:a + CAP], ALU.mult).then_inc(s["hid"], 1)
                        if ft == 1 and before:
                            weighted(e - 1)
                    if after:
                        modulate(e + 1)
                modulate(0)
                experts(dve, body)
                weighted(E - 1)


def stage_final(K):
    nc, d = K.nc, K.d
    with ExitStack() as ctx:
        def sb(name, shape):
            return ctx.enter_context(nc.sbuf_tensor(f"fin_{name}", shape, F32))
        s = K.sems("fin", "x_in0", "x_in1", "g_in", "sumsq", "root", "rcp", "y", "stored0", "stored1")
        x_in, stored = [s["x_in0"], s["x_in1"]], [s["stored0"], s["stored1"]]
        xt, y, g = sb("x", [P, 2, D]), sb("y", [P, 2, D]), sb("g", [P, D])
        junk, st = sb("junk", [P, D]), sb("stat", [P, 2, 4])
        with nc.Block() as block:
            @block.gpsimd
            def _(pool):
                pool.dma_start(g[:], d["g_final"].unsqueeze(0).to_broadcast([P, D])).then_inc(s["g_in"], 16)

                def body(tiles, r):
                    for t, b, u in tiles:
                        pool.wait_ge(s["y"], t + 1)
                        pool.dma_start(xt[:, b], K.xres[bass.ds(t * P, P), :]).then_inc(x_in[b], 16)
                over_tiles(pool, body)

            @block.sync
            def _(sp):
                for sem in stored:
                    sp.sem_inc(sem, 16)

                def body(tiles, r):
                    for t, b, u in tiles:
                        sp.wait_ge(s["y"], t + 3)
                        dst = d["o_y_prompt"][0] if r else d["o_y_sample"][0, bass.ds(t * P, P), :]
                        sp.dma_start(dst, y[:, b]).then_inc(stored[b], 16)
                over_tiles(sp, body)
                sp.wait_ge(stored[0], 16 + 16 * 5)
                sp.wait_ge(stored[1], 16 + 16 * 4)

            @block.scalar
            def _(act):
                def body(tiles, r):
                    for t, b, u in tiles:
                        act.wait_ge(x_in[b], u * 16 + 16)
                        act.activation(junk[:], xt[:, b], ACT.Square, accum_out=st[:, b, 0:1]).then_inc(s["sumsq"], 1)
                        act.wait_ge(s["sumsq"], t + 1)
                        act.activation(st[:, b, 1:2], st[:, b, 0:1], ACT.Sqrt, bias=K.eps[:], scale=1.0 / D).then_inc(s["root"], 1)
                over_tiles(act, body)

            @block.vector
            def _(dve):
                dve.sem_inc(s["y"], 2)
                dve.wait_ge(s["g_in"], 16)

                def body(tiles, r):
                    for t, b, u in tiles:
                        dve.wait_ge(s["root"], t + 1)
                        dve.reciprocal(st[:, b, 2:3], st[:, b, 1:2]).then_inc(s["rcp"], 1)
                        dve.wait_ge(s["rcp"], t + 1)
                        dve.wait_ge(stored[b], u * 16 + 16)
                        dve.scalar_tensor_tensor(y[:, b], xt[:, b], st[:, b, 2:3], g[:], ALU.mult, ALU.mult).then_inc(s["y"], 1)
                over_tiles(dve, body)
def stage_hgrn(K):
    nc, d = K.nc, K.d
    NSTATE = NS + 2
    N_STATE_STEPS = 2 * NS + 1
    with ExitStack() as ctx:
        def sb(name, shape):
            return ctx.enter_context(nc.sbuf_tensor(f"hg_{name}", shape, F32))[:]
        s = K.sems("hg", "f_in", "q_in", "v_in", "g_in", "st_in", "bias", "lb", "sig", "scaled", "level", "asm", "k_next",
                   "q_next", "t_next", "merged", "kT", "ktok", "kv", "states", "S_out", "out_ctx", "out", "o_out", "sq",
                   "ssum", "root", "silu", "norm", "spread", "modulated", "done", "order")
        ring = K.W[:].rearrange("p s k c -> p (s k c)")
        SLOT = KT * PIECE
        assert [(AT_OUT[1] + i) % SLOTS for i in range(2)] == [1, 2]
        used = {"at": 3 * SLOT, "end": 6 * SLOT}

        def in_ring(n):
            if used["at"] + n > used["end"]:
                used["at"], used["end"] = 0, SLOT
            used["at"] += n
            assert used["at"] <= used["end"]
            return ring[:, used["at"] - n:used["at"]]

        def directions(t):
            return t.rearrange("p (r t) -> p r t", r=2)
        G = [sb("G", [P, 2, T]), directions(in_ring(2 * T))]
        Kx = [sb("K", [P, 2, T]), directions(in_ring(2 * T))]
        Qx = [sb("Q", [P, 2, T]), directions(in_ring(2 * T))]
        att = [in_ring(T), in_ring(T)]
        A = [sb("A", [P, T]), in_ring(T)]
        O, SQ = in_ring(T), in_ring(T)
        g, v = in_ring(T), in_ring(T).rearrange("p (c f) -> p c f", f=P)
        q = sb("q", [P, T])
        S = sb("S", [P, 2, NSTATE, P])
        lens = [T >> i for i in range(LEVELS + 1)]
        Tl = [None] + [sb(f"T{i}", [P, 2, lens[i]]) for i in range(1, LEVELS + 1)]
        lb = sb("lb", [P, 4, HEADS_C])
        nbf = sb("nbf", [P, 2 * HEADS_C])
        rms = sb("rms", [P, 2, NT])
        R = [0, 3 * PIECE]
        TAIL = 6 * PIECE
        bf_at = PARAMS["b_f"][0]
        FULL = NS * P

        def blocks(t, m, lo, n):
            return bass.AP(t.tensor, t.offset + lo, [list(t.ap[0]), [2 * m, n // (2 * m)], [T + m, 2], [1, m]])

        def factors(t, i, start, pair_step, j_step):
            m = 1 << i
            return bass.AP(t.tensor, t.offset + start, [list(t.ap[0]), [pair_step, T // (2 * m)], [j_step, 2], [0, m]])

        def cols(c):
            return slice(c * P, (c + 1) * P)

        def chunk_of(r, k):
            return k if r == 0 else NS - 1 - k

        def run(eng, levels, tail):
            levels(0, 0, 0, None, True)
            with eng.Fori(0, HEADS_C // 2 - 1) as i:
                levels(i * 2 + 1, i + 4, 1, tail(i * 2, i, 0), True)
                levels(i * 2 + 2, i + 1, 0, tail(i * 2 + 1, i + 4, 1), True)
            levels(HEADS_C - 1, HEADS_C - 1, 1, tail(HEADS_C - 2, 3, 0), False)
            last = tail(HEADS_C - 1, HEADS_C - 1, 1)
            for k in range(LEVELS):
                last(k)

        def next_head(n, h, b):
            return h + 4 if b == 0 else h - 3

        with nc.Block() as block:
            @block.gpsimd
            def _(pool):
                def load_f(h, b):
                    for r in range(2):
                        pool.dma_start(G[b][:, r], K.featT[bass.ds(h + (16 + 8 * r), 1)].rearrange("a p t -> (a p) t")).then_inc(s["f_in"], 16)

                def load_q(h):
                    pool.dma_start(q, K.featT[bass.ds(h, 1)].rearrange("a p t -> (a p) t")).then_inc(s["q_in"], 16)

                def levels(n, h, b, tail, more):
                    if more:
                        pool.wait_ge(s["level"], n * (LEVELS + 1) + 1)
                        pool.wait_ge(s["q_next"], n * (LEVELS + 1) + 1)
                        load_q(next_head(n, h, b))
                        if tail:
                            pool.wait_ge(s["kv"], n * 3)
                        load_f(next_head(n, h, b), 1 - b)
                    if tail:
                        pool.wait_ge(s["out"], n)
                    pool.dma_start(v, K.tok.rearrange("n t p f -> n p t f")[b, :, :, bass.ds((h - 4 * b) * P, P)]).then_inc(s["v_in"], 16)
                    if tail:
                        pool.wait_ge(s["done"], n + 1)
                    pool.dma_start(g, K.featT[bass.ds(h + 8, 1)].rearrange("a p t -> (a p) t")).then_inc(s["g_in"], 16)
                load_f(0, 0)
                load_q(0)
                run(pool, levels, lambda n, h, b: lambda k: None)

            @block.sync
            def _(sp):
                sp.sem_inc(s["S_out"], 32)

                def levels(n, h, b, tail, more):
                    if tail:
                        tail(2)
                        sp.wait_ge(s["out"], n)
                    for r in range(2):
                        sp.dma_start(S[:, r, 0], d["state_hgrn_S"][0, 0, r, bass.ds(h, 1)].rearrange("a k v -> (a k) v")).then_inc(s["st_in"], 16)

                def tail(n, h, b):
                    def one(k):
                        if k == 2:
                            sp.wait_ge(s["states"], n * N_STATE_STEPS + N_STATE_STEPS)
                            for r in range(2):
                                sp.dma_start(d["o_new_S"][0, 0, r, bass.ds(h, 1)].rearrange("a k v -> (a k) v"),
                                             S[:, r, NS + 1]).then_inc(s["S_out"], 16)
                    return one
                run(sp, levels, tail)
                sp.wait_ge(s["S_out"], 32 * HEADS_C + 32)

            @block.scalar
            def _(act):
                act.wait_ge(s["lb"], 1)
                act.activation(lb[:, 1], lb[:, 0], ACT.Sigmoid).then_inc(s["lb"], 1)
                act.wait_ge(s["lb"], 3)

                def prepare(n, h, b, r):
                    act.activation(Kx[b][:, r], G[b][:, r], ACT.Sigmoid, scale=-1.0, bias=nbf[:, bass.ds(h + 8 * r, 1)])
                    act.activation(G[b][:, r], G[b][:, r], ACT.Sigmoid, bias=K.par[:, bass.ds(h + (bf_at + 8 * r), 1)]).then_inc(s["sig"], 1)
                    act.wait_ge(s["sig"], n * 2 + (r + 1))
                    act.sem_inc(s["order"], 1)
                    act.activation(Kx[b][:, r], Kx[b][:, r], ACT.Identity, scale=lb[:, 2, bass.ds(h, 1)]).then_inc(s["scaled"], 1)
                    act.activation(G[b][:, r], G[b][:, r], ACT.Identity, scale=lb[:, 2, bass.ds(h, 1)],
                                   bias=lb[:, 1, bass.ds(h, 1)]).then_inc(s["scaled"], 1)

                def levels(n, h, b, tail, more):
                    for i in range(LEVELS):
                        if i:
                            act.wait_ge(s["k_next"], n * LEVELS + i)
                        else:
                            act.wait_ge(s["scaled"], n * 4 + 4)
                        if i > 1:
                            act.wait_ge(s["level"], n * (LEVELS + 1) + i)
                        elif tail:
                            act.wait_ge(s["level"], n * (LEVELS + 1))
                        act.copy(A[i % 2].rearrange("p (b j m) -> p b j m", j=2, m=1 << i), blocks(Kx[b], 1 << i, 0, T)).then_inc(s["asm"], 1)
                        if tail:
                            tail(i)
                        if more and i >= LEVELS - 2:
                            if i == LEVELS - 2:
                                act.wait_ge(s["f_in"], n * 32 + 64)
                                act.sem_inc(s["order"], 1)
                            prepare(n + 1, next_head(n, h, b), 1 - b, i - (LEVELS - 2))
                    for r in range(2):
                        act.wait_ge(s["kT"], n * 2 + r + 1)
                        act.copy(G[b][:, r], K.ps[:, R[r]:R[r] + T]).then_inc(s["ktok"], 1)

                def tail(n, h, b):
                    def one(k):
                        if k == 0:
                            act.wait_ge(s["g_in"], n * 16 + 16)
                            act.activation(g, g, ACT.Silu).then_inc(s["silu"], 1)
                        if k == 2:
                            act.wait_ge(s["out_ctx"], n + 1)
                            act.copy(O[:, FULL:], K.ps[:, TAIL + PIECE:TAIL + PIECE + P]).then_inc(s["o_out"], 1)
                        if k == 3:
                            act.wait_ge(s["out"], n + 1)
                            act.copy(O[:, 0:FULL], K.ps[:, TAIL:TAIL + FULL]).then_inc(s["o_out"], 1)
                            act.wait_ge(s["o_out"], n * 2 + 2)
                            act.activation(SQ, O, ACT.Square).then_inc(s["sq"], 1)
                        if k == 4:
                            act.wait_ge(s["ssum"], n + 1)
                            act.activation(rms[:, 0], K.ps[:, TAIL:TAIL + NT], ACT.Sqrt, bias=K.eps[:], scale=1.0 / P).then_inc(s["root"], 1)
                    return one
                act.wait_ge(s["bias"], 1)
                act.wait_ge(s["f_in"], 32)
                for r in range(2):
                    prepare(0, 0, 0, r)
                run(act, levels, tail)

            @block.tensor
            def _(pe):
                def levels(n, h, b, tail, more):
                    pe.wait_ge(s["scaled"], n * 4 + 4)
                    pe.wait_ge(s["q_in"], n * 16 + 16)
                    if tail:
                        pe.wait_ge(s["ktok"], n * 2 - 1)
                    for c in range(NT):
                        a = R[0] + c * P
                        pe.matmul(K.ps[:, a:a + P], Kx[b][:, 0, cols(c)], q[:, cols(c)], start=True, stop=False)
                        mm = pe.matmul(K.ps[:, a:a + P], Kx[b][:, 1, cols(c)], q[:, cols(c)], start=False, stop=True)
                    mm.then_inc(s["level"], 1)
                    for i in range(LEVELS):
                        pe.wait_ge(s["asm"], n * LEVELS + i + 1)
                        pe.wait_ge(s["q_next"], n * (LEVELS + 1) + i + 1)
                        if i:
                            pe.wait_ge(s["merged"], n * (LEVELS + 1) + i)
                        elif tail:
                            pe.wait_ge(s["ktok"], n * 2)
                        for c in range(NT):
                            a = R[(i + 1) % 2] + c * P
                            mm = pe.matmul(K.ps[:, a:a + P], A[i % 2][:, cols(c)], blocks(Qx[b], 1 << i, c * P, P),
                                           start=True, stop=True)
                        mm.then_inc(s["level"], 1)
                        if tail:
                            tail(i)
                    pe.wait_ge(s["k_next"], (n + 1) * LEVELS)
                    for r in range(2):
                        pe.wait_ge(s["merged"], n * (LEVELS + 1) + (LEVELS + r))
                        for c in range(NT):
                            mm = pe.transpose(K.ps[:, R[r] + c * P:R[r] + (c + 1) * P], Kx[b][:, r, cols(c)], K.c("ident"))
                        mm.then_inc(s["kT"], 1)

                def tail(n, h, b):
                    def bank(r, k):
                        a = TAIL + r * PIECE + k * P
                        return K.ps[:, a:a + P]

                    def one(k):
                        if k < 2:
                            if k == 0:
                                pe.wait_ge(s["ktok"], n * 2 + 2)
                                pe.wait_ge(s["v_in"], n * 16 + 16)
                                pe.wait_ge(s["done"], n + 1)
                            else:
                                pe.wait_ge(s["states"], n * N_STATE_STEPS + NS)
                            for r in range(2):
                                for j in range(NS // 2):
                                    c = chunk_of(r, k * NS // 2 + j)
                                    mm = pe.matmul(bank(r, j), G[b][:, r, cols(c)], v[:, c], start=True, stop=True)
                            mm.then_inc(s["kv"], 1)
                        if k == 2:
                            pe.wait_ge(s["states"], n * N_STATE_STEPS + 2 * NS)
                            for r in range(2):
                                mm = pe.matmul(bank(0, r), G[b][:, r, cols(NS)], v[:, NS], start=True, stop=True)
                            mm.then_inc(s["kv"], 1)
                            pe.wait_ge(s["merged"], (n + 1) * (LEVELS + 1))
                            pe.matmul(bank(1, 0), v[:, NS], att[b][:, cols(NS)], start=True, stop=True).then_inc(s["out_ctx"], 1)
                        if k == 3:
                            pe.wait_ge(s["states"], n * N_STATE_STEPS + N_STATE_STEPS)
                            pe.wait_ge(s["o_out"], n * 2 + 1)
                            pe.wait_ge(s["q_next"], (n + 1) * (LEVELS + 1))
                            for c in range(NS):
                                pe.matmul(bank(0, c), S[:, 0, c], Qx[b][:, 1, cols(c)], start=True, stop=False)
                                pe.matmul(bank(0, c), S[:, 1, NS - 1 - c], Qx[b][:, 0, cols(c)], start=False, stop=False)
                                mm = pe.matmul(bank(0, c), v[:, c], att[b][:, cols(c)], start=False, stop=True)
                            mm.then_inc(s["out"], 1)
                        if k == 4:
                            pe.wait_ge(s["sq"], n + 1)
                            for c in range(NT):
                                mm = pe.matmul(K.ps[:, TAIL + c:TAIL + c + 1], SQ[:, cols(c)], K.c("ones")[:, 0:1], start=True, stop=True)
                            mm.then_inc(s["ssum"], 1)
                        if k == 5:
                            pe.wait_ge(s["norm"], n * 3 + 3)
                            for c in range(2):
                                mm = pe.matmul(K.ps[:, TAIL + c * PIECE:TAIL + (c + 1) * PIECE], K.c("ones"),
                                               SQ[:, c * PIECE:(c + 1) * PIECE], start=True, stop=True)
                            mm.then_inc(s["spread"], 1)
                        if k == 6:
                            pe.wait_ge(s["modulated"], n + 1)
                            pe.matmul(bank(0, 0), K.c("ones"), SQ[:, FULL:], start=True, stop=True).then_inc(s["spread"], 1)
                    return one
                run(pe, levels, tail)

            @block.vector
            def _(dve):
                dve.sem_inc(s["done"], 1)
                gm = PARAMS["gamma"][0]
                dve.tensor_tensor(lb[:, 0], K.par[:, gm + 8:gm + 16], K.par[:, gm:gm + 8], ALU.subtract).then_inc(s["lb"], 1)
                dve.tensor_scalar(nbf, K.p("b_f"), -1.0, None, ALU.mult).then_inc(s["bias"], 1)
                dve.wait_ge(s["lb"], 2)
                dve.tensor_scalar(lb[:, 2], lb[:, 1], -1.0, 1.0, ALU.mult, ALU.add).then_inc(s["lb"], 1)
                ident = K.c("ident").unsqueeze(1).to_broadcast([P, NT, P])

                def chunked(t):
                    return t.rearrange("p (c n) -> p c n", n=P)

                def levels(n, h, b, tail, more):
                    dve.wait_ge(s["scaled"], n * 4 + 4)
                    dve.wait_ge(s["q_in"], n * 16 + 16)
                    dve.tensor_tensor(Qx[b][:, 1], q, G[b][:, 0], ALU.mult)
                    dve.tensor_tensor(Qx[b][:, 0], q, G[b][:, 1], ALU.mult).then_inc(s["q_next"], 1)
                    dve.wait_ge(s["level"], n * (LEVELS + 1) + 1)
                    dve.tensor_tensor(chunked(att[b]), chunked(K.ps[:, R[0]:R[0] + T]), ident, ALU.mult).then_inc(s["merged"], 1)
                    for i in range(LEVELS):
                        m, L = 1 << i, lens[i]
                        Ti = Tl[i] if i else G[b]
                        kb, qb = blocks(Kx[b], m, 0, T), blocks(Qx[b], m, 0, T)
                        dve.wait_ge(s["asm"], n * LEVELS + i + 1)
                        if i:
                            dve.wait_ge(s["k_next"], n * LEVELS + i)
                            dve.wait_ge(s["t_next"], n * LEVELS + i)
                        dve.tensor_tensor(kb, kb, factors(Ti, i, 1, 2, L - 1), ALU.mult).then_inc(s["k_next"], 1)
                        dve.wait_ge(s["level"], n * (LEVELS + 1) + (i + 2))
                        dve.wait_ge(s["q_next"], n * (LEVELS + 1) + i + 1)
                        dve.tensor_tensor(qb, qb, factors(Ti, i, L + 1, 2, -(L + 1)), ALU.mult).then_inc(s["q_next"], 1)
                        pair = Ti.rearrange("p r (n two) -> p r n two", two=2)
                        dve.wait_ge(s["merged"], n * (LEVELS + 1) + i + 1)
                        dve.tensor_tensor(Tl[i + 1], pair[:, :, :, 0], pair[:, :, :, 1], ALU.mult).then_inc(s["t_next"], 1)
                        region = chunked(K.ps[:, R[(i + 1) % 2]:R[(i + 1) % 2] + T])
                        mask = K.level_masks[:, i].unsqueeze(1).to_broadcast([P, NT, P])
                        dve.copy_predicated(chunked(att[b]), mask, region).then_inc(s["merged"], 1)
                        if tail:
                            tail(i)

                def tail(n, h, b):
                    step = Steps(dve, s["states"], n, N_STATE_STEPS)

                    def one(k):
                        if k < 2:
                            dve.wait_ge(s["kv"], n * 3 + k + 1)
                            if k == 0:
                                dve.wait_ge(s["st_in"], n * 32 + 32)
                                dve.wait_ge(s["t_next"], (n + 1) * LEVELS)
                            for j in range(NS // 2):
                                for r in range(2):
                                    i0 = k * NS // 2 + j
                                    c = chunk_of(r, i0)
                                    a = TAIL + r * PIECE + j * P
                                    if i0:
                                        dve.wait_ge(s["states"], n * N_STATE_STEPS + (step.k - 1))
                                    step.did(dve.scalar_tensor_tensor(S[:, r, i0 + 1], S[:, r, i0], last_T(r, c), K.ps[:, a:a + P],
                                                                      ALU.mult, ALU.add))
                        if k == 2:
                            dve.wait_ge(s["kv"], n * 3 + 3)
                            dve.wait_ge(s["S_out"], n * 32 + 32)
                            step.did(dve.tensor_copy(S[:, :, NS + 1], K.ps[:, TAIL:TAIL + 2 * P].rearrange("p (r v) -> p r v", r=2)))
                            step.close()
                        if k == 4:
                            dve.wait_ge(s["silu"], n + 1)
                            dve.wait_ge(s["sq"], n + 1)
                            dve.scalar_tensor_tensor(O, O, K.par[:, bass.ds(h + PARAMS["g_hgrn"][0], 1)], g,
                                                     ALU.mult, ALU.mult).then_inc(s["norm"], 1)
                            dve.wait_ge(s["root"], n + 1)
                            dve.reciprocal(rms[:, 1], rms[:, 0]).then_inc(s["norm"], 1)
                            dve.wait_ge(s["norm"], n * 3 + 2)
                            dve.tensor_tensor(chunked(SQ), ident, rms[:, 1].unsqueeze(2).to_broadcast([P, NT, P]), ALU.mult).then_inc(s["norm"], 1)
                        if k > 4:
                            lo, hi = (0, FULL) if k == 5 else (FULL, T)
                            dve.wait_ge(s["spread"], n * 2 + (k - 4))
                            dve.tensor_tensor(K.hT[:, bass.ds(h, 1), lo:hi].rearrange("p a t -> p (a t)"), O[:, lo:hi],
                                              K.ps[:, TAIL:TAIL + hi - lo], ALU.mult).then_inc(s["modulated"] if k == 5 else s["done"], 1)
                    return one

                def last_T(r, c):
                    return Tl[LEVELS][:, r, c:c + 1]
                run(dve, levels, tail)




def build(nc, d, stages=None):
    ctx = ExitStack()
    in_stage = []
    with ctx:
        def sb(name, shape, dt=F32):
            return ctx.enter_context(nc.sbuf_tensor(name, shape, dt))

        def dram(name, shape):
            return nc.dram_tensor(name, shape, F32).ap()

        def sems(stage, *names):
            held = {n: nc.alloc_semaphore(name=f"{stage}_{n}") for n in names}
            in_stage.extend(held.values())
            return held

        K = Shared(nc, d, ctx, sb, dram, sems)
        for n, stage in enumerate([
            lambda: stage_adaln(K),
            lambda: stage_norm(K, 0, 0, False),
            lambda: stage_project(K, "in_ab", AT_IN_AB, 3, 4, True),
            lambda: stage_attention(K),
            lambda: stage_gates(K),
            lambda: stage_mlstm(K),
            lambda: stage_out(K, 0),
            lambda: stage_route(K, 0),
            lambda: stage_experts(K, 0),
            lambda: stage_norm(K, 1, 0, False),
            lambda: stage_project(K, "in_c", AT_IN_C, 8, 2, False),
            lambda: stage_hgrn(K),
            lambda: stage_out(K, 1),
            lambda: stage_route(K, 1),
            lambda: stage_experts(K, 1),
            lambda: stage_final(K),
        ]):
            if stages is None or n < stages:
                stage()
                nc.clear_and_free_semaphores(list(in_stage))
                in_stage.clear()
                nc.all_engine_barrier()
        if stages is not None and stages < 99:
            total = K.loaded_after[stages]
            with nc.Block() as block:
                @block.sync
                def _(sp):
                    for i in range(SLOTS):
                        sp.wait_ge(K.w_loaded[i], 16 * len(range(i, total, SLOTS)))


_OUTS = [("y_prompt", (1, T_P, D)), ("y_sample", (1, T_S, D)),
         ("new_k", (1, 1, P, HEADS_A, 2 * DQK)), ("new_v", (1, 1, P, HEADS_A, P)),
         ("new_C", (1, 1, 2, HEADS_B, P, P)), ("new_n", (1, 1, 2, HEADS_B, P)), ("new_m", (1, 1, 2, HEADS_B)),
         ("new_S", (1, 1, 2, HEADS_C, P, P))]


def columns(v):
    return np.ascontiguousarray(v).reshape(-1, P).T


def shape_constants():
    c = np.zeros((P, N_CONSTS), np.float32)

    def put(name, a):
        c[:a.shape[0], CONSTS[name][0]:CONSTS[name][0] + CONSTS[name][1]] = a
    i, j = np.arange(P)[:, None], np.arange(P)[None, :]
    put("ident", np.eye(P))
    put("ones", np.ones((P, P)))
    put("neg_fwd", np.where(i <= j, 0.0, NEG))
    put("neg_bwd", np.where(i >= j, 0.0, NEG))
    n_freq = DQK // 4
    inv = np.power(np.float32(10000.0), -np.arange(n_freq, dtype=np.float32) / n_freq).astype(np.float32)
    t = np.arange(T_S)
    ang = np.concatenate([(t // GRID_W).astype(np.float32)[:, None] * inv,
                          (t % GRID_W).astype(np.float32)[:, None] * inv], axis=1).astype(np.float32)
    cos, sin = np.cos(ang), np.sin(ang)
    rope = np.stack([np.concatenate(x, 1).reshape(NS, P, P).transpose(1, 0, 2)
                     for x in ([cos] * 4, [-sin, sin] * 2)], 1)
    k = np.arange(T)
    resets = np.tile(np.stack([k % P != 0, k % P != P - 1]).astype(np.float32), (4, 1, 1))
    masks = np.stack([((i >> (m + 1)) == (j >> (m + 1))) & ((i >> m) != (j >> m)) for m in range(LEVELS)], 1)
    return c, masks.astype(np.uint32), np.ascontiguousarray(rope, np.float32), resets


_DIRECT = ["x_prompt", "x_sample", "cache_dattn_k", "cache_dattn_v", "state_mlstm_C", "state_mlstm_n",
           "state_mlstm_m", "state_hgrn_S", "w_ada", "g_final", "w_in_ab", "b_ig_ab", "b_fg_ab", "w_out_ab",
           "w_in_c", "w_out_c", "w_router", "w_gate_e", "w_up_e", "w_down_e"]


def laid_out(inputs):
    a = {n: np.ascontiguousarray(inputs[n]) for n in _DIRECT}
    a["params"] = np.concatenate([columns(np.asarray(inputs[n])) for n in (
        "c", "c_ctx", "b_ada", "g_norm", "g_attn_ab", "g_mlstm_ab", "conv_ab", "b_f_c", "gamma_lb", "g_hgrn_c")], axis=1)
    a["lam_ab"] = np.ascontiguousarray(inputs["lam_ab"]).reshape(1, -1)
    a["consts"], a["level_masks"], a["rope"], a["resets"] = shape_constants()
    return a


def declare(nc, arrays):
    d = {n: nc.dram_tensor(f"in_{n}", a.shape, mybir.dt.from_np(a.dtype), kind="ExternalInput").ap()
         for n, a in arrays.items()}
    d.update({f"o_{n}": nc.dram_tensor(f"out_{n}", shape, F32, kind="ExternalOutput").ap() for n, shape in _OUTS})
    return d


def kernel(**inputs):
    import concourse.bacc as _bacc
    from concourse.bass_utils import run_bass_kernel_spmd as _run

    nc = _bacc.Bacc("TRN2", target_bir_lowering=False, num_devices=1)
    arrays = laid_out(inputs)
    build(nc, declare(nc, arrays))
    r = _run(nc, [{f"in_{n}": a for n, a in arrays.items()}], core_ids=[0])
    return tuple(r.results[0][f"out_{n}"] for n, _ in _OUTS)
```

```python
from contextlib import ExitStack

import numpy as np
import concourse.bass as bass
from concourse import mybir

P = 128
D = 1024
KT = D // P
T_S, T_P = 1024, 128
T = T_S + T_P
NT = T // P
NS = T_S // P
STREAMS = 2
DEPTH = 2
HEADS_A = HEADS_B = 4
HEADS_C = 8
DQK = 64
GRID_W = 64
EXPERTS = 16
CAP_S, CAP_P = 2 * T_S // EXPERTS, 2 * T_P // EXPERTS
CAP = CAP_S + CAP_P
PIECE = 512
SLOTS = 6
EPS = 1e-6
LAM_INIT = float(0.8 - 0.6 * np.exp(-0.3 * 0))
NEG = -1e30
LEVELS = 7

F32 = mybir.dt.float32
U32 = mybir.dt.uint32
I32 = mybir.dt.int32
ALU = mybir.AluOpType
ACT = mybir.ActivationFunctionType
AX_X = mybir.AxisListType.X


def fields(sizes):
    out, at = {}, 0
    for name, n in sizes:
        out[name] = (at, n)
        at += n
    return out, at


PARAMS, N_PARAMS = fields([
    ("c", KT), ("c_ctx", KT), ("b_ada", DEPTH * 6 * KT), ("g_norm", DEPTH * 2 * KT),
    ("g_attn", 4), ("g_mlstm", 4), ("conv", 3 * 8), ("b_f", 16), ("gamma", 16), ("g_hgrn", 8)])
CONSTS, N_CONSTS = fields([
    ("ident", P), ("ones", P), ("neg_fwd", P), ("neg_bwd", P)])


def weight_pieces(d):
    def cols(w, c):
        return w.rearrange("(k p) f -> p k f", p=P)[:, :, c * PIECE:(c + 1) * PIECE]

    out = [cols(d["w_ada"][l], c) for l in range(DEPTH) for c in range(12)]
    out += [cols(d["w_in_ab"][0], c) for c in AB_FEATURE + AB_TOKEN]
    for l in range(DEPTH):
        if l == 1:
            out += [cols(d["w_in_c"][0], c) for c in C_FEATURE + C_TOKEN]
        w_out = d["w_out_ab"][0] if l == 0 else d["w_out_c"][0]
        out += [cols(w_out, c) for c in range(2)]
        for e in range(EXPERTS):
            out += [cols(w, c) for c in range(2) for w in (d["w_gate_e"][l, e], d["w_up_e"][l, e])]
            out += [cols(d["w_down_e"][l, e], c) for c in range(2)]
    return out


AB_FEATURE, AB_TOKEN = [3, 4, 6], [0, 1, 2, 5]
C_FEATURE, C_TOKEN = [0, 1, 4, 5, 6, 7, 8, 9], [2, 3]
N_ADA = 24
AT_IN_AB = N_ADA
AT_OUT = [AT_IN_AB + 7, AT_IN_AB + 7 + 2 + 6 * EXPERTS + 10]
AT_EXPERTS = [a + 2 for a in AT_OUT]
AT_IN_C = AT_EXPERTS[0] + 6 * EXPERTS


class Shared:

    def __init__(self, nc, d, ctx, sb, dram, sems):
        self.nc, self.d, self.sems = nc, d, sems
        self.W = sb("weights", [P, SLOTS, KT, PIECE])
        self.pieces = weight_pieces(d)
        self.w_used = ctx.enter_context(nc.semaphore("w_used"))
        self.w_loaded = [ctx.enter_context(nc.semaphore(f"w_loaded{i}")) for i in range(SLOTS)]
        self.loaded_after = [0, 30, 30, 33, 33, 33, 33, 39, 39, 135, 135, 141, 141, 147, 147, 237, 237]
        self.ps = ctx.enter_context(nc.psum_tensor("ps", [P, 8 * PIECE], F32))
        self.par, self.cst = sb("params_sb", [P, N_PARAMS]), sb("consts_sb", [P, N_CONSTS])
        self.eps = sb("eps", [P, 1])
        self.level_masks = sb("level_masks_sb", [P, LEVELS, P], U32)
        self.w_router = sb("w_router_sb", [P, DEPTH, KT, EXPERTS])
        self.lam_row = sb("lam_row", [1, 4 * DQK])
        self.hT = sb("hT", [P, KT, T])
        self.ada, self.scale = sb("ada", [P, STREAMS, DEPTH * 6 * KT]), sb("scale", [P, DEPTH, 2, STREAMS, KT])
        self.idx_s, self.gate_s = sb("idx_s", [P, EXPERTS], I32), sb("gate_s", [P, EXPERTS])
        self.idx_p, self.gate_p = sb("idx_p", [CAP_P, EXPERTS], I32), sb("gate_p", [CAP_P, EXPERTS])
        self.w_arg, self.w_state = sb("w_arg", [P, 2, NT, HEADS_B]), sb("w_state", [P, 2, NT, HEADS_B])
        self.em_cols = sb("em_cols", [P, 2, NT, HEADS_B])
        self.xres, self.xnorm = dram("x_residual", [T, D]), dram("x_norm", [T, D])
        self.gate1_rows = dram("gate1_rows", [DEPTH, STREAMS, D])
        self.featT, self.tok = dram("feature_rows", [32, P, T]), dram("token_rows", [4, NT, P, PIECE])
        self.gate_rows, self.mrows = dram("mlstm_gate_rows", [4, 4, T]), dram("mlstm_rows", [2, 4, T])
        self.msmall = dram("mlstm_chunks", [2, 2, 4, NT])

    def p(self, name):
        at, n = PARAMS[name]
        return self.par[:, at:at + n]

    def c(self, name):
        at, n = CONSTS[name]
        return self.cst[:, at:at + n]


class Steps:

    def __init__(self, eng, sem, turn=0, per=0):
        self.eng, self.sem, self.base, self.k, self.per = eng, sem, turn * per, 0, per

    def did(self, ins):
        ins.then_inc(self.sem, 1)
        self.k += 1

    def wait(self):
        self.eng.wait_ge(self.sem, self.base + self.k)

    def close(self):
        assert self.k == self.per, self.k


def load_piece(K, sp, n, src=None):
    if n >= SLOTS:
        sp.wait_ge(K.w_used, n - SLOTS + 1)
    sp.dma_start(K.W[:, n % SLOTS], K.pieces[n] if src is None else src).then_inc(K.w_loaded[n % SLOTS], 16)


def wait_piece(K, pe, n):
    pe.wait_ge(K.w_loaded[n % SLOTS], 16 * (n // SLOTS + 1))


def free_slots(K, at_out):
    ring = K.W[:].rearrange("p s k c -> p (s k c)")
    slot = KT * PIECE
    assert [(at_out + i) % SLOTS for i in range(2)] == [1, 2]
    used = {"at": 3 * slot, "end": 6 * slot}

    def take(n):
        if used["at"] + n > used["end"]:
            used["at"], used["end"] = 0, slot
        used["at"] += n
        assert used["at"] <= used["end"]
        return ring[:, used["at"] - n:used["at"]]
    return take


def stage_adaln(K):
    nc, d = K.nc, K.d
    with ExitStack() as ctx:
        s = K.sems("ada", "par", "silu", "added", "mod", "turned", "rows", "rows_out", "x_copied", "consts", "pack", "copied", "columns", "turning")
        condT = ctx.enter_context(nc.sbuf_tensor("condT", [P, KT, STREAMS], F32))
        cpack = ctx.enter_context(nc.sbuf_tensor("cpack", [P, KT, STREAMS], F32))
        row2 = ctx.enter_context(nc.sbuf_tensor("ada_rows", [STREAMS, 2, PIECE], F32))
        rows = ctx.enter_context(nc.sbuf_tensor("gate_rows", [KT, DEPTH * STREAMS * P], F32))
        with nc.Block() as block:
            @block.sync
            def _(sp):
                for n in range(SLOTS):
                    load_piece(K, sp, n)
                for n in range(SLOTS, N_ADA + SLOTS):
                    load_piece(K, sp, n)

            @block.gpsimd
            def _(pool):
                pool.dma_start(K.xres[0:T_S, :], d["x_sample"][0]).then_inc(s["x_copied"], 16)
                pool.dma_start(K.xres[T_S:T, :], d["x_prompt"][0]).then_inc(s["x_copied"], 16)
                pool.wait_ge(s["rows"], 1)
                for l in range(DEPTH):
                    for r in range(STREAMS):
                        j = (l * STREAMS + r) * P
                        pool.dma_start(K.gate1_rows[l, r].rearrange("(k p) -> k p", p=P),
                                       rows[:, j:j + P]).then_inc(s["rows_out"], 16)
                pool.wait_ge(s["rows_out"], 16 * DEPTH * STREAMS)
                pool.wait_ge(s["x_copied"], 32)

            @block.scalar
            def _(act):
                act.dma_start(K.par[:], d["params"]).then_inc(s["par"], 16)
                act.dma_start(K.cst[:], d["consts"]).then_inc(s["consts"], 16)
                act.dma_start(K.level_masks[:], d["level_masks"]).then_inc(s["consts"], 16)
                act.dma_start(K.w_router[:], d["w_router"].rearrange("l (k p) e -> p l k e", p=P)).then_inc(s["consts"], 16)
                act.dma_start(K.lam_row[:], d["lam_ab"]).then_inc(s["consts"], 16)
                act.wait_ge(s["pack"], 3)
                act.activation(condT[:], cpack[:], ACT.Silu).then_inc(s["silu"], 1)
                act.sem_inc(s["copied"], 2)
                with act.Fori(0, N_ADA // 2) as i:
                    for par in range(2):
                        q = i * 2 + par
                        act.wait_ge(K.w_used, q + 1)
                        act.wait_ge(s["added"], q + 1)
                        act.copy(row2[:, par], K.ps[0:STREAMS, par * PIECE:(par + 1) * PIECE]).then_inc(s["copied"], 1)
                act.wait_ge(s["consts"], 64)

            @block.tensor
            def _(pe):
                def product(q, bank, turn):
                    pe.wait_ge(s["copied"], q + 1)
                    pe.wait_ge(K.w_loaded[bank], turn * 16 + 16)
                    for k in range(KT):
                        mm = pe.matmul(K.ps[0:STREAMS, bank % 2 * PIECE:(bank % 2 + 1) * PIECE], condT[:, k, :], K.W[:, bank, k],
                                       start=(k == 0), stop=(k == KT - 1))
                    mm.then_inc(K.w_used, 1)

                def turn_rows(q, bank):
                    pe.wait_ge(s["copied"], q + 3)
                    pe.wait_ge(s["added"], q + 1)
                    pe.sem_inc(s["turning"], 1)
                    for ft in range(4):
                        a = (2 + bank % 2) * PIECE + ft * STREAMS
                        mm = pe.transpose(K.ps[:, a:a + STREAMS], row2[:, bank % 2, ft * P:(ft + 1) * P], K.cst[0:STREAMS, 0:STREAMS])
                    mm.then_inc(s["columns"], 1)
                pe.wait_ge(s["silu"], 1)
                pe.wait_ge(s["consts"], 64)
                with pe.Fori(0, N_ADA // SLOTS) as i:
                    for slot in range(SLOTS):
                        product(i * SLOTS + slot, slot, i)
                        if slot:
                            turn_rows(i * SLOTS + slot - 1, slot - 1)
                    turn_rows(i * SLOTS + SLOTS - 1, SLOTS - 1)
                pe.wait_ge(s["mod"], 1)
                for l in range(DEPTH):
                    for r in range(STREAMS):
                        j = (l * STREAMS + r) * P
                        mm = pe.transpose(K.ps[0:KT, 4 * PIECE + j:4 * PIECE + j + P],
                                          K.ada[:, r, l * 48 + 16:l * 48 + 24], K.c("ident"))
                mm.then_inc(s["turned"], 1)

            @block.vector
            def _(dve):
                dve.sem_inc(s["added"], 2)
                dve.wait_ge(s["par"], 16)
                dve.tensor_copy(cpack[:, :, 0], K.p("c")).then_inc(s["pack"], 1)
                dve.tensor_copy(cpack[:, :, 1], K.p("c_ctx")).then_inc(s["pack"], 1)
                dve.memset(K.eps[:], EPS).then_inc(s["pack"], 1)
                b_ada = PARAMS["b_ada"][0]
                with dve.Fori(0, N_ADA // 2) as i:
                    for par in range(2):
                        q = i * 2 + par
                        dve.wait_ge(s["columns"], q + 1)
                        for r in range(STREAMS):
                            a = (2 + par) * PIECE
                            ins = dve.tensor_tensor(
                                K.ada[:, r, bass.ds(q * 4, 4)],
                                K.ps[:, a:a + 4 * STREAMS].rearrange("p (f r) -> p r f", r=STREAMS)[:, r],
                                K.par[:, bass.ds(q * 4 + b_ada, 4)], ALU.add)
                        ins.then_inc(s["added"], 1)
                dve.wait_ge(s["added"], 2 + N_ADA)
                gn = PARAMS["g_norm"][0]
                for l in range(DEPTH):
                    for j in range(2):
                        for r in range(STREAMS):
                            g0 = gn + (l * 2 + j) * KT
                            c = l * 48 + (3 * j + 1) * KT
                            ins = dve.scalar_tensor_tensor(K.scale[:, l, j, r, :], K.ada[:, r, c:c + KT], 1.0,
                                                           K.par[:, g0:g0 + KT], ALU.add, ALU.mult)
                ins.then_inc(s["mod"], 1)
                dve.wait_ge(s["turned"], 1)
                dve.tensor_copy(rows[:], K.ps[0:KT, 4 * PIECE:4 * PIECE + DEPTH * STREAMS * P]).then_inc(s["rows"], 1)


def over_tiles(eng, body):
    with eng.Fori(0, NS // 2) as i:
        body([(i * 2, 0, i), (i * 2 + 1, 1, i)], 0)
    body([(NS, 0, NS // 2)], 1)


def stage_norm(K, l, j, store):
    nc = K.nc
    with ExitStack() as ctx:
        s = K.sems(f"norm{l}{j}", "x_in0", "x_in1", "xn_ready", "sumsq", "root", "rcp", "turned", "act_evac", "dve_evac", "stored0", "stored1")
        x_in, stored = [s["x_in0"], s["x_in1"]], [s["stored0"], s["stored1"]]
        xt = ctx.enter_context(nc.sbuf_tensor(f"xt{l}{j}", [P, 2, D], F32))
        xn = ctx.enter_context(nc.sbuf_tensor(f"xn{l}{j}", [P, 2, D], F32))
        junk = ctx.enter_context(nc.sbuf_tensor(f"junk{l}{j}", [P, D], F32))
        st = ctx.enter_context(nc.sbuf_tensor(f"stat{l}{j}", [P, 2, 4], F32))
        shift_at = l * 48 + 3 * j * KT
        with nc.Block() as block:
            @block.gpsimd
            def _(pool):
                def body(tiles, r):
                    for t, b, u in tiles:
                        pool.wait_ge(s["xn_ready"], t + 1)
                        pool.dma_start(xt[:, b], K.xres[bass.ds(t * P, P), :]).then_inc(x_in[b], 16)
                over_tiles(pool, body)

            @block.sync
            def _(sp):
                if store:
                    sp.sem_inc(stored[0], 16)
                    sp.sem_inc(stored[1], 16)

                    def body(tiles, r):
                        for t, b, u in tiles:
                            sp.wait_ge(s["xn_ready"], t + 3)
                            sp.dma_start(K.xnorm[bass.ds(t * P, P), :], xn[:, b]).then_inc(stored[b], 16)
                    over_tiles(sp, body)
                    sp.wait_ge(stored[0], 16 + 16 * 5)
                    sp.wait_ge(stored[1], 16 + 16 * 4)

            @block.scalar
            def _(act):
                def body(tiles, r):
                    for t, b, u in tiles:
                        act.wait_ge(x_in[b], u * 16 + 16)
                        act.activation(junk[:], xt[:, b], ACT.Square, accum_out=st[:, b, 0:1]).then_inc(s["sumsq"], 1)
                        act.wait_ge(s["sumsq"], t + 1)
                        act.activation(st[:, b, 1:2], st[:, b, 0:1], ACT.Sqrt, bias=K.eps[:], scale=1.0 / D).then_inc(s["root"], 1)
                    for t, b, u in tiles:
                        act.wait_ge(s["turned"], t + 3)
                        for k in range(KT // 2):
                            ins = act.activation(K.hT[:, k, bass.ds(t * P, P)], K.ps[:, b * D + k * P:b * D + (k + 1) * P],
                                                 ACT.Identity, bias=K.ada[:, r, shift_at + k:shift_at + k + 1],
                                                 scale=K.scale[:, l, j, r, k:k + 1])
                        ins.then_inc(s["act_evac"], 1)
                act.sem_inc(s["act_evac"], 2)
                over_tiles(act, body)

            @block.tensor
            def _(pe):
                def body(tiles, r):
                    for t, b, u in tiles:
                        pe.wait_ge(s["xn_ready"], t + 3)
                        pe.wait_ge(s["act_evac"], t + 1)
                        pe.wait_ge(s["dve_evac"], t + 1)
                        for k in range(KT):
                            mm = pe.transpose(K.ps[:, b * D + k * P:b * D + (k + 1) * P],
                                              xn[:, b, k * P:(k + 1) * P], K.c("ident"))
                        mm.then_inc(s["turned"], 1)
                pe.sem_inc(s["turned"], 2)
                over_tiles(pe, body)

            @block.vector
            def _(dve):
                def body(tiles, r):
                    for t, b, u in tiles:
                        dve.wait_ge(s["root"], t + 1)
                        dve.reciprocal(st[:, b, 2:3], st[:, b, 1:2]).then_inc(s["rcp"], 1)
                        dve.wait_ge(s["rcp"], t + 1)
                        dve.wait_ge(s["turned"], t + 1)
                        if store:
                            dve.wait_ge(stored[b], u * 16 + 16)
                        dve.tensor_scalar(xn[:, b], xt[:, b], st[:, b, 2:3], None, ALU.mult).then_inc(s["xn_ready"], 1)
                    for t, b, u in tiles:
                        dve.wait_ge(s["turned"], t + 3)
                        for k in range(KT // 2, KT):
                            ins = dve.tensor_scalar(K.hT[:, k, bass.ds(t * P, P)], K.ps[:, b * D + k * P:b * D + (k + 1) * P],
                                                    K.scale[:, l, j, r, k:k + 1],
                                                    K.ada[:, r, shift_at + k:shift_at + k + 1], ALU.mult, ALU.add)
                        ins.then_inc(s["dve_evac"], 1)
                dve.sem_inc(s["xn_ready"], 2)
                dve.sem_inc(s["dve_evac"], 2)
                over_tiles(dve, body)


def stage_project(K, name, at, n_feature, n_token, gates):
    nc, d = K.nc, K.d
    TC = T // 3
    n_groups = n_feature * 12 + n_token * NT
    with ExitStack() as ctx:
        s = K.sems(name, "group", "even_out", "odd_out", "stored0", "stored1", "stored2", "stored3",
                   "wg_in", "gates", "round_out", "gates_out", "gates_stored")
        stored = [s["stored0"], s["stored1"], s["stored2"], s["stored3"]]
        stg = ctx.enter_context(nc.sbuf_tensor(f"{name}_stage", [P, 4, PIECE], F32))
        if gates:
            wg = ctx.enter_context(nc.sbuf_tensor("w_gates", [P, KT, 16], F32))
            gsb = ctx.enter_context(nc.sbuf_tensor("gates_sb", [4, 4, T], F32))

        def groups():
            for f in range(n_feature):
                yield "feature", f, f * 12
            for t in range(n_token):
                yield "token", t, n_feature * 12 + t * NT

        def take_out(eng, copy, mine, out_sem):
            def one(g, bank, width, use):
                eng.wait_ge(s["group"], g + 1)
                eng.wait_ge(stored[bank], use * 16 + 16)
                copy(stg[:, bank, 0:width], K.ps[:, bank * PIECE:bank * PIECE + width]).then_inc(out_sem, 1)
            for kind, n, g0 in groups():
                if kind == "feature":
                    with eng.Fori(0, 3) as c:
                        for ft in range(mine, 4, 2):
                            one(c * 4 + (g0 + ft), ft, TC, c + g0 // 4)
                else:
                    for t in range(NT):
                        g = g0 + t
                        if g % 2 == mine:
                            one(g, g % 4, PIECE, g // 4)

        with nc.Block() as block:
            @block.sync
            def _(sp):
                for sem in stored:
                    sp.sem_inc(sem, 16)

                def out(g):
                    return s["even_out"] if g % 2 == 0 else s["odd_out"]
                for kind, n, g0 in groups():
                    if kind == "feature":
                        with sp.Fori(0, 3) as c:
                            for ft in range(4):
                                sp.wait_ge(out(ft), c * 2 + ((g0 + ft) // 2 + 1))
                                sp.dma_start(K.featT[n * 4 + ft, :, bass.ds(c * TC, TC)],
                                             stg[:, ft, 0:TC]).then_inc(stored[ft], 16)
                    else:
                        for t in range(NT):
                            g = g0 + t
                            sp.wait_ge(out(g), g // 2 + 1)
                            sp.dma_start(K.tok[n, t], stg[:, g % 4, :]).then_inc(stored[g % 4], 16)
                    ahead = at + SLOTS + (n if kind == "feature" else n_feature + n)
                    if not any(a <= ahead < a + SLOTS for a in AT_EXPERTS):
                        load_piece(K, sp, ahead)
                for b in range(4):
                    sp.wait_ge(stored[b], 16 + 16 * len(range(b, n_groups, 4)))

            @block.gpsimd
            def _(pool):
                if gates:
                    pool.dma_start(wg[:], d["w_in_ab"][0].rearrange("(k p) f -> p k f", p=P)[:, :, 3584:3600]).then_inc(s["wg_in"], 16)
                    pool.wait_ge(s["gates_out"], 1)
                    pool.dma_start(K.gate_rows.rearrange("k h t -> h k t"), gsb[:]).then_inc(s["gates_stored"], 16)
                    pool.wait_ge(s["gates_stored"], 16)

            @block.scalar
            def _(act):
                take_out(act, act.copy, 1, s["odd_out"])

            @block.vector
            def _(dve):
                take_out(dve, dve.tensor_copy, 0, s["even_out"])
                if gates:
                    for rnd in range(2):
                        dve.wait_ge(s["gates"], rnd + 1)
                        ins = dve.tensor_copy(gsb[:, 2 * rnd:2 * rnd + 2, :],
                                              K.ps[0:4, 0:2 * T].rearrange("h (k t) -> h k t", k=2))
                        ins.then_inc(s["gates_out"] if rnd else s["round_out"], 1)

            @block.tensor
            def _(pe):
                def bank_free(g_mod, count):
                    pe.wait_ge(s["even_out"] if g_mod % 2 == 0 else s["odd_out"], count)
                for kind, n, g0 in groups():
                    piece = at + (n if kind == "feature" else n_feature + n)
                    wait_piece(K, pe, piece)
                    w = K.W[:, piece % SLOTS]
                    if kind == "feature":
                        def chunk(c, first):
                            for ft in range(4):
                                if not first:
                                    bank_free(ft, c * 2 + ((g0 + ft - 4) // 2 + 1))
                                for k in range(KT):
                                    mm = pe.matmul(K.ps[:, ft * PIECE:ft * PIECE + TC], w[:, k, ft * P:(ft + 1) * P],
                                                   K.hT[:, k, bass.ds(c * TC, TC)], start=(k == 0), stop=(k == KT - 1))
                                mm.then_inc(s["group"], 1)
                        if g0 == 0:
                            chunk(0, True)
                            with pe.Fori(1, 3) as c:
                                chunk(c, False)
                        else:
                            with pe.Fori(0, 3) as c:
                                chunk(c, False)
                    else:
                        for t in range(NT):
                            g = g0 + t
                            bank_free(g, (g - 4) // 2 + 1)
                            for k in range(KT):
                                mm = pe.matmul(K.ps[:, g % 4 * PIECE:(g % 4 + 1) * PIECE],
                                               K.hT[:, k, t * P:(t + 1) * P], w[:, k, :], start=(k == 0), stop=(k == KT - 1))
                            mm.then_inc(s["group"], 1)
                    pe.drain().then_inc(K.w_used, 1)
                if gates:
                    pe.wait_ge(s["wg_in"], 16)
                    bank_free(0, len(range(0, n_groups, 2)))
                    bank_free(1, len(range(1, n_groups, 2)))
                    for rnd in range(2):
                        if rnd:
                            pe.wait_ge(s["round_out"], 1)
                        for q in range(2):
                            kind = 2 * rnd + q
                            for c0, n in [(q * T + a, b) for a, b in ((0, 384), (384, 384), (768, 384))]:
                                cut = min(n, PIECE - c0 % PIECE)
                                for a, m in ((c0, cut), (c0 + cut, n - cut)):
                                    if m:
                                        for k in range(KT):
                                            mm = pe.matmul(K.ps[0:4, a:a + m], wg[:, k, kind * 4:kind * 4 + 4],
                                                           K.hT[:, k, a - q * T:a - q * T + m], start=(k == 0), stop=(k == KT - 1))
                        mm.then_inc(s["gates"], 1)


def stage_attention(K):
    nc, d = K.nc, K.d
    NK = NT + 1
    KEYS = T
    SC = float(DQK) ** -0.5
    CH = KEYS // 3
    PER_TILE = 6
    with ExitStack() as ctx:
        def sb(name, shape):
            return ctx.enter_context(nc.sbuf_tensor(f"att_{name}", shape, F32))
        s = K.sems("att", "q_in", "k_in", "v_in", "rope_in", "rope_steps", "steps", "roped", "k_turned", "q_turned", "kT_out",
                   "qT_out", "scored", "bias", "expd", "mixed", "aT", "aT_out", "av", "av_out", "root", "normed", "o_turned",
                   "o_out", "lam_steps", "lam_e", "lam_ps", "kept")
        q, k, v = sb("q", [P, NT, P]), sb("k", [P, NK, P]), sb("v", [P, NK, P])
        qr, tmp = sb("qr", [P, NS, P]), sb("tmp", [P, NS, P])
        kr = sb("kr", [P, NS, P])
        rope = sb("rope", [P, 2, NS, P])
        qT, kT = sb("qT", [P, T]), sb("kT", [P, NK * P])
        assert KEYS == T
        p0, p1 = K.hT[:, 4:6], sb("p1", [P, 2, KEYS])
        aT = K.hT[:, 6]
        o, sq = K.hT[:, 7].rearrange("p (t f) -> p t f", f=P), sb("sq", [P, P])
        rms = sb("rms", [P, 3, NT])
        st = sb("stat", [P, 2, 8])
        lam = sb("lam", [1, 4 * DQK])
        nlam = sb("nlam", [P, 1])
        gs = sb("g_scaled", [P, HEADS_A])
        S0 = 0
        TR, AV = 6 * PIECE, 7 * PIECE

        def q_cols(i):
            return slice(i * P, (i + 1) * P)

        def keys_of(i):
            return (0, NT) if i < NS else (KEYS, 1)

        def chunks(n_tiles):
            return [(c, CH) for c in range(3)] if n_tiles == NT else [(0, P)]

        def scores_ps(j, n_tiles):
            a = S0 + j * 3 * PIECE
            if n_tiles == 1:
                return K.ps[:, a:a + P].rearrange("p (c n) -> p c n", c=1)
            return K.ps[:, a:a + 3 * PIECE].rearrange("p (c n) -> p c n", c=3)[:, :, 0:CH]

        def rounds(n_tiles):
            return [(a, min(4, n_tiles - a)) for a in range(0, n_tiles, 4)]
        ROUNDS = [sum(len(rounds(keys_of(j)[1])) for j in range(i)) for i in range(NT + 1)]

        with nc.Block() as block:
            @block.sync
            def _(sp):
                sp.dma_start(d["o_new_k"][0, 0].rearrange("t h f -> t (h f)"), K.tok[1, NS]).then_inc(s["kept"], 16)
                sp.dma_start(d["o_new_v"][0, 0].rearrange("t h f -> t (h f)"), K.tok[2, NS]).then_inc(s["kept"], 16)
                sp.wait_ge(s["kept"], 32)

            @block.gpsimd
            def _(pool):
                pool.dma_start(rope[:], d["rope"]).then_inc(s["rope_in"], 16)
                tok = K.tok.rearrange("n t p f -> n p t f")

                def load_q(h):
                    pool.dma_start(q[:], tok[0, :, :, bass.ds(h * P, P)]).then_inc(s["q_in"], 16)

                def load_k(h):
                    pool.dma_start(k[:, 1:NK], tok[1, :, :, bass.ds(h * P, P)]).then_inc(s["k_in"], 16)
                    pool.dma_start(k[:, 0], d["cache_dattn_k"][0, 0, :, bass.ds(h, 1), :].rearrange("t a f -> t (a f)")).then_inc(s["k_in"], 16)

                def load_v(h):
                    pool.dma_start(v[:, 1:NK], tok[2, :, :, bass.ds(h * P, P)]).then_inc(s["v_in"], 16)
                    pool.dma_start(v[:, 0], d["cache_dattn_v"][0, 0, :, bass.ds(h, 1), :].rearrange("t a f -> t (a f)")).then_inc(s["v_in"], 16)
                load_q(0)
                load_k(0)
                load_v(0)
                with pool.Fori(1, HEADS_A) as h:
                    pool.wait_ge(s["k_turned"], h)
                    pool.wait_ge(s["q_turned"], h)
                    load_q(h)
                    load_k(h)
                    pool.wait_ge(s["av"], h * NT)
                    load_v(h)

            def over_heads(eng, body):
                with eng.Fori(0, HEADS_A - 1) as h:
                    body(h, True)
                body(HEADS_A - 1, False)

            @block.tensor
            def _(pe):
                pe.wait_ge(s["lam_steps"], 6)
                pe.matmul(K.ps[:, AV:AV + 1], K.cst[0:1, P:2 * P], lam[0:1, 8:9], start=True, stop=True).then_inc(s["lam_ps"], 1)

                def turn_k(h):
                    pe.wait_ge(s["roped"], h * 2 + 2)
                    for i in range(NK):
                        src = kr[:, i - 1] if 1 <= i <= NS else k[:, i]
                        mm = pe.transpose(K.ps[:, 3 * PIECE + i * P:3 * PIECE + (i + 1) * P], src, K.c("ident"))
                    mm.then_inc(s["k_turned"], 1)

                def turn_q(h):
                    pe.wait_ge(s["roped"], h * 2 + 1)
                    for i in range(NT):
                        src = qr[:, i] if i < NS else q[:, i]
                        mm = pe.transpose(K.ps[:, i * P:(i + 1) * P], src, K.c("ident"))
                    mm.then_inc(s["q_turned"], 1)
                turn_k(0)
                turn_q(0)

                def head(h, more):
                    pe.wait_ge(s["kT_out"], h + 1)
                    pe.wait_ge(s["qT_out"], h + 1)

                    def score(i):
                        k0, n = keys_of(i)
                        for j in range(2):
                            if i > 0:
                                pe.wait_ge(s["expd"], h * 2 * NT + (2 * (i - 1) + j + 1))
                            rows = slice(j * DQK, (j + 1) * DQK)
                            for c, w in chunks(n):
                                a = S0 + (3 * j + c) * PIECE
                                mm = pe.matmul(K.ps[:, a:a + w], qT[rows, q_cols(i)],
                                               kT[rows, k0 + c * CH:k0 + c * CH + w], start=True, stop=True)
                            mm.then_inc(s["scored"], 1)

                    def turn_and_product(i):
                        k0, n = keys_of(i)
                        pe.wait_ge(s["mixed"], h * NT + (i + 1))
                        for r, (a, m) in enumerate(rounds(n)):
                            done = ROUNDS[i] + r
                            pe.wait_ge(s["aT_out"], h * ROUNDS[NT] + done + 1)
                            for y in range(m):
                                mm = pe.transpose(K.ps[:, TR + y * P:TR + (y + 1) * P],
                                                  p0[:, i % 2, (a + y) * P:(a + y + 1) * P], K.c("ident"))
                            mm.then_inc(s["aT"], 1)
                        pe.wait_ge(s["aT_out"], h * ROUNDS[NT] + ROUNDS[i + 1] + 1)
                        pe.wait_ge(s["v_in"], h * 32 + 32)
                        pe.wait_ge(s["av_out"], h * NT + i + 1)
                        for y in range(n):
                            mm = pe.matmul(K.ps[:, AV:AV + P], aT[:, y * P:(y + 1) * P], v[:, k0 // P + y],
                                           start=(y == 0), stop=(y == n - 1))
                        mm.then_inc(s["av"], 1)

                    score(0)
                    for i in range(NT):
                        if i + 1 < NT:
                            score(i + 1)
                        turn_and_product(i)
                    if more:
                        turn_k(h + 1)
                    pe.wait_ge(s["normed"], h + 1)
                    for i in range(NT):
                        mm = pe.transpose(K.ps[:, i * P:(i + 1) * P], o[:, i], K.c("ident"))
                    mm.then_inc(s["o_turned"], 1)
                    if more:
                        pe.wait_ge(s["o_out"], h + 1)
                        turn_q(h + 1)
                over_heads(pe, head)

            @block.scalar
            def _(act):
                act.sem_inc(s["av_out"], 1)
                act.sem_inc(s["aT_out"], 1)
                act.wait_ge(s["lam_steps"], 4)
                act.activation(lam[0:1, 4:6], lam[0:1, 0:2], ACT.Exp).then_inc(s["lam_e"], 1)

                def copy_k(h):
                    act.wait_ge(s["k_turned"], h + 1)
                    act.copy(kT[:], K.ps[:, 3 * PIECE:3 * PIECE + NK * P]).then_inc(s["kT_out"], 1)

                def copy_q(h):
                    act.wait_ge(s["q_turned"], h + 1)
                    act.copy(qT[:], K.ps[:, 0:T]).then_inc(s["qT_out"], 1)
                copy_k(0)
                copy_q(0)

                def head(h, more):
                    def exp(i, j):
                        k0, n = keys_of(i)
                        act.wait_ge(s["bias"], h * 2 * NT + (2 * i + j + 1))
                        act.activation((p0, p1)[j][:, i % 2, 0:n * P].rearrange("p (c n) -> p c n", c=len(chunks(n))), scores_ps(j, n),
                                       ACT.Exp, bias=st[:, i % 2, 2 + j:3 + j], scale=SC,
                                       accum_out=st[:, i % 2, 4 + j:5 + j]).then_inc(s["expd"], 1)

                    exp(0, 0)
                    exp(0, 1)
                    for i in range(NT):
                        k0, n = keys_of(i)
                        for r, (a, m) in enumerate(rounds(n)):
                            act.wait_ge(s["aT"], h * ROUNDS[NT] + (ROUNDS[i] + r + 1))
                            if i > 0:
                                act.wait_ge(s["av"], h * NT + i)
                            act.copy(aT[:, a * P:(a + m) * P], K.ps[:, TR:TR + m * P]).then_inc(s["aT_out"], 1)
                            if i + 1 < NT and r < 2:
                                exp(i + 1, r)
                        act.wait_ge(s["av"], h * NT + (i + 1))
                        act.activation(sq[:], K.ps[:, AV:AV + P], ACT.Square, accum_out=rms[:, 0, i:i + 1])
                        act.copy(o[:, i], K.ps[:, AV:AV + P]).then_inc(s["av_out"], 1)
                    act.wait_ge(s["av_out"], h * NT + NT + 1)
                    act.activation(rms[:, 1], rms[:, 0], ACT.Sqrt, bias=K.eps[:], scale=1.0 / P).then_inc(s["root"], 1)
                    if more:
                        copy_k(h + 1)
                        copy_q(h + 1)
                over_heads(act, head)

            @block.vector
            def _(dve):
                one = Steps(dve, s["lam_steps"])
                one.did(dve.tensor_tensor(lam[0:1, 16:16 + DQK], K.lam_row[0:1, 0:DQK], K.lam_row[0:1, DQK:2 * DQK], ALU.mult))
                one.did(dve.tensor_tensor(lam[0:1, 96:96 + DQK], K.lam_row[0:1, 2 * DQK:3 * DQK], K.lam_row[0:1, 3 * DQK:4 * DQK], ALU.mult))
                one.wait()
                one.did(dve.tensor_reduce(lam[0:1, 0:1], lam[0:1, 16:16 + DQK], AX_X, ALU.add))
                one.did(dve.tensor_reduce(lam[0:1, 1:2], lam[0:1, 96:96 + DQK], AX_X, ALU.add))
                dve.wait_ge(s["lam_e"], 1)
                one.did(dve.tensor_tensor(lam[0:1, 6:7], lam[0:1, 5:6], lam[0:1, 4:5], ALU.subtract))
                one.wait()
                one.did(dve.tensor_scalar(lam[0:1, 8:9], lam[0:1, 6:7], -LAM_INIT, None, ALU.add))
                dve.wait_ge(s["lam_ps"], 1)
                one.did(dve.tensor_copy(nlam[:], K.ps[:, AV:AV + 1]))
                one.did(dve.tensor_scalar(gs[:], K.p("g_attn"), 1.0 - LAM_INIT, None, ALU.mult))
                one.wait()
                dve.wait_ge(s["rope_in"], 16)

                def rotate(which, h):
                    src, out, off, sem, per = ((q, qr, 0, s["q_in"], 16), (k, kr, 1, s["k_in"], 32))[which]
                    turn = Steps(dve, s["rope_steps"], h, 8)
                    turn.k = 4 * which
                    x = src[:, off:off + NS].rearrange("p t (j a f) -> p (t j) a f", j=2, a=2)
                    tp = tmp[:].rearrange("p t (j a f) -> p (t j) a f", j=2, a=2)
                    sn = rope[:, 1].rearrange("p t (j a f) -> p (t j) a f", j=2, a=2)
                    dve.wait_ge(sem, h * per + per)
                    turn.did(dve.tensor_tensor(out[:], src[:, off:off + NS], rope[:, 0], ALU.mult))
                    turn.did(dve.tensor_tensor(tp[:, :, 0], x[:, :, 1], sn[:, :, 0], ALU.mult))
                    turn.did(dve.tensor_tensor(tp[:, :, 1], x[:, :, 0], sn[:, :, 1], ALU.mult))
                    turn.wait()
                    turn.did(dve.tensor_tensor(out[:], out[:], tmp[:], ALU.add))
                    turn.wait()
                    dve.sem_inc(s["roped"], 1)
                rotate(0, 0)
                rotate(1, 0)

                def head(h, more):
                    step = Steps(dve, s["steps"], h, NT * PER_TILE + 2)

                    def softmax_bias(i):
                        k0, n = keys_of(i)
                        b = i % 2
                        for j in range(2):
                            dve.wait_ge(s["scored"], h * 2 * NT + (2 * i + j + 1))
                            axis = mybir.AxisListType.XY
                            step.did(dve.tensor_reduce(st[:, b, j:j + 1], scores_ps(j, n), axis, ALU.max))
                            step.wait()
                            dve.tensor_scalar(st[:, b, 2 + j:3 + j], st[:, b, j:j + 1], -SC, None, ALU.mult).then_inc(s["bias"], 1)

                    softmax_bias(0)
                    for i in range(NT):
                        b = i % 2
                        k0, n = keys_of(i)
                        dve.wait_ge(s["expd"], h * 2 * NT + 2 * (i + 1))
                        step.did(dve.reciprocal(st[:, b, 6:8], st[:, b, 4:6]))
                        step.wait()
                        step.did(dve.tensor_scalar(p0[:, b, 0:n * P], p0[:, b, 0:n * P], st[:, b, 6:7], None, ALU.mult))
                        step.did(dve.tensor_tensor(st[:, b, 7:8], st[:, b, 7:8], nlam[:], ALU.mult))
                        step.wait()
                        step.did(dve.scalar_tensor_tensor(p0[:, b, 0:n * P], p1[:, b, 0:n * P], st[:, b, 7:8], p0[:, b, 0:n * P],
                                                          ALU.mult, ALU.add))
                        step.wait()
                        dve.sem_inc(s["mixed"], 1)
                        if i + 1 < NT:
                            softmax_bias(i + 1)
                        if more and i in (3, 5):
                            rotate(i // 4, h + 1)
                    dve.wait_ge(s["root"], h + 1)
                    step.did(dve.reciprocal(rms[:, 2], rms[:, 1]))
                    step.wait()
                    step.did(dve.tensor_tensor(o, o, rms[:, 2].unsqueeze(2).to_broadcast([P, NT, P]), ALU.mult))
                    step.wait()
                    step.close()
                    dve.sem_inc(s["normed"], 1)
                    dve.wait_ge(s["o_turned"], h + 1)
                    dve.tensor_scalar(K.hT[:, bass.ds(h, 1), :].rearrange("p a t -> p (a t)"), K.ps[:, 0:T],
                                      gs[:, bass.ds(h, 1)], None, ALU.mult).then_inc(s["o_out"], 1)
                over_heads(dve, head)


def stage_gates(K):
    nc, d = K.nc, K.d
    with ExitStack() as ctx:
        def sb(name, shape):
            return ctx.enter_context(nc.sbuf_tensor(f"gate_{name}", shape, F32))
        s = K.sems("gate", "rows_in", "par_in", "steps", "abs", "exped", "log", "em", "rows_ready", "rows_out", "small", "small_out",
                   "wold", "turned", "cols", "m_out")
        g = sb("in", [4, 4, T])
        li, x = g[:, 0:2], g[:, 2:4]
        a, b, m = sb("a", [4, 2, T]), sb("b", [4, 2, T]), sb("m", [4, 2, T])
        resets = sb("resets", [4, 2, T])
        bias = sb("bias", [4, 3, 2])
        sm = sb("small", [4, 2, 2, NT])
        e = sb("end", [4, 3, 2, NT])

        def ends(t, r):
            return t[:, r].rearrange("h (c p) -> h c p", p=P)[:, :, (P - 1) if r == 0 else 0]

        def along(t, r, lo, hi):
            if r == 0:
                return t[:, 0, lo:hi]
            return t[:, 1, lo:hi][:, ::-1]

        with nc.Block() as block:
            @block.sync
            def _(sp):
                sp.dma_start(g[:], K.gate_rows.rearrange("k h t -> h k t")).then_inc(s["rows_in"], 16)
                sp.dma_start(resets[:], d["resets"]).then_inc(s["rows_in"], 16)
                with nc.allow_non_contiguous_dma("a few words"):
                    sp.dma_start(bias[:, 0], d["b_ig_ab"][0].rearrange("r h -> h r")).then_inc(s["par_in"], 16)
                    sp.dma_start(bias[:, 1], d["b_fg_ab"][0].rearrange("r h -> h r")).then_inc(s["par_in"], 16)
                    sp.dma_start(bias[:, 2], d["state_mlstm_m"][0, 0].rearrange("r h -> h r")).then_inc(s["par_in"], 16)
                    sp.wait_ge(s["rows_ready"], 1)
                    sp.dma_start(K.mrows.rearrange("r h t -> h r t"), x).then_inc(s["rows_out"], 16)
                    sp.wait_ge(s["wold"], 1)
                    sp.dma_start(K.msmall.rearrange("k r h c -> h k r c"), sm[:]).then_inc(s["small_out"], 16)
                    sp.dma_start(d["o_new_m"][0, 0].rearrange("r h -> h r"), e[:, 1, :, NS]).then_inc(s["m_out"], 16)
                sp.wait_ge(s["rows_out"], 16)
                sp.wait_ge(s["small_out"], 16)
                sp.wait_ge(s["m_out"], 16)

            @block.scalar
            def _(act):
                act.wait_ge(s["abs"], 1)
                act.activation(a[:], a[:], ACT.Exp, scale=-1.0).then_inc(s["exped"], 1)
                act.wait_ge(s["exped"], 1)
                act.activation(a[:], a[:], ACT.Ln, bias=1.0).then_inc(s["log"], 1)
                act.wait_ge(s["rows_ready"], 1)
                act.activation(a[:], m[:], ACT.Exp, scale=-1.0).then_inc(s["em"], 1)
                act.wait_ge(s["small"], 1)
                act.activation(sm[:, 1], sm[:, 1], ACT.Exp).then_inc(s["wold"], 1)
                act.wait_ge(s["turned"], 1)
                act.activation(K.w_state[:], K.ps[:, PIECE:PIECE + 72].rearrange("p (r c h) -> p r c h", r=2, c=NT),
                               ACT.Exp).then_inc(s["cols"], 1)
                act.copy(K.em_cols[:], K.ps[:, 2 * PIECE:2 * PIECE + 72].rearrange("p (r c h) -> p r c h", r=2, c=NT))

            @block.tensor
            def _(pe):
                pe.wait_ge(s["small"], 1)
                pe.wait_ge(s["em"], 1)
                for kind, src in ((0, b), (1, m), (2, a)):
                    for r in range(2):
                        for c in range(NT):
                            at = kind * PIECE + (r * NT + c) * 4
                            mm = pe.transpose(K.ps[:, at:at + 4], src[:, r, c * P:(c + 1) * P], K.cst[0:4, 0:4])
                mm.then_inc(s["turned"], 1)

            @block.vector
            def _(dve):
                step = Steps(dve, s["steps"])
                dve.wait_ge(s["rows_in"], 32)
                dve.wait_ge(s["par_in"], 48)
                for r in range(2):
                    step.did(dve.tensor_scalar(li[:, r], li[:, r], bias[:, 0, r:r + 1], None, ALU.add))
                    step.did(dve.tensor_scalar(x[:, r], x[:, r], bias[:, 1, r:r + 1], None, ALU.add))
                step.wait()
                dve.scalar_tensor_tensor(a[:], x, -1.0, x, ALU.mult, ALU.max).then_inc(s["abs"], 1)
                dve.wait_ge(s["log"], 1)
                step.did(dve.scalar_tensor_tensor(x, x, 0.0, a[:], ALU.min, ALU.subtract))
                step.wait()
                for r in range(2):
                    step.did(dve.tensor_tensor_scan(along(b, r, 0, T), along(resets, r, 0, T), along(x, r, 0, T), 0.0,
                                                    ALU.mult, ALU.add))
                    step.did(dve.tensor_tensor_scan(along(m, r, 0, T_S), along(x, r, 0, T_S), along(li, r, 0, T_S),
                                                    bias[:, 2, r:r + 1], ALU.add, ALU.max))
                    step.did(dve.tensor_tensor_scan(along(m, r, T_S, T), along(x, r, T_S, T), along(li, r, T_S, T),
                                                    0.0, ALU.add, ALU.max))
                step.wait()
                step.did(dve.tensor_tensor(x, b[:], m[:], ALU.subtract))
                for r in range(2):
                    step.did(dve.tensor_copy(e[:, 0, r], ends(b, r)))
                    step.did(dve.tensor_copy(e[:, 1, r], ends(m, r)))
                step.did(dve.memset(sm[:, 0, :, NS:NT], 0.0))
                step.did(dve.tensor_copy(sm[:, 0, 0, 0:1], bias[:, 2, 0:1]))
                step.did(dve.tensor_copy(sm[:, 0, 1, NS - 1:NS], bias[:, 2, 1:2]))
                step.wait()
                step.did(dve.tensor_copy(sm[:, 0, 0, 1:NS], e[:, 1, 0, 0:NS - 1]))
                step.did(dve.tensor_copy(sm[:, 0, 1, 0:NS - 1], e[:, 1, 1, 1:NS]))
                step.did(dve.tensor_tensor(e[:, 2], e[:, 0], e[:, 1], ALU.subtract))
                step.wait()
                dve.sem_inc(s["rows_ready"], 1)
                step.did(dve.tensor_tensor(sm[:, 1], e[:, 2], sm[:, 0], ALU.add))
                step.did(dve.tensor_tensor(b[:], li, b[:], ALU.subtract))
                step.wait()
                dve.wait_ge(s["em"], 1)
                for r in range(2):
                    step.did(dve.tensor_tensor(m[:, r].rearrange("h (c p) -> h c p", p=P),
                                               b[:, r].rearrange("h (c p) -> h c p", p=P),
                                               e[:, 2, r].unsqueeze(2).to_broadcast([4, NT, P]), ALU.add))
                step.wait()
                dve.sem_inc(s["small"], 1)
                dve.wait_ge(s["turned"], 1)
                dve.tensor_copy(K.w_arg[:], K.ps[:, 0:72].rearrange("p (r c h) -> p r c h", r=2, c=NT)).then_inc(s["cols"], 1)


def stage_mlstm(K):
    nc, d = K.nc, K.d
    NSTATE = NS + 2
    F1 = P + 1
    PER_BANK = 3
    with ExitStack() as ctx:
        def sb(name, shape):
            return ctx.enter_context(nc.sbuf_tensor(f"ml_{name}", shape, F32))[:]
        s = K.sems("ml", "x_in", "v_in", "o_in", "row_in", "small_in", "st_in", "conv_steps", "conv", "silu", "scaled", "sig",
                   "kT", "kw", "scT", "sc_out", "masked", "exped", "att", "kv", "states", "C_out", "num", "steps", "read",
                   "root", "normed", "h_turned", "done", "order", "sp_order")
        take = free_slots(K, AT_OUT[0])
        qx, kx, ox = sb("qx", [P, T]), sb("kx", [P, T]), sb("ox", [P, T])
        v = sb("v", [P, NT, F1])
        qc, kc = sb("qc", [P, T]), sb("kc", [P, T])
        ub, att, qw, kw = ([take(T), take(T)] for _ in range(4))
        sg, hs = take(T), take(T)
        C = [take(NSTATE * F1).rearrange("p (n f) -> p n f", f=F1) for r in range(2)]
        sc = take(T)
        small = sb("small", [P, 2, 2, NT])
        w_st = sb("w_state", [P, 2, NT, HEADS_B])
        den, rms = sb("den", [P, 2, NT]), sb("rms", [P, 3, NT])
        NUM = [0, 3 * PIECE]
        KV = [6 * PIECE, 7 * PIECE]
        K_SCALE = float(P) ** -0.5
        N_STATES = 2 * NT

        def chunk(t):
            return t.rearrange("p (c n) -> p c n", n=P)

        def cols(c):
            return slice(c * P, (c + 1) * P)

        def chunk_of(r, n):
            return NS if n == NS else (n if r == 0 else NS - 1 - n)

        def before(r, c):
            return c if r == 0 else NS - 1 - c

        def num(r, c):
            a = NUM[r] + c // PER_BANK * PIECE + c % PER_BANK * F1
            return K.ps[:, a:a + F1]

        def nums(r):
            banks = K.ps[:, NUM[r]:NUM[r] + 3 * PIECE].rearrange("p (b n) -> p b n", b=3)[:, :, 0:PER_BANK * F1]
            return banks.rearrange("p b (j f) -> p b j f", f=F1)

        def by_bank(t):
            return t.rearrange("p (b j) -> p b j", j=PER_BANK)

        def over_heads(eng, body):
            with eng.Fori(0, HEADS_B - 1) as h:
                body(h, True)
            body(HEADS_B - 1, False)

        with nc.Block() as block:
            @block.gpsimd
            def _(pool):
                def load_x(h):
                    pool.dma_start(qx, K.featT[bass.ds(h, 1)].rearrange("a p t -> (a p) t")).then_inc(s["x_in"], 16)
                    pool.dma_start(kx, K.featT[bass.ds(h + 4, 1)].rearrange("a p t -> (a p) t")).then_inc(s["x_in"], 16)

                def load_o(h):
                    pool.dma_start(ox, K.featT[bass.ds(h + 8, 1)].rearrange("a p t -> (a p) t")).then_inc(s["o_in"], 16)

                def load_v(h):
                    pool.dma_start(v[:, :, 0:P], K.tok.rearrange("n t p f -> n p t f")[3, :, :, bass.ds(h * P, P)]).then_inc(s["v_in"], 16)
                load_x(0)
                load_v(0)
                load_o(0)
                with pool.Fori(1, HEADS_B) as h:
                    pool.wait_ge(s["conv"], h * 2)
                    load_x(h)
                    pool.wait_ge(s["sig"], h)
                    load_o(h)
                    pool.wait_ge(s["num"], h * 2)
                    load_v(h)

            @block.sync
            def _(sp):
                sp.sem_inc(s["C_out"], 64)

                def load_rows(h):
                    for r in range(2):
                        sp.dma_start(ub[r], K.mrows[r, bass.ds(h, 1), :].to_broadcast([P, T])).then_inc(s["row_in"], 16)

                def load_small(h):
                    sp.dma_start(small, K.msmall[:, :, bass.ds(h, 1), :].rearrange("k r a c -> a k r c")
                                 .to_broadcast([P, 2, 2, NT])).then_inc(s["small_in"], 16)

                def load_state(h):
                    for r in range(2):
                        sp.dma_start(C[r][:, 0, 0:P], d["state_mlstm_C"][0, 0, r, bass.ds(h, 1)].rearrange("a k v -> (a k) v")).then_inc(s["st_in"], 16)
                        sp.dma_start(C[r][:, 0, P:F1], d["state_mlstm_n"][0, 0, r, bass.ds(h, 1)].rearrange("a k -> k a")).then_inc(s["st_in"], 16)

                def store_state(h):
                    for r in range(2):
                        sp.dma_start(d["o_new_C"][0, 0, r, bass.ds(h, 1)].rearrange("a k v -> (a k) v"), C[r][:, NS + 1, 0:P]).then_inc(s["C_out"], 16)
                        sp.dma_start(d["o_new_n"][0, 0, r, bass.ds(h, 1)].rearrange("a k -> k a"), C[r][:, NS + 1, P:F1]).then_inc(s["C_out"], 16)
                with nc.allow_non_contiguous_dma("a state's normaliser column"):
                    load_rows(0)
                    load_small(0)
                    load_state(0)
                    with sp.Fori(1, HEADS_B) as h:
                        sp.wait_ge(s["masked"], h * 2)
                        sp.sem_inc(s["sp_order"], 1)
                        sp.wait_ge(s["exped"], h * 4)
                        sp.sem_inc(s["sp_order"], 1)
                        load_rows(h)
                        sp.wait_ge(s["states"], h * N_STATES)
                        sp.sem_inc(s["sp_order"], 1)
                        load_small(h)
                        store_state(h - 1)
                        sp.wait_ge(s["num"], h * 2)
                        sp.sem_inc(s["sp_order"], 1)
                        load_state(h)
                    sp.wait_ge(s["states"], HEADS_B * N_STATES)
                    store_state(HEADS_B - 1)
                sp.wait_ge(s["C_out"], 64 * HEADS_B + 64)

            @block.scalar
            def _(act):
                def silu(h):
                    for j, t in enumerate((kc, qc)):
                        act.wait_ge(s["conv"], h * 2 + j + 1)
                        act.activation(t, t, ACT.Silu).then_inc(s["silu"], 1)

                silu(0)

                def head(h, more):
                    act.wait_ge(s["scT"], h + 1)
                    act.activation(sc, K.ps[:, NUM[1]:NUM[1] + T], ACT.Identity, scale=K_SCALE).then_inc(s["sc_out"], 1)
                    act.wait_ge(s["row_in"], h * 32 + 32)
                    act.wait_ge(s["small_in"], h * 16 + 16)
                    for r in range(2):
                        for c in range(NT):
                            e = act.activation(qw[r][:, cols(c)], ub[r][:, cols(c)], ACT.Exp, bias=small[:, 0, r, c:c + 1])
                        e.then_inc(s["exped"], 1)
                        act.wait_ge(s["masked"], h * 2 + r + 1)
                        act.sem_inc(s["order"], 1)
                        for c in range(NT):
                            e = act.activation(att[r][:, cols(c)], att[r][:, cols(c)], ACT.Exp, bias=K.w_arg[:, r, c, bass.ds(h, 1)])
                        e.then_inc(s["exped"], 1)
                    act.wait_ge(s["o_in"], h * 16 + 16)
                    act.wait_ge(s["done"], h + 1)
                    act.activation(sg, ox, ACT.Sigmoid).then_inc(s["sig"], 1)
                    if more:
                        silu(h + 1)
                    act.wait_ge(s["read"], h * 2 + 2)
                    for c in range(NT):
                        e = act.activation(kw[0][:, cols(c)], hs[:, cols(c)], ACT.Square, accum_out=rms[:, 0, c:c + 1])
                    e.then_inc(s["root"], 1)
                    act.wait_ge(s["root"], h * 2 + 1)
                    act.activation(rms[:, 1], rms[:, 0], ACT.Sqrt, bias=K.eps[:], scale=1.0 / P).then_inc(s["root"], 1)
                over_heads(act, head)

            @block.tensor
            def _(pe):
                def score(h):
                    pe.wait_ge(s["silu"], h * 2 + 2)
                    for c in range(NT):
                        mm = pe.matmul(K.ps[:, NUM[1] + c * P:NUM[1] + (c + 1) * P], kc[:, cols(c)], qc[:, cols(c)], start=True, stop=True)
                    mm.then_inc(s["scT"], 1)

                def turn_k(h):
                    for c in range(NT):
                        mm = pe.transpose(K.ps[:, cols(c)], kc[:, cols(c)], K.c("ident"))
                    mm.then_inc(s["kT"], 1)
                score(0)
                turn_k(0)

                def head(h, more):
                    pe.wait_ge(s["v_in"], h * 16 + 16)
                    pe.wait_ge(s["scaled"], 2)
                    pe.wait_ge(s["kw"], h * 2 + 2)
                    for k in range(NT // PER_BANK):
                        if k:
                            pe.wait_ge(s["states"], h * N_STATES + 2 * PER_BANK * k)
                        for r in range(2):
                            for j in range(PER_BANK):
                                c = chunk_of(r, k * PER_BANK + j)
                                mm = pe.matmul(K.ps[:, KV[r] + j * F1:KV[r] + (j + 1) * F1], kw[r][:, cols(c)], v[:, c], start=True, stop=True)
                        mm.then_inc(s["kv"], 1)
                    pe.wait_ge(s["states"], h * N_STATES + N_STATES)
                    for r in range(2):
                        pe.wait_ge(s["att"], h * 2 + r + 1)
                        for c in range(NT):
                            if c < NS:
                                pe.matmul(num(r, c), qw[r][:, cols(c)], C[r][:, before(r, c)], start=True, stop=False)
                            mm = pe.matmul(num(r, c), att[r][:, cols(c)], v[:, c], start=(c == NS), stop=True)
                        mm.then_inc(s["num"], 1)
                    if more:
                        pe.wait_ge(s["read"], h * 2 + 2)
                        score(h + 1)
                    pe.wait_ge(s["normed"], h + 1)
                    for c in range(NT):
                        mm = pe.transpose(K.ps[:, cols(c)], hs[:, cols(c)], K.c("ident"))
                    mm.then_inc(s["h_turned"], 1)
                    if more:
                        pe.wait_ge(s["done"], h + 2)
                        turn_k(h + 1)
                over_heads(pe, head)

            @block.vector
            def _(dve):
                dve.sem_inc(s["done"], 1)
                dve.memset(v[:, :, P:F1], 1.0).then_inc(s["scaled"], 1)
                dve.tensor_scalar(w_st, K.w_state[:], K_SCALE, None, ALU.mult).then_inc(s["scaled"], 1)
                dve.wait_ge(s["scaled"], 2)
                conv_at = PARAMS["conv"][0]

                def convolve(h):
                    step = Steps(dve, s["conv_steps"], h, 10)
                    dve.wait_ge(s["x_in"], h * 32 + 32)
                    for j, x, y in ((1, kx, kc), (0, qx, qc)):
                        def w(i):
                            return K.par[:, bass.ds(h + (conv_at + i * 8 + j * 4), 1)]
                        step.did(dve.tensor_scalar(y, x, w(1), None, ALU.mult))
                        step.wait()
                        for lo, hi in ((0, T_S), (T_S, T)):
                            step.did(dve.scalar_tensor_tensor(y[:, lo + 1:hi], x[:, lo:hi - 1], w(0), y[:, lo + 1:hi], ALU.mult, ALU.add))
                        step.wait()
                        for lo, hi in ((0, T_S), (T_S, T)):
                            step.did(dve.scalar_tensor_tensor(y[:, lo:hi - 1], x[:, lo + 1:hi], w(2), y[:, lo:hi - 1], ALU.mult, ALU.add))
                        step.wait()
                        dve.sem_inc(s["conv"], 1)
                convolve(0)

                def head(h, more):
                    dve.wait_ge(s["row_in"], h * 32 + 32)
                    for r in range(2):
                        neg = K.c("neg_fwd" if r == 0 else "neg_bwd").unsqueeze(1).to_broadcast([P, NT, P])
                        dve.tensor_tensor(chunk(att[r]), chunk(ub[r]), neg, ALU.add).then_inc(s["masked"], 1)
                    dve.wait_ge(s["kT"], h + 1)
                    for r in range(2):
                        dve.tensor_tensor(chunk(kw[r]), chunk(K.ps[:, 0:T]), w_st[:, r, :, bass.ds(h, 1)].to_broadcast([P, NT, P]),
                                          ALU.mult).then_inc(s["kw"], 1)
                    state = Steps(dve, s["states"], h, N_STATES)
                    dve.wait_ge(s["st_in"], h * 64 + 64)
                    dve.wait_ge(s["small_in"], h * 16 + 16)
                    dve.wait_ge(s["C_out"], h * 64 + 64)
                    for n in range(NT):
                        if n % PER_BANK == 0:
                            dve.wait_ge(s["kv"], h * 3 + n // PER_BANK + 1)
                        for r in range(2):
                            a = KV[r] + n % PER_BANK * F1
                            c = chunk_of(r, n)
                            if n == NS:
                                state.did(dve.tensor_copy(C[r][:, NS + 1], K.ps[:, a:a + F1]))
                            else:
                                if n:
                                    dve.wait_ge(s["states"], h * N_STATES + (state.k - 1))
                                state.did(dve.scalar_tensor_tensor(C[r][:, n + 1], C[r][:, n], small[:, 1, r, c:c + 1], K.ps[:, a:a + F1],
                                                                   ALU.mult, ALU.add))
                    state.close()
                    dve.wait_ge(s["sc_out"], h + 1)
                    for r in range(2):
                        dve.wait_ge(s["exped"], h * 4 + 2 * r + 2)
                        dve.tensor_tensor(qw[r], qw[r], qc, ALU.mult)
                        dve.tensor_tensor(att[r], att[r], sc, ALU.mult).then_inc(s["att"], 1)
                    if more:
                        dve.wait_ge(s["att"], h * 2 + 2)
                        convolve(h + 1)
                    step = Steps(dve, s["steps"], h, 2 * 5 + 2)
                    hs4 = hs.rearrange("p (b j f) -> p b j f", b=3, f=P)
                    for r in range(2):
                        dve.wait_ge(s["num"], h * 2 + r + 1)
                        dn = by_bank(den[:, r])
                        step.did(dve.tensor_copy(dn, nums(r)[:, :, :, P]))
                        step.wait()
                        step.did(dve.scalar_tensor_tensor(dn, dn, -1.0, dn, ALU.mult, ALU.max))
                        step.wait()
                        step.did(dve.tensor_tensor(den[:, r], den[:, r], K.em_cols[:, r, :, bass.ds(h, 1)].rearrange("p c a -> p (c a)"), ALU.max))
                        step.wait()
                        step.did(dve.reciprocal(den[:, r], den[:, r]))
                        step.wait()
                        if r == 0:
                            step.did(dve.tensor_tensor(hs4, nums(0)[:, :, :, 0:P], dn.unsqueeze(3).to_broadcast([P, 3, PER_BANK, P]), ALU.mult))
                        else:
                            for c in range(NT):
                                ins = dve.scalar_tensor_tensor(hs[:, cols(c)], num(1, c)[:, 0:P], den[:, 1, c:c + 1], hs[:, cols(c)],
                                                               ALU.mult, ALU.add)
                            step.did(ins)
                        step.wait()
                        dve.sem_inc(s["read"], 1)
                    dve.wait_ge(s["root"], h * 2 + 2)
                    step.did(dve.reciprocal(rms[:, 2], rms[:, 1]))
                    step.wait()
                    step.did(dve.tensor_tensor(chunk(hs), chunk(hs), rms[:, 2].unsqueeze(2).to_broadcast([P, NT, P]), ALU.mult))
                    step.wait()
                    step.close()
                    dve.sem_inc(s["normed"], 1)
                    dve.wait_ge(s["sig"], h + 1)
                    dve.wait_ge(s["h_turned"], h + 1)
                    dve.scalar_tensor_tensor(K.hT[:, bass.ds(h + 4, 1), :].rearrange("p a t -> p (a t)"), K.ps[:, 0:T],
                                             K.par[:, bass.ds(h + PARAMS["g_mlstm"][0], 1)], sg, ALU.mult, ALU.mult).then_inc(s["done"], 1)
                over_heads(dve, head)


def stage_out(K, l):
    nc = K.nc
    at = AT_OUT[l]
    with ExitStack() as ctx:
        def sb(name, shape):
            return ctx.enter_context(nc.sbuf_tensor(f"out{l}_{name}", shape, F32))
        s = K.sems(f"out{l}", "x_in0", "x_in1", "gate_in", "product", "gated", "x_new", "x_stored0", "x_stored1", "sumsq",
                   "root", "rcp", "xn_ready", "turned", "act_evac", "dve_evac", "xn_stored0", "xn_stored1")
        x_in, x_stored, xn_stored = [s["x_in0"], s["x_in1"]], [s["x_stored0"], s["x_stored1"]], [s["xn_stored0"], s["xn_stored1"]]
        xt, xn = sb("x", [P, 2, D]), sb("xn", [P, 2, D])
        tmp, junk = sb("tmp", [P, 2, D]), sb("junk", [P, D])
        gate = sb("gate", [P, STREAMS, D])
        st = sb("stat", [P, 2, 4])
        TURN = 4 * PIECE
        shift_at = l * 48 + 3 * KT
        with nc.Block() as block:
            @block.gpsimd
            def _(pool):
                for r in range(STREAMS):
                    pool.dma_start(gate[:, r], K.gate1_rows[l, r:r + 1].to_broadcast([P, D])).then_inc(s["gate_in"], 16)

                def body(tiles, r):
                    for t, b, u in tiles:
                        pool.wait_ge(s["xn_ready"], t + 1)
                        pool.wait_ge(x_stored[b], u * 16 + 16)
                        pool.dma_start(xt[:, b], K.xres[bass.ds(t * P, P), :]).then_inc(x_in[b], 16)
                over_tiles(pool, body)

            @block.sync
            def _(sp):
                def body(tiles, r):
                    for t, b, u in tiles:
                        sp.wait_ge(s["x_new"], t + 1)
                        sp.dma_start(K.xres[bass.ds(t * P, P), :], xt[:, b]).then_inc(x_stored[b], 16)
                    for t, b, u in tiles:
                        sp.wait_ge(s["xn_ready"], t + 3)
                        sp.dma_start(K.xnorm[bass.ds(t * P, P), :], xn[:, b]).then_inc(xn_stored[b], 16)
                for sem in x_stored + xn_stored:
                    sp.sem_inc(sem, 16)
                for i in range(SLOTS - 2):
                    load_piece(K, sp, AT_EXPERTS[l] + i)
                over_tiles(sp, body)
                for i in range(2):
                    load_piece(K, sp, at + SLOTS + i)
                for sems in (x_stored, xn_stored):
                    sp.wait_ge(sems[0], 16 + 16 * 5)
                    sp.wait_ge(sems[1], 16 + 16 * 4)

            @block.scalar
            def _(act):
                def body(tiles, r):
                    for t, b, u in tiles:
                        act.wait_ge(s["x_new"], t + 1)
                        act.activation(junk[:], xt[:, b], ACT.Square, accum_out=st[:, b, 0:1]).then_inc(s["sumsq"], 1)
                        act.wait_ge(s["sumsq"], t + 1)
                        act.activation(st[:, b, 1:2], st[:, b, 0:1], ACT.Sqrt, bias=K.eps[:], scale=1.0 / D).then_inc(s["root"], 1)
                    for t, b, u in tiles:
                        act.wait_ge(s["turned"], t + 3)
                        for k in range(KT // 2):
                            a = TURN + b * D + k * P
                            ins = act.activation(K.hT[:, k, bass.ds(t * P, P)], K.ps[:, a:a + P], ACT.Identity,
                                                 bias=K.ada[:, r, shift_at + k:shift_at + k + 1], scale=K.scale[:, l, 1, r, k:k + 1])
                        ins.then_inc(s["act_evac"], 1)
                act.sem_inc(s["act_evac"], 2)
                over_tiles(act, body)

            @block.tensor
            def _(pe):
                pe.sem_inc(s["turned"], 2)

                def product(t):
                    b = t % 2
                    pe.wait_ge(s["gated"], t + 1)
                    for c in range(2):
                        if t == 0:
                            wait_piece(K, pe, at + c)
                        for k in range(KT):
                            mm = pe.matmul(K.ps[:, b * D + c * PIECE:b * D + (c + 1) * PIECE], K.hT[:, k, t * P:(t + 1) * P],
                                           K.W[:, (at + c) % SLOTS, k], start=(k == 0), stop=(k == KT - 1))
                    mm.then_inc(s["product"], 1)

                def turn(t):
                    b = t % 2
                    pe.wait_ge(s["xn_ready"], t + 3)
                    pe.wait_ge(s["act_evac"], t + 1)
                    pe.wait_ge(s["dve_evac"], t + 1)
                    for k in range(KT):
                        a = TURN + b * D + k * P
                        mm = pe.transpose(K.ps[:, a:a + P], xn[:, b, k * P:(k + 1) * P], K.c("ident"))
                    mm.then_inc(s["turned"], 1)
                product(0)
                product(1)
                for t in range(NT):
                    if t + 2 < NT:
                        product(t + 2)
                    if t + 2 == NT:
                        pe.drain().then_inc(K.w_used, 2)
                    turn(t)

            @block.vector
            def _(dve):
                def body(tiles, r):
                    for t, b, u in tiles:
                        dve.wait_ge(s["product"], t + 1)
                        dve.tensor_tensor(tmp[:, b], K.ps[:, b * D:(b + 1) * D], gate[:, r], ALU.mult).then_inc(s["gated"], 1)
                        dve.wait_ge(s["gated"], t + 3)
                        dve.wait_ge(x_in[b], u * 16 + 16)
                        dve.tensor_tensor(xt[:, b], xt[:, b], tmp[:, b], ALU.add).then_inc(s["x_new"], 1)
                    for t, b, u in tiles:
                        dve.wait_ge(s["root"], t + 1)
                        dve.reciprocal(st[:, b, 2:3], st[:, b, 1:2]).then_inc(s["rcp"], 1)
                        dve.wait_ge(s["rcp"], t + 1)
                        dve.wait_ge(s["turned"], t + 1)
                        dve.wait_ge(xn_stored[b], u * 16 + 16)
                        dve.tensor_scalar(xn[:, b], xt[:, b], st[:, b, 2:3], None, ALU.mult).then_inc(s["xn_ready"], 1)
                    for t, b, u in tiles:
                        dve.wait_ge(s["turned"], t + 3)
                        for k in range(KT // 2, KT):
                            a = TURN + b * D + k * P
                            ins = dve.tensor_scalar(K.hT[:, k, bass.ds(t * P, P)], K.ps[:, a:a + P], K.scale[:, l, 1, r, k:k + 1],
                                                    K.ada[:, r, shift_at + k:shift_at + k + 1], ALU.mult, ALU.add)
                        ins.then_inc(s["dve_evac"], 1)
                dve.sem_inc(s["xn_ready"], 2)
                dve.sem_inc(s["dve_evac"], 2)
                dve.sem_inc(s["gated"], 2)
                dve.wait_ge(s["gate_in"], 32)
                over_tiles(dve, body)


def stage_route(K, l):
    nc = K.nc
    E = EXPERTS
    with ExitStack() as ctx:
        def sb(name, shape, dt=F32):
            return ctx.enter_context(nc.sbuf_tensor(f"route{l}_{name}", shape, dt))
        s = K.sems(f"route{l}", "logits", "steps", "less_max", "exped", "aff", "affT", "picked", "columns")
        e, st = sb("e", [P, NT, E]), sb("stat", [P, 3, NT])
        aff = sb("aff", [E, T])
        val, idx = sb("val", [E, CAP]), sb("idx", [E, CAP], U32)
        idxf = sb("idxf", [E, CAP])
        with nc.Block() as block:
            @block.tensor
            def _(pe):
                for t in range(NT):
                    for k in range(KT):
                        mm = pe.matmul(K.ps[:, t * E:(t + 1) * E], K.hT[:, k, t * P:(t + 1) * P], K.w_router[:, l, k],
                                       start=(k == 0), stop=(k == KT - 1))
                mm.then_inc(s["logits"], 1)
                pe.wait_ge(s["aff"], 1)
                for t in range(NT):
                    mm = pe.transpose(K.ps[0:E, PIECE + t * P:PIECE + (t + 1) * P], e[:, t], K.c("ident"))
                mm.then_inc(s["affT"], 1)
                pe.wait_ge(s["picked"], 1)
                idn = K.cst[0:E, 0:E]
                for n, src in enumerate((idxf, val)):
                    pe.transpose(K.ps[:, n * E:(n + 1) * E], src[:, 0:CAP_S], idn)
                    mm = pe.transpose(K.ps[0:CAP_P, 64 + n * E:64 + (n + 1) * E], src[:, CAP_S:CAP], idn)
                mm.then_inc(s["columns"], 1)

            @block.scalar
            def _(act):
                act.wait_ge(s["less_max"], 1)
                act.activation(e[:], e[:], ACT.Exp).then_inc(s["exped"], 1)

            @block.vector
            def _(dve):
                step = Steps(dve, s["steps"])
                logits = K.ps[:, 0:NT * E].rearrange("p (t e) -> p t e", e=E)

                def wide(i):
                    return st[:, i].unsqueeze(2).to_broadcast([P, NT, E])
                dve.wait_ge(s["logits"], 1)
                step.did(dve.tensor_reduce(st[:, 0], logits, AX_X, ALU.max))
                step.wait()
                dve.tensor_tensor(e[:], logits, wide(0), ALU.subtract).then_inc(s["less_max"], 1)
                dve.wait_ge(s["exped"], 1)
                step.did(dve.tensor_reduce(st[:, 1], e[:], AX_X, ALU.add))
                step.wait()
                step.did(dve.reciprocal(st[:, 2], st[:, 1]))
                step.wait()
                dve.tensor_tensor(e[:], e[:], wide(2), ALU.mult).then_inc(s["aff"], 1)
                dve.wait_ge(s["affT"], 1)
                step.did(dve.tensor_copy(aff[:], K.ps[0:E, PIECE:PIECE + T]))
                step.wait()
                for at, cap, lo, hi in ((0, CAP_S, 0, T_S), (CAP_S, CAP_P, T_S, T)):
                    for n in range(at, at + cap, 8):
                        step.did(dve.max(val[:, n:n + 8], aff[:, lo:hi]))
                        step.wait()
                        step.did(dve.max_index(idx[:, n:n + 8], val[:, n:n + 8], aff[:, lo:hi]))
                        step.wait()
                        if n + 8 < at + cap:
                            step.did(dve.match_replace(aff[:, lo:hi], val[:, n:n + 8], aff[:, lo:hi], -1.0))
                            step.wait()
                step.did(dve.tensor_copy(idxf[:, 0:CAP_S], idx[:, 0:CAP_S]))
                step.did(dve.tensor_scalar(idxf[:, CAP_S:CAP], idx[:, CAP_S:CAP], float(T_S), None, ALU.add))
                step.wait()
                dve.sem_inc(s["picked"], 1)
                dve.wait_ge(s["columns"], 1)
                step.did(dve.tensor_copy(K.idx_s[:], K.ps[:, 0:E]))
                step.did(dve.tensor_copy(K.gate_s[:], K.ps[:, E:2 * E]))
                step.did(dve.tensor_copy(K.idx_p[:], K.ps[0:CAP_P, 64:64 + E]))
                step.did(dve.tensor_copy(K.gate_p[:], K.ps[0:CAP_P, 64 + E:64 + 2 * E]))
                step.wait()


def stage_experts(K, l):
    nc = K.nc
    at = AT_EXPERTS[l]
    E = EXPERTS
    GU = [0, PIECE]
    DN = [2 * PIECE, 3 * PIECE]
    TR = 4 * PIECE
    with ExitStack() as ctx:
        def sb(name, shape, dt=F32):
            return ctx.enter_context(nc.sbuf_tensor(f"moe{l}_{name}", shape, dt))
        s = K.sems(f"moe{l}", "idx_g", "idx_s", "xs_in", "xp_in", "x_turned", "xT", "xT2", "gate", "up", "silu", "hid",
                   "down", "y_act", "y_dve", "y_turned", "ys_out", "yp_out", "ys_added", "yp_added", "added", "order")
        xs, xp = sb("xs", [CAP_S, D]), sb("xp", [CAP_P, D])
        xT, hid, yT = sb("xT", [P, KT, CAP]), sb("hid", [P, KT, CAP]), sb("yT", [P, KT, CAP])
        sg = sb("silu", [P, 2, CAP])
        ys, yp = sb("ys", [CAP_S, D]), sb("yp", [CAP_P, D])
        ig, ipg = sb("ig", [P, 1], I32), sb("ipg", [CAP_P, 1], I32)
        isc, ips = sb("is", [P, 1], I32), sb("ips", [CAP_P, 1], I32)
        shift_at, gate2_at = l * 48 + 3 * KT, l * 48 + 5 * KT

        def turned_x(k):
            return TR + (k // 3) * PIECE + (k % 3) * CAP

        def turn_x(pe, e):
            pe.wait_ge(s["xs_in"], e * 16 + 16)
            pe.wait_ge(s["xp_in"], e * 16 + 16)
            for k in range(KT):
                a = turned_x(k)
                pe.transpose(K.ps[:, a:a + CAP_S], xs[:, k * P:(k + 1) * P], K.c("ident"))
                mm = pe.transpose(K.ps[:, a + CAP_S:a + CAP], xp[:, k * P:(k + 1) * P], K.cst[0:CAP_P, 0:CAP_P])
            mm.then_inc(s["x_turned"], 1)

        def turn_y(pe, e):
            pe.wait_ge(s["y_act"], e * KT + KT)
            for k in range(KT):
                pe.transpose(K.ps[:, TR + k * P:TR + (k + 1) * P], yT[:, k, 0:CAP_S], K.c("ident"))
            for k in range(KT):
                mm = pe.transpose(K.ps[0:CAP_P, TR + D + k * P:TR + D + (k + 1) * P], yT[:, k, CAP_S:CAP], K.c("ident"))
            mm.then_inc(s["y_turned"], 1)

        def experts(eng, body):
            body(0, False, True)
            with eng.Fori(1, E - 1) as e:
                body(e, True, True)
            body(E - 1, True, False)

        with nc.Block() as block:
            @block.sync
            def _(sp):
                def used(i, e):
                    if i < 4:
                        sp.wait_ge(s["up"], e * KT + 4 * (i // 2 + 1))
                    else:
                        sp.wait_ge(s["down"], e * KT + 4 * (i - 3))
                with sp.Fori(0, E - 1) as e:
                    for i in range(SLOTS):
                        used(i, e)
                        w = (K.d["w_gate_e"], K.d["w_up_e"], K.d["w_gate_e"], K.d["w_up_e"], K.d["w_down_e"], K.d["w_down_e"])[i]
                        c = (0, 0, 1, 1, 0, 1)[i]
                        src = w[l, bass.ds(e + 1, 1)].rearrange("a (k p) f -> p (a k) f", p=P)[:, :, c * PIECE:(c + 1) * PIECE]
                        sp.dma_start(K.W[:, (at + i) % SLOTS], src).then_inc(K.w_loaded[(at + i) % SLOTS], 16)
                for i in range(SLOTS):
                    n = at + E * SLOTS + i
                    if n < len(K.pieces):
                        used(i, E - 1)
                        sp.dma_start(K.W[:, n % SLOTS], K.pieces[n]).then_inc(K.w_loaded[n % SLOTS], 16)

            @block.gpsimd
            def _(pool):
                pool.sem_inc(s["added"], 1)

                def gather(e):
                    pool.tensor_copy(ig[:], K.idx_s[:, bass.ds(e, 1)]).then_inc(s["idx_g"], 1)
                    pool.tensor_copy(ipg[:], K.idx_p[:, bass.ds(e, 1)]).then_inc(s["idx_g"], 1)
                    pool.wait_ge(s["idx_g"], e * 2 + 2)
                    pool.sem_inc(s["order"], 1)
                    pool.indirect_dma_start(xs[:], None, K.xnorm, bass.IndirectOffsetOnAxis(ig[:, 0:1], 0)).then_inc(s["xs_in"], 16)
                    pool.indirect_dma_start(xp[:], None, K.xnorm, bass.IndirectOffsetOnAxis(ipg[:, 0:1], 0)).then_inc(s["xp_in"], 16)

                def add(e):
                    pool.tensor_copy(isc[:], K.idx_s[:, bass.ds(e, 1)]).then_inc(s["idx_s"], 1)
                    pool.tensor_copy(ips[:], K.idx_p[:, bass.ds(e, 1)]).then_inc(s["idx_s"], 1)
                    pool.wait_ge(s["idx_s"], e * 2 + 2)
                    pool.wait_ge(s["ys_out"], e + 1 + 1)
                    pool.sem_inc(s["order"], 1)
                    pool.indirect_dma_start(K.xres, bass.IndirectOffsetOnAxis(isc[:, 0:1], 0), ys[:], None,
                                            compute_op=ALU.add).then_inc(s["ys_added"], 16)
                    pool.wait_ge(s["yp_out"], e + 1 + 1)
                    pool.sem_inc(s["order"], 1)
                    pool.indirect_dma_start(K.xres, bass.IndirectOffsetOnAxis(ips[:, 0:1], 0), yp[:], None,
                                            compute_op=ALU.add).then_inc(s["yp_added"], 16)
                    pool.wait_ge(s["ys_added"], e * 16 + 16)
                    pool.wait_ge(s["yp_added"], e * 16 + 16)
                    pool.sem_inc(s["added"], 1)

                def body(e, before, after):
                    if after:
                        pool.wait_ge(s["x_turned"], e + 1)
                        gather(e + 1)
                    if before:
                        add(e - 1)
                gather(0)
                experts(pool, body)
                add(E - 1)

            @block.tensor
            def _(pe):
                def column_tile(e, ft):
                    half, col = ft // 4, (ft % 4) * P
                    pe.wait_ge(s["hid"], e * KT + max(ft - 1, 0) + 1)
                    for j in range(2):
                        n = at + 2 * half + j
                        slot = n % SLOTS
                        if ft % 4 == 0:
                            pe.wait_ge(K.w_loaded[slot], e * 16 + 16 * (n // SLOTS + 1))
                        a = GU[ft % 2] + j * CAP
                        for k in range(KT):
                            mm = pe.matmul(K.ps[:, a:a + CAP], K.W[:, slot, k, col:col + P], xT[:, k, :],
                                           start=(k == 0), stop=(k == KT - 1))
                    mm.then_inc(s["up"], 1)

                def body(e, before, after):
                    pe.wait_ge(s["xT"], e + 1)
                    pe.wait_ge(s["xT2"], e + 1)
                    column_tile(e, 0)
                    if before:
                        turn_y(pe, e - 1)
                    for ft in range(1, KT):
                        column_tile(e, ft)
                    if after:
                        pe.wait_ge(s["ys_out"], e + 1)
                        pe.wait_ge(s["yp_out"], e + 1)
                        turn_x(pe, e + 1)
                    pe.wait_ge(s["hid"], e * KT + KT + 1)
                    for dt in range(KT):
                        n = at + 4 + dt // 4
                        slot, col = n % SLOTS, (dt % 4) * P
                        if dt % 4 == 0:
                            pe.wait_ge(K.w_loaded[slot], e * 16 + 16 * (n // SLOTS + 1))
                        if dt >= 2:
                            pe.wait_ge(s["y_act"], e * KT + dt - 1)
                        for k in range(KT):
                            mm = pe.matmul(K.ps[:, DN[dt % 2]:DN[dt % 2] + CAP], K.W[:, slot, k, col:col + P], hid[:, k, :],
                                           start=(k == 0), stop=(k == KT - 1))
                        mm.then_inc(s["down"], 1)
                turn_x(pe, 0)
                experts(pe, body)
                turn_y(pe, E - 1)
                pe.drain().then_inc(K.w_used, E * SLOTS)

            @block.scalar
            def _(act):
                act.sem_inc(s["ys_out"], 1)

                def modulate(e):
                    act.wait_ge(s["x_turned"], e + 1)
                    for k in range(3, 6):
                        for r, (lo, hi) in enumerate(((0, CAP_S), (CAP_S, CAP))):
                            a = turned_x(k)
                            ins = act.activation(xT[:, k, lo:hi], K.ps[:, a + lo:a + hi], ACT.Identity,
                                                 bias=K.ada[:, r, shift_at + k:shift_at + k + 1], scale=K.scale[:, l, 1, r, k:k + 1])
                    ins.then_inc(s["xT"], 1)

                def weighted(e):
                    act.wait_ge(s["y_turned"], e + 1)
                    act.wait_ge(s["added"], e + 1)
                    act.activation(ys[:], K.ps[:, TR:TR + D], ACT.Copy, scale=K.gate_s[:, bass.ds(e, 1)]).then_inc(s["ys_out"], 1)

                def body(e, before, after):
                    for ft in range(KT):
                        act.wait_ge(s["up"], e * KT + (ft + 1))
                        if ft >= 2:
                            act.wait_ge(s["hid"], e * KT + (ft - 1) + 1)
                        act.activation(sg[:, ft % 2], K.ps[:, GU[ft % 2]:GU[ft % 2] + CAP], ACT.Silu).then_inc(s["silu"], 1)
                        if ft == 1 and before:
                            weighted(e - 1)
                    if after:
                        modulate(e + 1)
                    for dt in range(KT):
                        act.wait_ge(s["down"], e * KT + (dt + 1))
                        for r, (lo, hi) in enumerate(((0, CAP_S), (CAP_S, CAP))):
                            ins = act.activation(yT[:, dt, lo:hi], K.ps[:, DN[dt % 2] + lo:DN[dt % 2] + hi], ACT.Copy,
                                                 scale=K.ada[:, r, gate2_at + dt:gate2_at + dt + 1])
                        ins.then_inc(s["y_act"], 1)
                modulate(0)
                experts(act, body)
                weighted(E - 1)

            @block.vector
            def _(dve):
                dve.sem_inc(s["hid"], 1)
                dve.sem_inc(s["yp_out"], 1)

                def modulate(e):
                    dve.wait_ge(s["x_turned"], e + 1)
                    for k in (0, 1, 2, 6, 7):
                        for r, (lo, hi) in enumerate(((0, CAP_S), (CAP_S, CAP))):
                            a = turned_x(k)
                            ins = dve.tensor_scalar(xT[:, k, lo:hi], K.ps[:, a + lo:a + hi], K.scale[:, l, 1, r, k:k + 1],
                                                    K.ada[:, r, shift_at + k:shift_at + k + 1], ALU.mult, ALU.add)
                    ins.then_inc(s["xT2"], 1)

                def weighted(e):
                    dve.wait_ge(s["y_turned"], e + 1)
                    dve.wait_ge(s["added"], e + 1)
                    dve.tensor_scalar(yp[:], K.ps[0:CAP_P, TR + D:TR + 2 * D], K.gate_p[:, bass.ds(e, 1)], None,
                                      ALU.mult).then_inc(s["yp_out"], 1)

                def body(e, before, after):
                    for ft in range(KT):
                        dve.wait_ge(s["silu"], e * KT + (ft + 1))
                        a = GU[ft % 2] + CAP
                        dve.tensor_tensor(hid[:, ft], sg[:, ft % 2], K.ps[:, a:a + CAP], ALU.mult).then_inc(s["hid"], 1)
                        if ft == 1 and before:
                            weighted(e - 1)
                    if after:
                        modulate(e + 1)
                modulate(0)
                experts(dve, body)
                weighted(E - 1)


def stage_final(K):
    nc, d = K.nc, K.d
    with ExitStack() as ctx:
        def sb(name, shape):
            return ctx.enter_context(nc.sbuf_tensor(f"fin_{name}", shape, F32))
        s = K.sems("fin", "x_in0", "x_in1", "g_in", "sumsq", "root", "rcp", "y", "stored0", "stored1")
        x_in, stored = [s["x_in0"], s["x_in1"]], [s["stored0"], s["stored1"]]
        xt, y, g = sb("x", [P, 2, D]), sb("y", [P, 2, D]), sb("g", [P, D])
        junk, st = sb("junk", [P, D]), sb("stat", [P, 2, 4])
        with nc.Block() as block:
            @block.gpsimd
            def _(pool):
                pool.dma_start(g[:], d["g_final"].unsqueeze(0).to_broadcast([P, D])).then_inc(s["g_in"], 16)

                def body(tiles, r):
                    for t, b, u in tiles:
                        pool.wait_ge(s["y"], t + 1)
                        pool.dma_start(xt[:, b], K.xres[bass.ds(t * P, P), :]).then_inc(x_in[b], 16)
                over_tiles(pool, body)

            @block.sync
            def _(sp):
                for sem in stored:
                    sp.sem_inc(sem, 16)

                def body(tiles, r):
                    for t, b, u in tiles:
                        sp.wait_ge(s["y"], t + 3)
                        dst = d["o_y_prompt"][0] if r else d["o_y_sample"][0, bass.ds(t * P, P), :]
                        sp.dma_start(dst, y[:, b]).then_inc(stored[b], 16)
                over_tiles(sp, body)
                sp.wait_ge(stored[0], 16 + 16 * 5)
                sp.wait_ge(stored[1], 16 + 16 * 4)

            @block.scalar
            def _(act):
                def body(tiles, r):
                    for t, b, u in tiles:
                        act.wait_ge(x_in[b], u * 16 + 16)
                        act.activation(junk[:], xt[:, b], ACT.Square, accum_out=st[:, b, 0:1]).then_inc(s["sumsq"], 1)
                        act.wait_ge(s["sumsq"], t + 1)
                        act.activation(st[:, b, 1:2], st[:, b, 0:1], ACT.Sqrt, bias=K.eps[:], scale=1.0 / D).then_inc(s["root"], 1)
                over_tiles(act, body)

            @block.vector
            def _(dve):
                dve.sem_inc(s["y"], 2)
                dve.wait_ge(s["g_in"], 16)

                def body(tiles, r):
                    for t, b, u in tiles:
                        dve.wait_ge(s["root"], t + 1)
                        dve.reciprocal(st[:, b, 2:3], st[:, b, 1:2]).then_inc(s["rcp"], 1)
                        dve.wait_ge(s["rcp"], t + 1)
                        dve.wait_ge(stored[b], u * 16 + 16)
                        dve.scalar_tensor_tensor(y[:, b], xt[:, b], st[:, b, 2:3], g[:], ALU.mult, ALU.mult).then_inc(s["y"], 1)
                over_tiles(dve, body)
def stage_hgrn(K):
    nc, d = K.nc, K.d
    NSTATE = NS + 2
    N_STATE_STEPS = 2 * NS + 1
    with ExitStack() as ctx:
        def sb(name, shape):
            return ctx.enter_context(nc.sbuf_tensor(f"hg_{name}", shape, F32))[:]
        s = K.sems("hg", "f_in", "q_in", "v_in", "g_in", "st_in", "bias", "lb", "sig", "scaled", "level", "asm", "k_next",
                   "q_next", "t_next", "merged", "kT", "ktok", "kv", "states", "S_out", "out_ctx", "out", "o_out", "sq",
                   "ssum", "root", "silu", "norm", "spread", "modulated", "done", "order")
        in_ring = free_slots(K, AT_OUT[1])

        def directions(t):
            return t.rearrange("p (r t) -> p r t", r=2)
        G = [sb("G", [P, 2, T]), directions(in_ring(2 * T))]
        Kx = [sb("K", [P, 2, T]), directions(in_ring(2 * T))]
        Qx = [sb("Q", [P, 2, T]), directions(in_ring(2 * T))]
        att = [in_ring(T), in_ring(T)]
        A = [sb("A", [P, T]), in_ring(T)]
        O, SQ = in_ring(T), in_ring(T)
        g, v = in_ring(T), in_ring(T).rearrange("p (c f) -> p c f", f=P)
        q = sb("q", [P, T])
        S = sb("S", [P, 2, NSTATE, P])
        lens = [T >> i for i in range(LEVELS + 1)]
        Tl = [None] + [sb(f"T{i}", [P, 2, lens[i]]) for i in range(1, LEVELS + 1)]
        lb = sb("lb", [P, 4, HEADS_C])
        nbf = sb("nbf", [P, 2 * HEADS_C])
        rms = sb("rms", [P, 2, NT])
        R = [0, 3 * PIECE]
        TAIL = 6 * PIECE
        bf_at = PARAMS["b_f"][0]
        FULL = NS * P

        def blocks(t, m, lo, n):
            return bass.AP(t.tensor, t.offset + lo, [list(t.ap[0]), [2 * m, n // (2 * m)], [T + m, 2], [1, m]])

        def factors(t, i, start, pair_step, j_step):
            m = 1 << i
            return bass.AP(t.tensor, t.offset + start, [list(t.ap[0]), [pair_step, T // (2 * m)], [j_step, 2], [0, m]])

        def cols(c):
            return slice(c * P, (c + 1) * P)

        def chunk_of(r, k):
            return k if r == 0 else NS - 1 - k

        def run(eng, levels, tail):
            levels(0, 0, 0, None, True)
            with eng.Fori(0, HEADS_C // 2 - 1) as i:
                levels(i * 2 + 1, i + 4, 1, tail(i * 2, i, 0), True)
                levels(i * 2 + 2, i + 1, 0, tail(i * 2 + 1, i + 4, 1), True)
            levels(HEADS_C - 1, HEADS_C - 1, 1, tail(HEADS_C - 2, 3, 0), False)
            last = tail(HEADS_C - 1, HEADS_C - 1, 1)
            for k in range(LEVELS):
                last(k)

        def next_head(n, h, b):
            return h + 4 if b == 0 else h - 3

        with nc.Block() as block:
            @block.gpsimd
            def _(pool):
                def load_f(h, b):
                    for r in range(2):
                        pool.dma_start(G[b][:, r], K.featT[bass.ds(h + (16 + 8 * r), 1)].rearrange("a p t -> (a p) t")).then_inc(s["f_in"], 16)

                def load_q(h):
                    pool.dma_start(q, K.featT[bass.ds(h, 1)].rearrange("a p t -> (a p) t")).then_inc(s["q_in"], 16)

                def levels(n, h, b, tail, more):
                    if more:
                        pool.wait_ge(s["level"], n * (LEVELS + 1) + 1)
                        pool.wait_ge(s["q_next"], n * (LEVELS + 1) + 1)
                        load_q(next_head(n, h, b))
                        if tail:
                            pool.wait_ge(s["kv"], n * 3)
                        load_f(next_head(n, h, b), 1 - b)
                    if tail:
                        pool.wait_ge(s["out"], n)
                    pool.dma_start(v, K.tok.rearrange("n t p f -> n p t f")[b, :, :, bass.ds((h - 4 * b) * P, P)]).then_inc(s["v_in"], 16)
                    if tail:
                        pool.wait_ge(s["done"], n + 1)
                    pool.dma_start(g, K.featT[bass.ds(h + 8, 1)].rearrange("a p t -> (a p) t")).then_inc(s["g_in"], 16)
                load_f(0, 0)
                load_q(0)
                run(pool, levels, lambda n, h, b: lambda k: None)

            @block.sync
            def _(sp):
                sp.sem_inc(s["S_out"], 32)

                def levels(n, h, b, tail, more):
                    if tail:
                        tail(2)
                        sp.wait_ge(s["out"], n)
                    for r in range(2):
                        sp.dma_start(S[:, r, 0], d["state_hgrn_S"][0, 0, r, bass.ds(h, 1)].rearrange("a k v -> (a k) v")).then_inc(s["st_in"], 16)

                def tail(n, h, b):
                    def one(k):
                        if k == 2:
                            sp.wait_ge(s["states"], n * N_STATE_STEPS + N_STATE_STEPS)
                            for r in range(2):
                                sp.dma_start(d["o_new_S"][0, 0, r, bass.ds(h, 1)].rearrange("a k v -> (a k) v"),
                                             S[:, r, NS + 1]).then_inc(s["S_out"], 16)
                    return one
                run(sp, levels, tail)
                sp.wait_ge(s["S_out"], 32 * HEADS_C + 32)

            @block.scalar
            def _(act):
                act.wait_ge(s["lb"], 1)
                act.activation(lb[:, 1], lb[:, 0], ACT.Sigmoid).then_inc(s["lb"], 1)
                act.wait_ge(s["lb"], 3)

                def prepare(n, h, b, r):
                    act.activation(Kx[b][:, r], G[b][:, r], ACT.Sigmoid, scale=-1.0, bias=nbf[:, bass.ds(h + 8 * r, 1)])
                    act.activation(G[b][:, r], G[b][:, r], ACT.Sigmoid, bias=K.par[:, bass.ds(h + (bf_at + 8 * r), 1)]).then_inc(s["sig"], 1)
                    act.wait_ge(s["sig"], n * 2 + (r + 1))
                    act.sem_inc(s["order"], 1)
                    act.activation(Kx[b][:, r], Kx[b][:, r], ACT.Identity, scale=lb[:, 2, bass.ds(h, 1)]).then_inc(s["scaled"], 1)
                    act.activation(G[b][:, r], G[b][:, r], ACT.Identity, scale=lb[:, 2, bass.ds(h, 1)],
                                   bias=lb[:, 1, bass.ds(h, 1)]).then_inc(s["scaled"], 1)

                def levels(n, h, b, tail, more):
                    for i in range(LEVELS):
                        if i:
                            act.wait_ge(s["k_next"], n * LEVELS + i)
                        else:
                            act.wait_ge(s["scaled"], n * 4 + 4)
                        if i > 1:
                            act.wait_ge(s["level"], n * (LEVELS + 1) + i)
                        elif tail:
                            act.wait_ge(s["level"], n * (LEVELS + 1))
                        act.copy(A[i % 2].rearrange("p (b j m) -> p b j m", j=2, m=1 << i), blocks(Kx[b], 1 << i, 0, T)).then_inc(s["asm"], 1)
                        if tail:
                            tail(i)
                        if more and i >= LEVELS - 2:
                            if i == LEVELS - 2:
                                act.wait_ge(s["f_in"], n * 32 + 64)
                                act.sem_inc(s["order"], 1)
                            prepare(n + 1, next_head(n, h, b), 1 - b, i - (LEVELS - 2))
                    for r in range(2):
                        act.wait_ge(s["kT"], n * 2 + r + 1)
                        act.copy(G[b][:, r], K.ps[:, R[r]:R[r] + T]).then_inc(s["ktok"], 1)

                def tail(n, h, b):
                    def one(k):
                        if k == 0:
                            act.wait_ge(s["g_in"], n * 16 + 16)
                            act.activation(g, g, ACT.Silu).then_inc(s["silu"], 1)
                        if k == 2:
                            act.wait_ge(s["out_ctx"], n + 1)
                            act.copy(O[:, FULL:], K.ps[:, TAIL + PIECE:TAIL + PIECE + P]).then_inc(s["o_out"], 1)
                        if k == 3:
                            act.wait_ge(s["out"], n + 1)
                            act.copy(O[:, 0:FULL], K.ps[:, TAIL:TAIL + FULL]).then_inc(s["o_out"], 1)
                            act.wait_ge(s["o_out"], n * 2 + 2)
                            act.activation(SQ, O, ACT.Square).then_inc(s["sq"], 1)
                        if k == 4:
                            act.wait_ge(s["ssum"], n + 1)
                            act.activation(rms[:, 0], K.ps[:, TAIL:TAIL + NT], ACT.Sqrt, bias=K.eps[:], scale=1.0 / P).then_inc(s["root"], 1)
                    return one
                act.wait_ge(s["bias"], 1)
                act.wait_ge(s["f_in"], 32)
                for r in range(2):
                    prepare(0, 0, 0, r)
                run(act, levels, tail)

            @block.tensor
            def _(pe):
                def levels(n, h, b, tail, more):
                    pe.wait_ge(s["scaled"], n * 4 + 4)
                    pe.wait_ge(s["q_in"], n * 16 + 16)
                    if tail:
                        pe.wait_ge(s["ktok"], n * 2 - 1)
                    for c in range(NT):
                        a = R[0] + c * P
                        pe.matmul(K.ps[:, a:a + P], Kx[b][:, 0, cols(c)], q[:, cols(c)], start=True, stop=False)
                        mm = pe.matmul(K.ps[:, a:a + P], Kx[b][:, 1, cols(c)], q[:, cols(c)], start=False, stop=True)
                    mm.then_inc(s["level"], 1)
                    for i in range(LEVELS):
                        pe.wait_ge(s["asm"], n * LEVELS + i + 1)
                        pe.wait_ge(s["q_next"], n * (LEVELS + 1) + i + 1)
                        if i:
                            pe.wait_ge(s["merged"], n * (LEVELS + 1) + i)
                        elif tail:
                            pe.wait_ge(s["ktok"], n * 2)
                        for c in range(NT):
                            a = R[(i + 1) % 2] + c * P
                            mm = pe.matmul(K.ps[:, a:a + P], A[i % 2][:, cols(c)], blocks(Qx[b], 1 << i, c * P, P),
                                           start=True, stop=True)
                        mm.then_inc(s["level"], 1)
                        if tail:
                            tail(i)
                    pe.wait_ge(s["k_next"], (n + 1) * LEVELS)
                    for r in range(2):
                        pe.wait_ge(s["merged"], n * (LEVELS + 1) + (LEVELS + r))
                        for c in range(NT):
                            mm = pe.transpose(K.ps[:, R[r] + c * P:R[r] + (c + 1) * P], Kx[b][:, r, cols(c)], K.c("ident"))
                        mm.then_inc(s["kT"], 1)

                def tail(n, h, b):
                    def bank(r, k):
                        a = TAIL + r * PIECE + k * P
                        return K.ps[:, a:a + P]

                    def one(k):
                        if k < 2:
                            if k == 0:
                                pe.wait_ge(s["ktok"], n * 2 + 2)
                                pe.wait_ge(s["v_in"], n * 16 + 16)
                                pe.wait_ge(s["done"], n + 1)
                            else:
                                pe.wait_ge(s["states"], n * N_STATE_STEPS + NS)
                            for r in range(2):
                                for j in range(NS // 2):
                                    c = chunk_of(r, k * NS // 2 + j)
                                    mm = pe.matmul(bank(r, j), G[b][:, r, cols(c)], v[:, c], start=True, stop=True)
                            mm.then_inc(s["kv"], 1)
                        if k == 2:
                            pe.wait_ge(s["states"], n * N_STATE_STEPS + 2 * NS)
                            for r in range(2):
                                mm = pe.matmul(bank(0, r), G[b][:, r, cols(NS)], v[:, NS], start=True, stop=True)
                            mm.then_inc(s["kv"], 1)
                            pe.wait_ge(s["merged"], (n + 1) * (LEVELS + 1))
                            pe.matmul(bank(1, 0), v[:, NS], att[b][:, cols(NS)], start=True, stop=True).then_inc(s["out_ctx"], 1)
                        if k == 3:
                            pe.wait_ge(s["states"], n * N_STATE_STEPS + N_STATE_STEPS)
                            pe.wait_ge(s["o_out"], n * 2 + 1)
                            pe.wait_ge(s["q_next"], (n + 1) * (LEVELS + 1))
                            for c in range(NS):
                                pe.matmul(bank(0, c), S[:, 0, c], Qx[b][:, 1, cols(c)], start=True, stop=False)
                                pe.matmul(bank(0, c), S[:, 1, NS - 1 - c], Qx[b][:, 0, cols(c)], start=False, stop=False)
                                mm = pe.matmul(bank(0, c), v[:, c], att[b][:, cols(c)], start=False, stop=True)
                            mm.then_inc(s["out"], 1)
                        if k == 4:
                            pe.wait_ge(s["sq"], n + 1)
                            for c in range(NT):
                                mm = pe.matmul(K.ps[:, TAIL + c:TAIL + c + 1], SQ[:, cols(c)], K.c("ones")[:, 0:1], start=True, stop=True)
                            mm.then_inc(s["ssum"], 1)
                        if k == 5:
                            pe.wait_ge(s["norm"], n * 3 + 3)
                            for c in range(2):
                                mm = pe.matmul(K.ps[:, TAIL + c * PIECE:TAIL + (c + 1) * PIECE], K.c("ones"),
                                               SQ[:, c * PIECE:(c + 1) * PIECE], start=True, stop=True)
                            mm.then_inc(s["spread"], 1)
                        if k == 6:
                            pe.wait_ge(s["modulated"], n + 1)
                            pe.matmul(bank(0, 0), K.c("ones"), SQ[:, FULL:], start=True, stop=True).then_inc(s["spread"], 1)
                    return one
                run(pe, levels, tail)

            @block.vector
            def _(dve):
                dve.sem_inc(s["done"], 1)
                gm = PARAMS["gamma"][0]
                dve.tensor_tensor(lb[:, 0], K.par[:, gm + 8:gm + 16], K.par[:, gm:gm + 8], ALU.subtract).then_inc(s["lb"], 1)
                dve.tensor_scalar(nbf, K.p("b_f"), -1.0, None, ALU.mult).then_inc(s["bias"], 1)
                dve.wait_ge(s["lb"], 2)
                dve.tensor_scalar(lb[:, 2], lb[:, 1], -1.0, 1.0, ALU.mult, ALU.add).then_inc(s["lb"], 1)
                ident = K.c("ident").unsqueeze(1).to_broadcast([P, NT, P])

                def chunked(t):
                    return t.rearrange("p (c n) -> p c n", n=P)

                def levels(n, h, b, tail, more):
                    dve.wait_ge(s["scaled"], n * 4 + 4)
                    dve.wait_ge(s["q_in"], n * 16 + 16)
                    dve.tensor_tensor(Qx[b][:, 1], q, G[b][:, 0], ALU.mult)
                    dve.tensor_tensor(Qx[b][:, 0], q, G[b][:, 1], ALU.mult).then_inc(s["q_next"], 1)
                    dve.wait_ge(s["level"], n * (LEVELS + 1) + 1)
                    dve.tensor_tensor(chunked(att[b]), chunked(K.ps[:, R[0]:R[0] + T]), ident, ALU.mult).then_inc(s["merged"], 1)
                    for i in range(LEVELS):
                        m, L = 1 << i, lens[i]
                        Ti = Tl[i] if i else G[b]
                        kb, qb = blocks(Kx[b], m, 0, T), blocks(Qx[b], m, 0, T)
                        dve.wait_ge(s["asm"], n * LEVELS + i + 1)
                        if i:
                            dve.wait_ge(s["k_next"], n * LEVELS + i)
                            dve.wait_ge(s["t_next"], n * LEVELS + i)
                        dve.tensor_tensor(kb, kb, factors(Ti, i, 1, 2, L - 1), ALU.mult).then_inc(s["k_next"], 1)
                        dve.wait_ge(s["level"], n * (LEVELS + 1) + (i + 2))
                        dve.wait_ge(s["q_next"], n * (LEVELS + 1) + i + 1)
                        dve.tensor_tensor(qb, qb, factors(Ti, i, L + 1, 2, -(L + 1)), ALU.mult).then_inc(s["q_next"], 1)
                        pair = Ti.rearrange("p r (n two) -> p r n two", two=2)
                        dve.wait_ge(s["merged"], n * (LEVELS + 1) + i + 1)
                        dve.tensor_tensor(Tl[i + 1], pair[:, :, :, 0], pair[:, :, :, 1], ALU.mult).then_inc(s["t_next"], 1)
                        region = chunked(K.ps[:, R[(i + 1) % 2]:R[(i + 1) % 2] + T])
                        mask = K.level_masks[:, i].unsqueeze(1).to_broadcast([P, NT, P])
                        dve.copy_predicated(chunked(att[b]), mask, region).then_inc(s["merged"], 1)
                        if tail:
                            tail(i)

                def tail(n, h, b):
                    step = Steps(dve, s["states"], n, N_STATE_STEPS)

                    def one(k):
                        if k < 2:
                            dve.wait_ge(s["kv"], n * 3 + k + 1)
                            if k == 0:
                                dve.wait_ge(s["st_in"], n * 32 + 32)
                                dve.wait_ge(s["t_next"], (n + 1) * LEVELS)
                            for j in range(NS // 2):
                                for r in range(2):
                                    i0 = k * NS // 2 + j
                                    c = chunk_of(r, i0)
                                    a = TAIL + r * PIECE + j * P
                                    if i0:
                                        dve.wait_ge(s["states"], n * N_STATE_STEPS + (step.k - 1))
                                    step.did(dve.scalar_tensor_tensor(S[:, r, i0 + 1], S[:, r, i0], last_T(r, c), K.ps[:, a:a + P],
                                                                      ALU.mult, ALU.add))
                        if k == 2:
                            dve.wait_ge(s["kv"], n * 3 + 3)
                            dve.wait_ge(s["S_out"], n * 32 + 32)
                            step.did(dve.tensor_copy(S[:, :, NS + 1], K.ps[:, TAIL:TAIL + 2 * P].rearrange("p (r v) -> p r v", r=2)))
                            step.close()
                        if k == 4:
                            dve.wait_ge(s["silu"], n + 1)
                            dve.wait_ge(s["sq"], n + 1)
                            dve.scalar_tensor_tensor(O, O, K.par[:, bass.ds(h + PARAMS["g_hgrn"][0], 1)], g,
                                                     ALU.mult, ALU.mult).then_inc(s["norm"], 1)
                            dve.wait_ge(s["root"], n + 1)
                            dve.reciprocal(rms[:, 1], rms[:, 0]).then_inc(s["norm"], 1)
                            dve.wait_ge(s["norm"], n * 3 + 2)
                            dve.tensor_tensor(chunked(SQ), ident, rms[:, 1].unsqueeze(2).to_broadcast([P, NT, P]), ALU.mult).then_inc(s["norm"], 1)
                        if k > 4:
                            lo, hi = (0, FULL) if k == 5 else (FULL, T)
                            dve.wait_ge(s["spread"], n * 2 + (k - 4))
                            dve.tensor_tensor(K.hT[:, bass.ds(h, 1), lo:hi].rearrange("p a t -> p (a t)"), O[:, lo:hi],
                                              K.ps[:, TAIL:TAIL + hi - lo], ALU.mult).then_inc(s["modulated"] if k == 5 else s["done"], 1)
                    return one

                def last_T(r, c):
                    return Tl[LEVELS][:, r, c:c + 1]
                run(dve, levels, tail)




def build(nc, d, stages=None):
    ctx = ExitStack()
    in_stage = []
    with ctx:
        def sb(name, shape, dt=F32):
            return ctx.enter_context(nc.sbuf_tensor(name, shape, dt))

        def dram(name, shape):
            return nc.dram_tensor(name, shape, F32).ap()

        def sems(stage, *names):
            held = {n: nc.alloc_semaphore(name=f"{stage}_{n}") for n in names}
            in_stage.extend(held.values())
            return held

        K = Shared(nc, d, ctx, sb, dram, sems)
        for n, stage in enumerate([
            lambda: stage_adaln(K),
            lambda: stage_norm(K, 0, 0, False),
            lambda: stage_project(K, "in_ab", AT_IN_AB, 3, 4, True),
            lambda: stage_attention(K),
            lambda: stage_gates(K),
            lambda: stage_mlstm(K),
            lambda: stage_out(K, 0),
            lambda: stage_route(K, 0),
            lambda: stage_experts(K, 0),
            lambda: stage_norm(K, 1, 0, False),
            lambda: stage_project(K, "in_c", AT_IN_C, 8, 2, False),
            lambda: stage_hgrn(K),
            lambda: stage_out(K, 1),
            lambda: stage_route(K, 1),
            lambda: stage_experts(K, 1),
            lambda: stage_final(K),
        ]):
            if stages is None or n < stages:
                stage()
                nc.clear_and_free_semaphores(list(in_stage))
                in_stage.clear()
                nc.all_engine_barrier()
        if stages is not None and stages < 99:
            total = K.loaded_after[stages]
            with nc.Block() as block:
                @block.sync
                def _(sp):
                    for i in range(SLOTS):
                        sp.wait_ge(K.w_loaded[i], 16 * len(range(i, total, SLOTS)))


_OUTS = [("y_prompt", (1, T_P, D)), ("y_sample", (1, T_S, D)),
         ("new_k", (1, 1, P, HEADS_A, 2 * DQK)), ("new_v", (1, 1, P, HEADS_A, P)),
         ("new_C", (1, 1, 2, HEADS_B, P, P)), ("new_n", (1, 1, 2, HEADS_B, P)), ("new_m", (1, 1, 2, HEADS_B)),
         ("new_S", (1, 1, 2, HEADS_C, P, P))]


def columns(v):
    return np.ascontiguousarray(v).reshape(-1, P).T


def shape_constants():
    c = np.zeros((P, N_CONSTS), np.float32)

    def put(name, a):
        c[:a.shape[0], CONSTS[name][0]:CONSTS[name][0] + CONSTS[name][1]] = a
    i, j = np.arange(P)[:, None], np.arange(P)[None, :]
    put("ident", np.eye(P))
    put("ones", np.ones((P, P)))
    put("neg_fwd", np.where(i <= j, 0.0, NEG))
    put("neg_bwd", np.where(i >= j, 0.0, NEG))
    n_freq = DQK // 4
    inv = np.power(np.float32(10000.0), -np.arange(n_freq, dtype=np.float32) / n_freq).astype(np.float32)
    t = np.arange(T_S)
    ang = np.concatenate([(t // GRID_W).astype(np.float32)[:, None] * inv,
                          (t % GRID_W).astype(np.float32)[:, None] * inv], axis=1).astype(np.float32)
    cos, sin = np.cos(ang), np.sin(ang)
    rope = np.stack([np.concatenate(x, 1).reshape(NS, P, P).transpose(1, 0, 2)
                     for x in ([cos] * 4, [-sin, sin] * 2)], 1)
    k = np.arange(T)
    resets = np.tile(np.stack([k % P != 0, k % P != P - 1]).astype(np.float32), (4, 1, 1))
    masks = np.stack([((i >> (m + 1)) == (j >> (m + 1))) & ((i >> m) != (j >> m)) for m in range(LEVELS)], 1)
    return c, masks.astype(np.uint32), np.ascontiguousarray(rope, np.float32), resets


_DIRECT = ["x_prompt", "x_sample", "cache_dattn_k", "cache_dattn_v", "state_mlstm_C", "state_mlstm_n",
           "state_mlstm_m", "state_hgrn_S", "w_ada", "g_final", "w_in_ab", "b_ig_ab", "b_fg_ab", "w_out_ab",
           "w_in_c", "w_out_c", "w_router", "w_gate_e", "w_up_e", "w_down_e"]


def laid_out(inputs):
    a = {n: np.ascontiguousarray(inputs[n]) for n in _DIRECT}
    a["params"] = np.concatenate([columns(np.asarray(inputs[n])) for n in (
        "c", "c_ctx", "b_ada", "g_norm", "g_attn_ab", "g_mlstm_ab", "conv_ab", "b_f_c", "gamma_lb", "g_hgrn_c")], axis=1)
    a["lam_ab"] = np.ascontiguousarray(inputs["lam_ab"]).reshape(1, -1)
    a["consts"], a["level_masks"], a["rope"], a["resets"] = shape_constants()
    return a


def declare(nc, arrays):
    d = {n: nc.dram_tensor(f"in_{n}", a.shape, mybir.dt.from_np(a.dtype), kind="ExternalInput").ap()
         for n, a in arrays.items()}
    d.update({f"o_{n}": nc.dram_tensor(f"out_{n}", shape, F32, kind="ExternalOutput").ap() for n, shape in _OUTS})
    return d


def kernel(**inputs):
    import concourse.bacc as _bacc
    from concourse.bass_utils import run_bass_kernel_spmd as _run

    nc = _bacc.Bacc("TRN2", target_bir_lowering=False, num_devices=1)
    arrays = laid_out(inputs)
    build(nc, declare(nc, arrays))
    r = _run(nc, [{f"in_{n}": a for n, a in arrays.items()}], core_ids=[0])
    return tuple(r.results[0][f"out_{n}"] for n, _ in _OUTS)
```
